# Optimizing a Trainium2 kernel written in Bass

```python
import math
import jax, jax.numpy as jnp
from jax import lax
import numpy as np

D_MODEL = 1024
BATCH = 1
SEQ = 512
DEPTH = 2

N_ATTN_HEADS = 4
QK_NOPE_DIM = 128
QK_ROPE_DIM = 64
QK_HEAD_DIM = QK_NOPE_DIM + QK_ROPE_DIM
V_HEAD_DIM = 128
Q_RANK = 256
KV_RANK = 128
ATTN_WIDTH = N_ATTN_HEADS * V_HEAD_DIM
ROPE_THETA = 10000.0
Q_BLOCK = 128
CONV_CH = 512
CONV_WIDTH = 31
CONV_PAD = CONV_WIDTH // 2
D_MIX = ATTN_WIDTH + CONV_CH
IN_WIDTH = Q_RANK + KV_RANK + QK_ROPE_DIM + 2 * CONV_CH
N_EXPERTS = 16
CAPACITY_FACTOR = 2
EXPERT_FF = 1024
N_MOD = 6
EPS = 1e-6


def rms_norm(x, g):
    xf = x.astype(jnp.float32)
    y = xf * lax.rsqrt(jnp.mean(xf * xf, axis=-1, keepdims=True) + EPS)
    return (y * g.astype(jnp.float32)).astype(x.dtype)

def layer_norm(x, g, b):
    xf = x.astype(jnp.float32)
    mu = jnp.mean(xf, axis=-1, keepdims=True)
    var = jnp.mean(jnp.square(xf - mu), axis=-1, keepdims=True)
    y = (xf - mu) * lax.rsqrt(var + EPS)
    return (y * g.astype(jnp.float32) + b.astype(jnp.float32)).astype(x.dtype)

def rope_tables(positions):
    inv_freq = 1.0 / (ROPE_THETA ** (jnp.arange(0, QK_ROPE_DIM, 2, dtype=jnp.float32) / QK_ROPE_DIM))
    ang = positions.astype(jnp.float32)[..., None] * inv_freq
    return jnp.cos(ang), jnp.sin(ang)

def apply_rope(x, cos, sin):
    half = x.shape[-1] // 2
    x1 = x[..., :half].astype(jnp.float32)
    x2 = x[..., half:].astype(jnp.float32)
    c = cos[:, :, None, :]
    s = sin[:, :, None, :]
    return jnp.concatenate([x1 * c - x2 * s, x2 * c + x1 * s], axis=-1).astype(x.dtype)

def mla_group(c_q, c_kv, k_rope, cos, sin, q_latent_g, w_uq, kv_latent_g, w_ukv, q_head_g, k_head_g):
    B, S, _ = c_q.shape
    q = jnp.einsum('bsr,rk->bsk', rms_norm(c_q, q_latent_g), w_uq).reshape(B, S, N_ATTN_HEADS, QK_HEAD_DIM)
    kv = jnp.einsum('bsr,rk->bsk', rms_norm(c_kv, kv_latent_g), w_ukv).reshape(
        B, S, N_ATTN_HEADS, QK_NOPE_DIM + V_HEAD_DIM)
    k_nope, v = kv[..., :QK_NOPE_DIM], kv[..., QK_NOPE_DIM:]
    k_r = jnp.broadcast_to(k_rope[:, :, None, :], (B, S, N_ATTN_HEADS, QK_ROPE_DIM))
    k = jnp.concatenate([k_nope, k_r], axis=-1)
    q = rms_norm(q, q_head_g)
    k = rms_norm(k, k_head_g)
    q = jnp.concatenate([q[..., :QK_NOPE_DIM], apply_rope(q[..., QK_NOPE_DIM:], cos, sin)], axis=-1)
    k = jnp.concatenate([k[..., :QK_NOPE_DIM], apply_rope(k[..., QK_NOPE_DIM:], cos, sin)], axis=-1)
    scale = 1.0 / math.sqrt(QK_HEAD_DIM)
    n_blocks = S // Q_BLOCK
    qb = q.reshape(B, n_blocks, Q_BLOCK, N_ATTN_HEADS, QK_HEAD_DIM).transpose(1, 0, 3, 2, 4)
    kt = k.transpose(0, 2, 1, 3)
    vt = v.transpose(0, 2, 1, 3)

    def attend(q_blk):
        s = jnp.einsum('bhqd,bhkd->bhqk', q_blk, kt, preferred_element_type=jnp.float32) * scale
        p = jax.nn.softmax(s, axis=-1).astype(vt.dtype)
        return jnp.einsum('bhqk,bhkd->bhqd', p, vt)

    o = lax.map(attend, qb)
    return o.transpose(1, 0, 3, 2, 4).reshape(B, S, ATTN_WIDTH)

def conv_group(u, conv_w, conv_b, conv_norm_g, conv_norm_b):
    a, g = u[..., :CONV_CH], u[..., CONV_CH:]
    y = a * jax.nn.sigmoid(g)
    y = lax.conv_general_dilated(
        y, conv_w[:, None, :].astype(y.dtype), window_strides=(1,), padding=[(CONV_PAD, CONV_PAD)],
        dimension_numbers=('NWC', 'WIO', 'NWC'), feature_group_count=CONV_CH)
    y = y + conv_b
    return jax.nn.silu(layer_norm(y, conv_norm_g, conv_norm_b))

def expert_choice_ffn(h, w_router, w_gate, w_up, w_down):
    B, S, D = h.shape
    cap = CAPACITY_FACTOR * S // N_EXPERTS
    logits = jnp.einsum('bsd,de->bse', h, w_router).astype(jnp.float32)
    aff = jax.nn.softmax(logits, axis=-1)
    gate, idx = lax.top_k(aff.transpose(0, 2, 1), cap)
    xe = jax.vmap(lambda hb, ib: hb[ib])(h, idx)
    hid = jax.nn.silu(jnp.einsum('becd,edf->becf', xe, w_gate)) * jnp.einsum('becd,edf->becf', xe, w_up)
    ye = jnp.einsum('becf,efd->becd', hid, w_down) * gate[..., None].astype(h.dtype)
    return jax.vmap(lambda ib, yb: jnp.zeros((S, D), yb.dtype).at[ib.reshape(-1)].add(yb.reshape(-1, D)))(idx, ye)

def first_inputs(seed: int = 0) -> dict:
    key = jax.random.key(seed)
    ks = jax.random.split(key, 24)
    f32 = jnp.float32
    nrm = lambda k, shape, s: jax.random.normal(k, shape, f32) * s
    gain = lambda k, shape: 1.0 + 0.05 * jax.random.normal(k, shape, f32)
    L = DEPTH
    offset = jax.random.randint(ks[2], (BATCH, 1), 0, 1024, dtype=jnp.int32)
    positions = offset + jnp.arange(SEQ, dtype=jnp.int32)[None, :]
    return {
        "x": nrm(ks[0], (BATCH, SEQ, D_MODEL), 1.0),
        "c": nrm(ks[1], (BATCH, D_MODEL), 1.0),
        "positions": positions,
        "norm1_g": gain(ks[3], (L, D_MODEL)),
        "w_ada": nrm(ks[4], (L, D_MODEL, N_MOD * D_MODEL), 0.5 * D_MODEL ** -0.5),
        "b_ada": nrm(ks[5], (L, N_MOD * D_MODEL), 0.01),
        "w_in": nrm(ks[6], (L, D_MODEL, IN_WIDTH), D_MODEL ** -0.5),
        "q_latent_g": gain(ks[7], (L, Q_RANK)),
        "w_uq": nrm(ks[8], (L, Q_RANK, N_ATTN_HEADS * QK_HEAD_DIM), Q_RANK ** -0.5),
        "kv_latent_g": gain(ks[9], (L, KV_RANK)),
        "w_ukv": nrm(ks[10], (L, KV_RANK, N_ATTN_HEADS * (QK_NOPE_DIM + V_HEAD_DIM)), KV_RANK ** -0.5),
        "q_head_g": gain(ks[11], (L, QK_HEAD_DIM)),
        "k_head_g": gain(ks[12], (L, QK_HEAD_DIM)),
        "conv_w": nrm(ks[13], (L, CONV_WIDTH, CONV_CH), CONV_WIDTH ** -0.5),
        "conv_b": nrm(ks[14], (L, CONV_CH), 0.01),
        "conv_norm_g": gain(ks[15], (L, CONV_CH)),
        "conv_norm_b": nrm(ks[16], (L, CONV_CH), 0.01),
        "w_out": nrm(ks[17], (L, D_MIX, D_MODEL), D_MIX ** -0.5),
        "norm2_g": gain(ks[18], (L, D_MODEL)),
        "w_router": nrm(ks[19], (L, D_MODEL, N_EXPERTS), D_MODEL ** -0.5),
        "w_gate": nrm(ks[20], (L, N_EXPERTS, D_MODEL, EXPERT_FF), D_MODEL ** -0.5),
        "w_up": nrm(ks[21], (L, N_EXPERTS, D_MODEL, EXPERT_FF), D_MODEL ** -0.5),
        "w_down": nrm(ks[22], (L, N_EXPERTS, EXPERT_FF, D_MODEL), EXPERT_FF ** -0.5),
    }

def first_block(x, c, positions, norm1_g, w_ada, b_ada, w_in, q_latent_g, w_uq, kv_latent_g, w_ukv,
              q_head_g, k_head_g, conv_w, conv_b, conv_norm_g, conv_norm_b, w_out, norm2_g,
              w_router, w_gate, w_up, w_down):
    cos, sin = rope_tables(positions)
    c_act = jax.nn.silu(c)
    o1 = Q_RANK
    o2 = o1 + KV_RANK
    o3 = o2 + QK_ROPE_DIM
    for l in range(DEPTH):
        mod = jnp.einsum('bd,dk->bk', c_act, w_ada[l]) + b_ada[l]
        shift1, scale1, gate1, shift2, scale2, gate2 = [m[:, None, :] for m in jnp.split(mod, N_MOD, axis=-1)]
        h = rms_norm(x, norm1_g[l]) * (1.0 + scale1) + shift1
        proj = jnp.einsum('bsd,dk->bsk', h, w_in[l])
        c_q, c_kv = proj[..., :o1], proj[..., o1:o2]
        k_rope = proj[..., o2:o3]
        conv_u = proj[..., o3:]
        attn_out = mla_group(c_q, c_kv, k_rope, cos, sin, q_latent_g[l], w_uq[l], kv_latent_g[l], w_ukv[l],
                             q_head_g[l], k_head_g[l])
        conv_out = conv_group(conv_u, conv_w[l], conv_b[l], conv_norm_g[l], conv_norm_b[l])
        mix = jnp.einsum('bsk,kd->bsd', jnp.concatenate([attn_out, conv_out], axis=-1), w_out[l])
        x = x + gate1 * mix
        h2 = rms_norm(x, norm2_g[l]) * (1.0 + scale2) + shift2
        x = x + gate2 * expert_choice_ffn(h2, w_router[l], w_gate[l], w_up[l], w_down[l])
    return x


DEPTH_2 = 1

N_MEM = 256
CHUNK = 128
A_GROUPS = 8
A_WIDTH = 1024
A_GROUP_DIM = A_WIDTH // A_GROUPS
B_HEADS = 10
B_WIDTH = 1280
B_HEAD_DIM = B_WIDTH // B_HEADS
CONV_WIDTH_2 = 4
LRU_C = 8.0
C_HEADS = 4
C_HEAD_DIM = 256
C_WIDTH = C_HEADS * C_HEAD_DIM
N_BRANCH = 3
IN_WIDTH_2 = 2 * A_WIDTH + 2 * B_WIDTH + C_WIDTH + N_BRANCH * D_MODEL
SPLIT_POINTS = (A_WIDTH, 2 * A_WIDTH, 2 * A_WIDTH + B_WIDTH, 2 * A_WIDTH + 2 * B_WIDTH,
                2 * A_WIDTH + 2 * B_WIDTH + C_WIDTH)
N_GROUPS = 4
EXPERTS_PER_GROUP = 4
N_EXPERTS_2 = N_GROUPS * EXPERTS_PER_GROUP
TOP_K = 2
D_EXPERT = 256
ALPHA = (2 * DEPTH_2) ** 0.25
BETA = (8 * DEPTH_2) ** -0.25
LN_EPS = 1e-5


def layer_norm_2(x, g, b):
    xf = x.astype(jnp.float32)
    mu = jnp.mean(xf, axis=-1, keepdims=True)
    var = jnp.mean(jnp.square(xf - mu), axis=-1, keepdims=True)
    y = (xf - mu) * lax.rsqrt(var + LN_EPS)
    return (y * g.astype(jnp.float32) + b.astype(jnp.float32)).astype(x.dtype)

def spatial_gating(u, v, ln_g, ln_b, w_s, b_s):
    bsz, seq, _ = v.shape
    n_chunks = seq // CHUNK
    v = layer_norm_2(v, ln_g, ln_b)
    causal = jnp.tril(jnp.ones((CHUNK, CHUNK), dtype=bool))
    w = jnp.where(causal[None], w_s, jnp.zeros_like(w_s))
    vc = v.reshape(bsz, n_chunks, CHUNK, A_GROUPS, A_GROUP_DIM)
    s = jnp.einsum('gts,bcsgd->bctgd', w, vc) + b_s.T[None, None, :, :, None]
    return u * s.reshape(bsz, seq, A_WIDTH)

def causal_depthwise_conv(x, w, b):
    seq = x.shape[1]
    xp = jnp.pad(x, ((0, 0), (CONV_WIDTH_2 - 1, 0), (0, 0)))
    out = b
    for k in range(CONV_WIDTH_2):
        out = out + w[k] * xp[:, k:k + seq]
    return out

def rg_lru(x, w_a, b_a, w_x, b_x, lam):
    bsz, seq, _ = x.shape
    xh = x.reshape(bsz, seq, B_HEADS, B_HEAD_DIM)
    r = jax.nn.sigmoid(jnp.einsum('bshi,hij->bshj', xh, w_a).reshape(bsz, seq, B_WIDTH) + b_a)
    i = jax.nn.sigmoid(jnp.einsum('bshi,hij->bshj', xh, w_x).reshape(bsz, seq, B_WIDTH) + b_x)
    log_a = -LRU_C * r.astype(jnp.float32) * jax.nn.softplus(-lam.astype(jnp.float32))
    a = jnp.exp(log_a)
    mult = jnp.sqrt(-jnp.expm1(2.0 * log_a))
    bx = mult * (i * x).astype(jnp.float32)

    def combine(c1, c2):
        a1, b1 = c1
        a2, b2 = c2
        return a1 * a2, a2 * b1 + b2

    _, h = lax.associative_scan(combine, (a, bx), axis=1)
    return h.astype(x.dtype)

def memory_attention(q, mem_n, w_kv):
    bsz, seq, _ = q.shape
    kv = jnp.einsum('bmd,de->bme', mem_n, w_kv)
    k, v = jnp.split(kv, 2, axis=-1)
    qh = q.reshape(bsz, seq, C_HEADS, C_HEAD_DIM)
    kh = k.reshape(bsz, N_MEM, C_HEADS, C_HEAD_DIM)
    vh = v.reshape(bsz, N_MEM, C_HEADS, C_HEAD_DIM)
    scores = jnp.einsum('bshd,bmhd->bhsm', qh, kh).astype(jnp.float32) * (C_HEAD_DIM ** -0.5)
    p = jax.nn.softmax(scores, axis=-1).astype(q.dtype)
    o = jnp.einsum('bhsm,bmhd->bshd', p, vh)
    return o.reshape(bsz, seq, C_WIDTH)

def hybrid_mixer(x, mem_n, w_in, b_in, ln_v_g, ln_v_b, w_s, b_s, conv_w, conv_b,
                 w_a, b_a, w_x, b_x, lam, w_kv, p_a, p_b, p_c, w_o, b_o):
    z = jnp.einsum('bsd,de->bse', x, w_in) + b_in
    u_a, v_a, x_b, gate_b, q_c, merge = jnp.split(z, SPLIT_POINTS, axis=-1)
    o_a = spatial_gating(jax.nn.gelu(u_a), jax.nn.gelu(v_a), ln_v_g, ln_v_b, w_s, b_s)
    o_b = rg_lru(causal_depthwise_conv(x_b, conv_w, conv_b), w_a, b_a, w_x, b_x, lam) * jax.nn.gelu(gate_b)
    o_c = memory_attention(q_c, mem_n, w_kv)
    g_a, g_b, g_c = jnp.split(jax.nn.sigmoid(merge), N_BRANCH, axis=-1)
    y = (g_a * jnp.einsum('bse,ed->bsd', o_a, p_a)
         + g_b * jnp.einsum('bse,ed->bsd', o_b, p_b)
         + g_c * jnp.einsum('bse,ed->bsd', o_c, p_c))
    return jnp.einsum('bsd,de->bse', y, w_o) + b_o

def hierarchical_moe(x, w_rg, b_rg, w_re, b_re, w_up, w_down):
    bsz, seq, d = x.shape
    xf = x.reshape(bsz * seq, d)
    n_tok = xf.shape[0]
    group_p = jax.nn.softmax((xf @ w_rg + b_rg).astype(jnp.float32), axis=-1)
    p_top, g_top = lax.top_k(group_p, 1)
    exp_logits = (xf @ w_re + b_re).astype(jnp.float32).reshape(n_tok, N_GROUPS, EXPERTS_PER_GROUP)
    in_group = exp_logits[jnp.arange(n_tok), g_top[:, 0]]
    e_p, e_idx = lax.top_k(jax.nn.softmax(in_group, axis=-1), TOP_K)
    weights = p_top * e_p / jnp.sum(e_p, axis=-1, keepdims=True)
    expert_id = g_top * EXPERTS_PER_GROUP + e_idx
    gate = jnp.sum(jax.nn.one_hot(expert_id, N_EXPERTS_2, dtype=jnp.float32) * weights[..., None],
                   axis=1).astype(x.dtype)
    h = jnp.einsum('nd,edf->nef', xf, w_up)
    h_g, h_u = jnp.split(h, 2, axis=-1)
    h = jax.nn.silu(h_g) * h_u * gate[:, :, None]
    y = jnp.einsum('nef,efd->nd', h, w_down)
    return y.reshape(bsz, seq, d)

def second_inputs(seed: int = 0) -> dict:
    key = jax.random.key(seed)
    ks = jax.random.split(key, 40)
    f32 = jnp.float32

    def nrm(k, shape, scale):
        return jax.random.normal(k, shape, dtype=f32) * scale

    lam_u = jax.random.uniform(ks[18], (DEPTH_2, B_WIDTH), dtype=f32, minval=0.9, maxval=0.999)
    a0 = lam_u ** (1.0 / LRU_C)
    lam = jnp.log(a0) - jnp.log1p(-a0)
    return {
        "x": nrm(ks[0], (BATCH, SEQ, D_MODEL), 1.0),
        "mem": nrm(ks[1], (BATCH, N_MEM, D_MODEL), 1.0),
        "ln_in_g": 1.0 + nrm(ks[2], (D_MODEL,), 0.02),
        "ln_in_b": nrm(ks[3], (D_MODEL,), 0.02),
        "ln_mem_g": 1.0 + nrm(ks[4], (D_MODEL,), 0.02),
        "ln_mem_b": nrm(ks[5], (D_MODEL,), 0.02),
        "w_in": nrm(ks[6], (DEPTH_2, D_MODEL, IN_WIDTH_2), D_MODEL ** -0.5),
        "b_in": nrm(ks[7], (DEPTH_2, IN_WIDTH_2), 0.02),
        "ln_v_g": 1.0 + nrm(ks[8], (DEPTH_2, A_WIDTH), 0.02),
        "ln_v_b": nrm(ks[9], (DEPTH_2, A_WIDTH), 0.02),
        "w_s": nrm(ks[10], (DEPTH_2, A_GROUPS, CHUNK, CHUNK), CHUNK ** -0.5),
        "b_s": 1.0 + nrm(ks[11], (DEPTH_2, A_GROUPS, CHUNK), 0.02),
        "conv_w": nrm(ks[12], (DEPTH_2, CONV_WIDTH_2, B_WIDTH), CONV_WIDTH_2 ** -0.5),
        "conv_b": nrm(ks[13], (DEPTH_2, B_WIDTH), 0.02),
        "w_a": nrm(ks[14], (DEPTH_2, B_HEADS, B_HEAD_DIM, B_HEAD_DIM), B_HEAD_DIM ** -0.5),
        "b_a": nrm(ks[15], (DEPTH_2, B_WIDTH), 0.02),
        "w_x": nrm(ks[16], (DEPTH_2, B_HEADS, B_HEAD_DIM, B_HEAD_DIM), B_HEAD_DIM ** -0.5),
        "b_x": nrm(ks[17], (DEPTH_2, B_WIDTH), 0.02),
        "lam": lam,
        "w_kv": nrm(ks[19], (DEPTH_2, D_MODEL, 2 * C_WIDTH), D_MODEL ** -0.5),
        "p_a": nrm(ks[20], (DEPTH_2, A_WIDTH, D_MODEL), A_WIDTH ** -0.5),
        "p_b": nrm(ks[21], (DEPTH_2, B_WIDTH, D_MODEL), B_WIDTH ** -0.5),
        "p_c": nrm(ks[22], (DEPTH_2, C_WIDTH, D_MODEL), C_WIDTH ** -0.5),
        "w_o": nrm(ks[23], (DEPTH_2, D_MODEL, D_MODEL), BETA * D_MODEL ** -0.5),
        "b_o": nrm(ks[24], (DEPTH_2, D_MODEL), 0.02),
        "ln1_g": 1.0 + nrm(ks[25], (DEPTH_2, D_MODEL), 0.02),
        "ln1_b": nrm(ks[26], (DEPTH_2, D_MODEL), 0.02),
        "w_rg": nrm(ks[27], (DEPTH_2, D_MODEL, N_GROUPS), D_MODEL ** -0.5),
        "b_rg": nrm(ks[28], (DEPTH_2, N_GROUPS), 0.01),
        "w_re": nrm(ks[29], (DEPTH_2, D_MODEL, N_EXPERTS_2), D_MODEL ** -0.5),
        "b_re": nrm(ks[30], (DEPTH_2, N_EXPERTS_2), 0.01),
        "w_up": nrm(ks[31], (DEPTH_2, N_EXPERTS_2, D_MODEL, 2 * D_EXPERT), D_MODEL ** -0.5),
        "w_down": nrm(ks[32], (DEPTH_2, N_EXPERTS_2, D_EXPERT, D_MODEL), BETA * D_EXPERT ** -0.5),
        "ln2_g": 1.0 + nrm(ks[33], (DEPTH_2, D_MODEL), 0.02),
        "ln2_b": nrm(ks[34], (DEPTH_2, D_MODEL), 0.02),
    }

def second_block(x, mem, ln_in_g, ln_in_b, ln_mem_g, ln_mem_b, w_in, b_in, ln_v_g, ln_v_b,
              w_s, b_s, conv_w, conv_b, w_a, b_a, w_x, b_x, lam, w_kv, p_a, p_b, p_c,
              w_o, b_o, ln1_g, ln1_b, w_rg, b_rg, w_re, b_re, w_up, w_down, ln2_g, ln2_b):
    x = layer_norm_2(x, ln_in_g, ln_in_b)
    mem_n = layer_norm_2(mem, ln_mem_g, ln_mem_b)
    for l in range(DEPTH_2):
        m = hybrid_mixer(x, mem_n, w_in[l], b_in[l], ln_v_g[l], ln_v_b[l], w_s[l], b_s[l],
                         conv_w[l], conv_b[l], w_a[l], b_a[l], w_x[l], b_x[l], lam[l],
                         w_kv[l], p_a[l], p_b[l], p_c[l], w_o[l], b_o[l])
        x = layer_norm_2(ALPHA * x + m, ln1_g[l], ln1_b[l])
        f = hierarchical_moe(x, w_rg[l], b_rg[l], w_re[l], b_re[l], w_up[l], w_down[l])
        x = layer_norm_2(ALPHA * x + f, ln2_g[l], ln2_b[l])
    return x


_first_inputs = second_inputs


def second_inputs(seed=0):
    import zlib

    import numpy as np

    out = dict(_first_inputs(seed))
    spreads = {}
    factors = {'ln_mem_g': 29.765,
     'ln_mem_b': 65.062,
     'b_in': 2.986,
     'ln_v_g': 169.141,
     'ln_v_b': 147.876,
     'b_s': 102.697,
     'conv_b': 23.16,
     'b_a': 200.0,
     'b_x': 200.0,
     'b_o': 17.757,
     'b_rg': 160.09,
     'b_re': 29.036,
     'ln2_g': 23.157,
     'ln2_b': 23.141,
     'w_a': 33.8,
     'lam': 23.528,
     'conv_w': 8.0,
     'w_x': 8.0,
     'p_b': 8.0}
    for name, (base, spread) in spreads.items():
        noise = np.random.default_rng([zlib.crc32(name.encode()), seed]).standard_normal(out[name].shape)
        drawn = base * np.exp(spread * noise) if base else spread * noise
        out[name] = __import__('jax').numpy.asarray(drawn.astype(out[name].dtype))
    for name, factor in factors.items():
        out[name] = (out[name] * factor).astype(out[name].dtype)
    return out


_narrow_inputs = second_inputs


def second_inputs(seed=0):

    out = dict(_narrow_inputs(seed))
    wider = {'ln_mem_b': 3.53,
     'ln_v_g': 3.87,
     'ln_v_b': 4.12,
     'b_s': 3.88,
     'b_o': 4.91,
     'ln2_g': 3.21,
     'ln2_b': 3.21}
    for name, times in wider.items():
        mean = out[name].mean()
        out[name] = (mean + times * (out[name] - mean)).astype(out[name].dtype)
    return out


def setup_inputs(seed=0):
    out = dict(first_inputs(seed))
    for name, value in second_inputs(seed + 1).items():
        if name != "x":
            out[name + "_2"] = value
    return out


def reference(
    x, c, positions, norm1_g, w_ada, b_ada, w_in, q_latent_g, w_uq, kv_latent_g, w_ukv,
    q_head_g, k_head_g, conv_w, conv_b, conv_norm_g, conv_norm_b, w_out, norm2_g, w_router,
    w_gate, w_up, w_down, mem_2, ln_in_g_2, ln_in_b_2, ln_mem_g_2, ln_mem_b_2, w_in_2, b_in_2,
    ln_v_g_2, ln_v_b_2, w_s_2, b_s_2, conv_w_2, conv_b_2, w_a_2, b_a_2, w_x_2, b_x_2, lam_2,
    w_kv_2, p_a_2, p_b_2, p_c_2, w_o_2, b_o_2, ln1_g_2, ln1_b_2, w_rg_2, b_rg_2, w_re_2, b_re_2,
    w_up_2, w_down_2, ln2_g_2, ln2_b_2,
):
    x = first_block(
        x, c, positions, norm1_g, w_ada, b_ada, w_in, q_latent_g, w_uq, kv_latent_g, w_ukv,
        q_head_g, k_head_g, conv_w, conv_b, conv_norm_g, conv_norm_b, w_out, norm2_g, w_router,
        w_gate, w_up, w_down,
    )
    return second_block(
        x, mem_2, ln_in_g_2, ln_in_b_2, ln_mem_g_2, ln_mem_b_2, w_in_2, b_in_2, ln_v_g_2,
        ln_v_b_2, w_s_2, b_s_2, conv_w_2, conv_b_2, w_a_2, b_a_2, w_x_2, b_x_2, lam_2, w_kv_2,
        p_a_2, p_b_2, p_c_2, w_o_2, b_o_2, ln1_g_2, ln1_b_2, w_rg_2, b_rg_2, w_re_2, b_re_2,
        w_up_2, w_down_2, ln2_g_2, ln2_b_2,
    )


_drawn_inputs = setup_inputs


def setup_inputs(seed=0):
    import zlib

    import numpy as np

    out = dict(_drawn_inputs(seed))
    spreads = {}
    factors = {'q_latent_g': 8.0,
     'kv_latent_g': 3.834,
     'q_head_g': 7.658,
     'k_head_g': 7.41,
     'conv_b': 5.205,
     'conv_norm_b': 8.0}
    for name, (base, spread) in spreads.items():
        noise = np.random.default_rng([zlib.crc32(name.encode()), seed]).standard_normal(out[name].shape)
        drawn = base * np.exp(spread * noise) if base else spread * noise
        out[name] = __import__('jax').numpy.asarray(drawn.astype(out[name].dtype))
    for name, factor in factors.items():
        out[name] = (out[name] * factor).astype(out[name].dtype)
    return out
```

```python
import math
from contextlib import ExitStack

import concourse.bass as bass
from concourse import mybir

F32 = mybir.dt.float32
I32 = mybir.dt.int32
ALU = mybir.AluOpType
ACT = mybir.ActivationFunctionType
AX_X = mybir.AxisListType.X

P = 128
D = 1024
KT = D // P
S = 512
TT = S // P
DEPTH = 2
N_MOD = 6
HEADS, NOPE, ROPE, VD = 4, 128, 64, 128
QK = NOPE + ROPE
Q_RANK, KV_RANK = 256, 128
CONV_CH, TAPS = 512, 31
CT = CONV_CH // P
PAD = TAPS // 2
YW = S + 2 * PAD
IN_W = Q_RANK + KV_RANK + ROPE + 2 * CONV_CH
EXPERTS, CAP, FF = 16, 64, 1024
HALF = 512
EPS = 1e-6
TABLES = 5 * TT * D + 2 * HEADS * QK + HEADS * (NOPE + VD)
QSCALE = 1.0 / math.sqrt(QK)
PI = 3.141592653589793
TWO_PI_A = 6.28125
TWO_PI_B = 0.0019350051879882812
TWO_PI_C = 2 * PI - TWO_PI_A - TWO_PI_B
ROUND = 1.5 * 2.0 ** 23

N1G, N2G, ADA, QLG, KVG, CB, CNG, CNB, QHG, KHG, QRG, KRG, NVEC = 0, 8, 16, 64, 66, 67, 71, 75, 79, 80, 81, 82, 83
SHIFT1, SCALE1, GATE1, SHIFT2, SCALE2, GATE2 = (m * KT for m in range(N_MOD))
C_IDENT, C_ROT, C_SLOT, C_FREQ, C_PSLOT, C_EPS6, C_EPS5, C_ALL = 0, 128, 256, 384, 385, 386, 387, 388


class Steps:

    def __init__(self, engine, semaphore):
        self.engine, self.semaphore, self.count = engine, semaphore, 0

    def __call__(self, instruction):
        self.count += 1
        instruction.then_inc(self.semaphore, 1)

    def settle(self):
        self.engine.wait_ge(self.semaphore, self.count)


def prologue(nc, A, sem, M):
    ps, const, xT = M["ps"], M["const"], M["xT"]
    ident = const[:, C_IDENT:C_IDENT + P]
    x_tok, scr = M["ring"][:, 0:TT * D].rearrange("p (t d) -> p t d", t=TT), M["scr"]
    c_rows, c_rep, ones = M["one_hot_T"][:, 0:P], M["c_rep"], M["ones"]
    cos, sin = M["ring"][:, TABLES:TABLES + S], M["ring"][:, TABLES + S:TABLES + 2 * S]
    pos_i = M["ring"][:, TT * D:TT * D + S].bitcast(I32)
    const_in, x_in, pos_in, c_in = (sem(n) for n in ("const_in", "x_in", "pos_in", "c_in"))
    x_turned, c_turned, x_kept, c_raw, c_sig, c_act, ones_set = (
        sem(n) for n in ("x_turned", "c_turned", "x_kept", "c_raw", "c_sig", "c_act", "ones_set"))
    angle_ready, p_step, p_act, tables_out = sem("angle_ready"), sem("p_step"), sem("p_act"), sem("tables_out")
    with nc.Block() as block:
        @block.sync
        def _(sp):
            sp.dma_start(const[:], A["const"]).then_inc(const_in, 16)
            sp.dma_start(x_tok, A["x"][0].rearrange("(t p) d -> p t d", p=P)).then_inc(x_in, 16)
            sp.dma_start(c_rows[0:KT, :], A["c"].rearrange("a (t p) -> (a t) p", p=P)).then_inc(c_in, 16)
            sp.dma_start(pos_i, A["positions"].to_broadcast([P, S])).then_inc(pos_in, 16)
            sp.wait_ge(p_act, 2)
            sp.dma_start(A["rope"], M["ring"][:, TABLES:TABLES + 2 * S]).then_inc(tables_out, 16)
            sp.wait_ge(tables_out, 16)

        @block.tensor
        def _(pe):
            pe.wait_ge(const_in, 16)
            pe.wait_ge(c_in, 16)
            pe.transpose(ps[:, 7, 0:KT], c_rows[0:KT, :], ident[0:KT, 0:KT]).then_inc(c_turned, 1)
            pe.wait_ge(x_in, 16)
            for kt in range(KT):
                if kt == 7:
                    pe.wait_ge(c_act, 1)
                for t in range(TT):
                    turn = pe.transpose(ps[:, kt, t * P:(t + 1) * P], x_tok[:, t, kt * P:(kt + 1) * P], ident)
                turn.then_inc(x_turned, 1)

        @block.scalar
        def _(act):
            act.wait_ge(c_turned, 1)
            act.activation(scr[:, 0, 0:KT], ps[:, 7, 0:KT], ACT.Silu).then_inc(c_sig, 1)
            act.wait_ge(angle_ready, 1)
            act.activation(sin, sin, ACT.Sin).then_inc(p_act, 1)
            act.wait_ge(angle_ready, 2)
            act.activation(cos, cos, ACT.Sin).then_inc(p_act, 1)

        @block.vector
        def _(dve):
            step = Steps(dve, p_step)
            dve.memset(ones[:], 1.0).then_inc(ones_set, 1)
            dve.wait_ge(c_sig, 1)
            dve.tensor_copy(c_rep[:], scr[:, 0, 0:KT].unsqueeze(2).to_broadcast([P, KT, 32])).then_inc(c_act, 1)
            ang, turns = scr[:, 1, :], scr[:, 2, :]
            dve.wait_ge(pos_in, 16)
            dve.wait_ge(const_in, 16)
            step(dve.tensor_copy(ang, pos_i))
            step.settle()
            step(dve.tensor_scalar(ang, ang, const[:, C_FREQ:C_FREQ + 1], None, ALU.mult))
            step.settle()
            step(dve.tensor_scalar(turns, ang, 1.0 / (2 * PI), ROUND, ALU.mult, ALU.add))
            step.settle()
            step(dve.tensor_scalar(turns, turns, ROUND, None, ALU.subtract))
            for part in (TWO_PI_A, TWO_PI_B, TWO_PI_C):
                step.settle()
                step(dve.scalar_tensor_tensor(ang, turns, -part, ang, ALU.mult, ALU.add))
            step.settle()
            dve.tensor_scalar(sin, ang, -3.1415925, 3.1415925, ALU.max, ALU.min).then_inc(angle_ready, 1)
            step(dve.tensor_scalar(turns, ang, -1.0, None, ALU.mult))
            step.settle()
            step(dve.tensor_tensor(turns, turns, ang, ALU.max))
            step.settle()
            dve.tensor_scalar(cos, turns, -1.0, PI / 2, ALU.mult, ALU.add).then_inc(angle_ready, 1)
            for kt in range(KT):
                dve.wait_ge(x_turned, kt + 1)
                dve.tensor_copy(xT[:, kt, :], ps[:, kt, :]).then_inc(x_kept, 1)

        @block.gpsimd
        def _(pool):
            pass


def layer(nc, A, sem, M, l):
    ps, const, xT, ring, scr = M["ps"], M["const"], M["xT"], M["ring"], M["scr"]
    ident, rot = const[:, C_IDENT:C_IDENT + P], const[:, C_ROT:C_ROT + P]
    eps = const[:, C_EPS6:C_EPS6 + 1]
    slot_row, slot_col = const[:, C_SLOT:C_SLOT + P], const[:, C_PSLOT:C_PSLOT + 1]
    c_rep, ones = M["c_rep"], M["ones"]
    cos, sin = ring[:, TABLES:TABLES + S], ring[:, TABLES + S:TABLES + 2 * S]
    hy, h_tok, one_hot_T = M["hy"], M["h_tok"], M["one_hot_T"]
    hT = hy[:, 0:KT * S].rearrange("p (k n) -> p k n", k=KT)
    mix = hT
    ye = hy[:, 0:EXPERTS * HALF].rearrange("p (e n) -> p e n", e=EXPERTS)
    rin = hy[:, KT * S:2 * KT * S].rearrange("p (k n) -> p k n", k=2 * HEADS)
    vec, convw, mod, smod = (M[n] for n in ("vec", "convw", "mod", "smod"))
    CHUNK = TT * D
    ada = [ring[:, i * 8192:(i + 1) * 8192].rearrange("p (k n) -> p k n", k=4) for i in range(3)]
    w_in = ring[:, 0:KT * IN_W].rearrange("p (k n) -> p k n", k=KT)
    w_out = ring[:, 3 * CHUNK:5 * CHUNK].rearrange("p (k n) -> p k n", k=KT)
    w_uq = ring[:, 5 * CHUNK:5 * CHUNK + 2 * HEADS * QK].rearrange("p (k n) -> p k n", k=2)
    w_ukv = ring[:, 5 * CHUNK + 2 * HEADS * QK:5 * CHUNK + 2 * HEADS * QK + HEADS * (NOPE + VD)]
    chunk = [ring[:, i * CHUNK:(i + 1) * CHUNK].rearrange("p (k n) -> p k n", k=4) for i in range(6)]
    def cut(region, at, n):
        return region[:, at * HALF:(at + n) * HALF].rearrange("p (k n) -> p k n", k=n)
    qn, qr, kn, kr = cut(ring, 0, 4), cut(ring, 4, 2), cut(ring, 6, 4), cut(ring, 10, 2)
    V, PT, prob = cut(ring, 12, 4), cut(ring, 16, 4), cut(ring, 20, 2)
    ypad = h_tok[:, 0:CT * YW].rearrange("p (c n) -> p c n", c=CT)
    w_r = h_tok[:, CT * YW:CT * YW + KT * EXPERTS].rearrange("p (k n) -> p k n", k=KT)
    cq = h_tok[:, 2560:2560 + 1024].rearrange("p (k n) -> p k n", k=2)
    ckv = h_tok[:, 3584:4096]
    sqs, acc, sig, krg = cut(one_hot_T, 0, 11), cut(one_hot_T, 11, 4), one_hot_T[:, 15 * HALF:16 * HALF], M["krg"]
    h_tok3 = h_tok[:].rearrange("p (t d) -> p t d", t=TT)
    ohT = one_hot_T[:].rearrange("p (e n) -> p e n", e=EXPERTS)
    stat = M["stat"]
    mx, nmx, rsum, rrs = stat[:, 0:16], stat[:, 16:32], stat[:, 32:48], stat[:, 48:64]
    rowsA, rowsB = one_hot_T[:, 12 * S:12 * S + P], one_hot_T[:, 13 * S:13 * S + P]
    diag = ring[:, 22 * HALF:22 * HALF + 2 * P].rearrange("p (i n) -> p i n", i=2)
    lg, aff, top8, rankT = (M[n] for n in ("lg", "aff", "top8", "rankT"))
    work, affT, rank = (one_hot_T[0:EXPERTS, i * S:(i + 1) * S] for i in range(3))
    rankm = M["krg"][0:EXPERTS, :]
    sel_e, gcol = M["sel_e"], M["gcol"]
    x_e, sg, hid = scr[:, 0, :], scr[:, 1, :], scr[:, 2, :]
    hidT = x_e
    s_e = scr[:, 3, :].rearrange("p (t n) -> p t n", t=TT)

    rows_in, rowsT_done, vec_ready = sem("rows_in"), sem("rowsT_done"), sem("vec_ready")
    ada_in = [sem(f"ada_in{i}") for i in range(3)]
    ada_used, ada_rows, ada_cols, mod_ready = sem("ada_used"), sem("ada_rows"), sem("ada_cols"), sem("mod_ready")
    w_in_in, uq_in, w_out_in, w_r_in = sem("w_in_in"), sem("uq_in"), sem("w_out_in"), sem("w_r_in")
    n_sq, n_ss, n_root, n_xn, h_ready = sem("n_sq"), sem("n_ss"), sem("n_root"), sem("n_xn"), sem("h_ready")
    pad_zero, proj, act_proj, dve_proj, sig_ready, y_ready = (sem(n) for n in ("pad_zero", "proj", "act_proj", "dve_proj", "sig_ready", "y_ready"))
    lat_sq, lat_ss, lat_root, lat_ready = sem("lat_sq"), sem("lat_ss"), sem("lat_root"), sem("lat_ready")
    qk_mm, qk_ev, rot_mm, rot_used, head_ss, head_root, qk_ready = (sem(n) for n in ("qk_mm", "qk_ev", "rot_mm", "rot_used", "head_ss", "head_root", "qk_ready"))
    s_done, nm_ready, exp_done, diag_ready, t_done, pt_ev, pv_done, pv_ev = (
        sem(n) for n in ("s_done", "nm_ready", "exp_done", "diag_ready", "t_done", "pt_ev", "pv_done", "pv_ev"))
    conv_done, cmean, cdev, csq, cvar, croot, cnorm, cmix = (
        sem(n) for n in ("conv_done", "cmean", "cdev", "csq", "cvar", "croot", "cnorm", "cmix"))
    wout_done, x1_ready = sem("wout_done"), sem("x1_ready")
    r_done, r_sub, r_exp, aff_ready, affT_done, htok_mm, htok_ev, rank_ready, rankT_done = (
        sem(n) for n in ("r_done", "r_sub", "r_exp", "aff_ready", "affT_done", "htok_mm", "htok_ev", "rank_ready", "rankT_done"))
    chunk_in = [sem(f"chunk_in{i}") for i in range(6)]
    chunk_used, s_built, xe_mm, xe_ready, st_mm, st_free, sg_ready, hid_ready, hidT_mm, hidT_ready, ye_free = (
        sem(n) for n in ("chunk_used", "s_built", "xe_mm", "xe_ready", "st_mm", "st_free", "sg_ready", "hid_ready", "hidT_mm", "hidT_ready", "ye_free"))
    loop_step, out_done, x2_ready = sem("loop_step"), sem("out_done"), sem("x2_ready")
    d_step, a_step = sem("d_step"), sem("a_step")

    def at(name):
        return A[name][bass.ds(l, 1)]

    with nc.Block() as block:
        @block.sync
        def _(sp):
            w_ada = at("w_ada").rearrange("a (k p) n -> p (a k) n", p=P)
            for c in range(6):
                if c >= 3:
                    sp.wait_ge(ada_used, c - 2)
                sp.dma_start(ada[c % 3], w_ada[:, 4 * (c % 2):4 * (c % 2) + 4, 2048 * (c // 2):2048 * (c // 2 + 1)]).then_inc(ada_in[c % 3], 16)
            sp.wait_ge(ada_used, 6)
            w = at("w_in").rearrange("a (k p) n -> p (a k) n", p=P)
            for k in range(0, KT, 2):
                sp.dma_start(w_in[:, k:k + 2], w[:, k:k + 2]).then_inc(w_in_in, 16)
            sp.dma_start(w_uq, at("w_uq").rearrange("a (k p) n -> p (a k) n", p=P)).then_inc(uq_in, 16)
            sp.dma_start(w_ukv, at("w_ukv").rearrange("a p n -> p (a n)")).then_inc(uq_in, 16)
            sp.dma_start(ring[:, TABLES:TABLES + 2 * S], A["rope"]).then_inc(uq_in, 16)
            sp.dma_start(w_r, at("w_router").rearrange("a (k p) n -> p (a k) n", p=P)).then_inc(w_r_in, 16)
            w = at("w_out").rearrange("a (k p) n -> p (a k) n", p=P)
            for k in range(0, KT, 4):
                sp.dma_start(w_out[:, k:k + 4], w[:, k:k + 4]).then_inc(w_out_in, 16)

            def expert(e):
                for j in range(6):
                    name, k = ("w_gate", "w_up", "w_down")[j // 2], 4 * (j % 2)
                    if e is not None:
                        sp.wait_ge(chunk_used, 6 * e + (j - 5))
                    w = A[name][bass.ds(l, 1), bass.ds(0 if e is None else e, 1)].rearrange("a e (k p) n -> p (a e k) n", p=P)
                    sp.dma_start(chunk[j], w[:, k:k + 4]).then_inc(chunk_in[j], 16)

            sp.wait_ge(wout_done, KT)
            expert(None)
            with sp.Fori(1, EXPERTS) as e:
                expert(e)

        @block.gpsimd
        def _(pool):
            pool.memset(ypad[:, :, 0:PAD], 0.0)
            pool.memset(ypad[:, :, PAD + S:YW], 0.0).then_inc(pad_zero, 1)

        @block.tensor
        def _(pe):
            def norm(k):
                for kt in range(KT):
                    pe.wait_ge(n_sq, KT * k + kt + 1)
                    pe.matmul(ps[:, 6 - 6 * k, :], ones[:], scr[:, kt % 4, :], start=(kt == 0), stop=(kt == KT - 1)).then_inc(n_ss, 1)

            pe.wait_ge(rows_in, 16 * 13)
            pe.transpose(ps[:, 5, 0:NVEC], rowsA[0:NVEC, :], ident[0:NVEC, 0:NVEC]).then_inc(rowsT_done, 1)
            pe.transpose(ps[:, 7, 0:TAPS * CT], rowsB[0:TAPS * CT, :], ident[0:TAPS * CT, 0:TAPS * CT]).then_inc(rowsT_done, 1)
            norm(0)
            for c in range(6):
                pe.wait_ge(ada_in[c % 3], 16 * (c // 3 + 1))
                for k in range(4):
                    kt = 4 * (c % 2) + k
                    for g in range(4):
                        mm = pe.matmul(ps[32 * g:32 * g + 32, c // 2, :], c_rep[:, kt, :], ada[c % 3][:, k, g * HALF:(g + 1) * HALF],
                                       start=(kt == 0), stop=(kt == KT - 1))
                mm.then_inc(ada_used, 1)
            for r in range(3):
                pe.wait_ge(ada_rows, r + 1)
                if r == 2:
                    pe.wait_ge(vec_ready, 2)
                for b in range(4):
                    mm = pe.transpose(ps[:, 3 + r, b * P:(b + 1) * P], sqs[:, r, b * P:(b + 1) * P], ident)
                mm.then_inc(ada_cols, 1)
            pe.wait_ge(w_in_in, 16 * 4)
            pe.wait_ge(h_ready, KT)
            first = Q_RANK + KV_RANK + ROPE
            cols = []
            for c in range(CT):
                cols += [first + CONV_CH + c * P, first + c * P]
            cols += [0, P, Q_RANK, Q_RANK + KV_RANK]
            for i, c0 in enumerate(cols):
                if i in (6, 8, 10):
                    pe.wait_ge(act_proj, (i - 6) // 2 + 1)
                if i in (7, 9, 11):
                    pe.wait_ge(dve_proj, (i - 7) // 2 + 1)
                for kt in range(KT):
                    go = dict(start=(kt == 0), stop=(kt == KT - 1))
                    if i < 11:
                        mm = pe.matmul(ps[:, i % 6, :], w_in[:, kt, c0:c0 + P], hT[:, kt, :], **go)
                    else:
                        pe.matmul(ps[0:ROPE, i % 6, :], w_in[:, kt, c0:c0 + ROPE], hT[:, kt, :], **go)
                        mm = pe.matmul(ps[ROPE:P, i % 6, :], w_in[:, kt, c0:c0 + ROPE], hT[:, kt, :], **go)
                mm.then_inc(proj, 1)
            for i in range(3):
                pe.wait_ge(lat_sq, i + 1)
                pe.matmul(ps[:, 6 + i // 2, :], ones[:], scr[:, i, :], start=(i != 1), stop=(i != 0)).then_inc(lat_ss, 1)
            pe.wait_ge(uq_in, 48)
            pe.wait_ge(lat_ready, 3)
            for i in range(14):
                if i == 5:
                    pe.wait_ge(act_proj, 8)
                if i >= 6:
                    pe.wait_ge(qk_ev, i - 5)
                out = ps[:, i % 6, :]
                if i < 6:
                    for k in range(2):
                        go = dict(start=(k == 0), stop=(k == 1))
                        if i % 3 < 2:
                            h = 2 * (i // 3) + i % 3
                            mm = pe.matmul(out, w_uq[:, k, h * QK:h * QK + NOPE], cq[:, k, :], **go)
                        else:
                            for half in range(2):
                                h = 2 * (i // 3) + half
                                mm = pe.matmul(ps[ROPE * half:ROPE * (half + 1), i % 6, :], w_uq[:, k, h * QK + NOPE:(h + 1) * QK], cq[:, k, :], **go)
                elif i < 10:
                    h = i - 6
                    mm = pe.matmul(out, w_ukv[:, h * 2 * P:h * 2 * P + P], ckv, start=True, stop=True)
                else:
                    t = i - 10
                    mm = pe.matmul(out, ckv[:, t * P:(t + 1) * P], w_ukv.rearrange("p (h c) -> p h c", h=HEADS)[:, :, NOPE:NOPE + VD],
                                   start=True, stop=True)
                mm.then_inc(qk_mm, 1)
            for i in range(3):
                pe.wait_ge(qk_ev, 9 + i)
                pe.matmul(ps[:, 2 + i, :], rot, krg[:] if i == 0 else qr[:, i - 1, :], start=True, stop=True).then_inc(rot_mm, 1)
            for s in range(2 * HEADS):
                h, key = s // 2, s % 2
                if s >= 2:
                    pe.wait_ge(head_root, s - 1)
                half = slice(ROPE * (h % 2), ROPE * (h % 2 + 1))
                pe.matmul(ps[:, 6 + key, :], ones[:], sqs[:, (6 if key else 0) + h, :], start=True, stop=False)
                pe.matmul(ps[:, 6 + key, :], ones[half, :], sqs[half, 10 if key else 4 + h // 2, :], start=False, stop=True).then_inc(head_ss, 1)
            pe.wait_ge(qk_ev, 14)
            for i in range(4 * HEADS + 2):
                if i < 4 * HEADS:
                    h, q0 = i // TT, (i % TT) * P
                    pe.wait_ge(qk_ready, h + 1)
                    if i >= 3:
                        pe.wait_ge(exp_done, i - 2)
                    half = slice(ROPE * (h % 2), ROPE * (h % 2 + 1))
                    pe.matmul(ps[:, i % 3, :], qn[:, h, q0:q0 + P], kn[:, h, :], start=True, stop=False)
                    pe.matmul(ps[:, i % 3, :], qr[half, h // 2, q0:q0 + P], kr[half, h // 2, :], start=False, stop=True).then_inc(s_done, 1)
                j = i - 1
                if 0 <= j < 4 * HEADS:
                    pe.wait_ge(diag_ready, j + 1)
                    if j >= 2:
                        pe.wait_ge(pt_ev, j - 1)
                    for kc in range(TT):
                        mm = pe.matmul(ps[:, 3 + j % 2, kc * P:(kc + 1) * P], prob[:, j % 2, kc * P:(kc + 1) * P], diag[:, j % 2, :], start=True, stop=True)
                    mm.then_inc(t_done, 1)
                if i >= 5 and i % TT == 1:
                    h = (i - 5) // TT
                    pe.wait_ge(pt_ev, TT * (h + 1))
                    if h >= 1:
                        pe.wait_ge(pv_ev, h)
                    for kc in range(TT):
                        mm = pe.matmul(ps[:, 5, :], V[:, kc, h * VD:(h + 1) * VD], PT[:, kc, :], start=(kc == 0), stop=(kc == TT - 1))
                    mm.then_inc(pv_done, 1)
            for c in range(CT):
                pe.wait_ge(conv_done, c + 1)
                mm = pe.matmul(ps[:, 6, :], ones[:], acc[:, c, :], start=(c == 0), stop=(c == CT - 1))
            mm.then_inc(cmean, 1)
            for c in range(CT):
                pe.wait_ge(csq, c + 1)
                mm = pe.matmul(ps[:, 7, :], ones[:], scr[:, c, :], start=(c == 0), stop=(c == CT - 1))
            mm.then_inc(cvar, 1)
            pe.wait_ge(w_out_in, 32)
            pe.wait_ge(pv_ev, HEADS)
            pe.wait_ge(cmix, CT)
            for dt in range(KT):
                for kt in range(KT):
                    mm = pe.matmul(ps[:, dt, :], w_out[:, kt, dt * P:(dt + 1) * P], mix[:, kt, :], start=(kt == 0), stop=(kt == KT - 1))
                mm.then_inc(wout_done, 1)
            norm(1)
            pe.wait_ge(w_r_in, 16)
            pe.wait_ge(h_ready, 2 * KT)
            for t in range(TT):
                for kt in range(KT):
                    mm = pe.matmul(ps[:, 0, t * EXPERTS:(t + 1) * EXPERTS], hT[:, kt, t * P:(t + 1) * P], w_r[:, kt, :], start=(kt == 0), stop=(kt == KT - 1))
            mm.then_inc(r_done, 1)
            for i in range(2 * TT):
                t, g = i // 2, i % 2
                if i >= 4:
                    pe.wait_ge(htok_ev, i - 3)
                for b in range(4):
                    kt = 4 * g + b
                    mm = pe.transpose(ps[:, 2 + i % 4, b * P:(b + 1) * P], hT[:, kt, t * P:(t + 1) * P], ident)
                mm.then_inc(htok_mm, 1)
            pe.wait_ge(aff_ready, 1)
            for t in range(TT):
                mm = pe.transpose(ps[0:EXPERTS, 1, t * P:(t + 1) * P], aff[:, t, :], ident)
            mm.then_inc(affT_done, 1)
            pe.wait_ge(rank_ready, 1)
            for t in range(TT):
                mm = pe.transpose(ps[:, 6, t * EXPERTS:(t + 1) * EXPERTS], rankm[:, t * P:(t + 1) * P], ident[0:EXPERTS, 0:EXPERTS])
            mm.then_inc(rankT_done, 1)
            pe.wait_ge(htok_ev, 2 * TT)
            with pe.Fori(0, EXPERTS) as e:
                pe.wait_ge(s_built, e + 1)
                for kt in range(KT):
                    for t in range(TT):
                        mm = pe.matmul(ps[:, 0, kt * CAP:(kt + 1) * CAP], h_tok3[:, t, kt * P:(kt + 1) * P], s_e[:, t, 0:CAP], start=(t == 0), stop=(t == TT - 1))
                mm.then_inc(xe_mm, 1)
                pe.wait_ge(st_free, e + 1)
                for t in range(TT):
                    pe.matmul(ps[:, 7, 0:1], s_e[:, t, :], aff[:, t, bass.ds(e, 1)], start=(t == 0), stop=(t == TT - 1))
                pe.matmul(ps[:, 6, :], sel_e[:], rankm, start=True, stop=True).then_inc(st_mm, 1)
                pe.wait_ge(xe_ready, e + 1)
                for j in range(4):
                    pe.wait_ge(chunk_in[j], 16 * e + 16)
                    for k in range(4):
                        kt = 4 * (j % 2) + k
                        for half in range(2):
                            mm = pe.matmul(ps[CAP * half:CAP * (half + 1), 1 + j // 2, :], x_e[:, kt * CAP:(kt + 1) * CAP],
                                           chunk[j][:, k, half * HALF:(half + 1) * HALF], start=(kt == 0), stop=(kt == KT - 1))
                    mm.then_inc(chunk_used, 1)
                pe.wait_ge(hid_ready, e + 1)
                for b in range(4):
                    mm = pe.transpose(ps[:, 3, b * P:(b + 1) * P], hid[:, b * P:(b + 1) * P], ident)
                mm.then_inc(hidT_mm, 1)
                pe.wait_ge(hidT_ready, e + 1)
                pe.wait_ge(ye_free, e + 1)
                for j in range(4, 6):
                    pe.wait_ge(chunk_in[j], 16 * e + 16)
                    for k in range(4):
                        at_f = k * P + CAP * (j - 4)
                        for half in range(2):
                            mm = pe.matmul(ps[CAP * half:CAP * (half + 1), 4, :], hidT[:, at_f:at_f + CAP],
                                           chunk[j][:, k, half * HALF:(half + 1) * HALF], start=(j == 4 and k == 0), stop=(j == 5 and k == 3))
                    mm.then_inc(chunk_used, 1)
            pe.wait_ge(ye_free, EXPERTS + 1)
            pe.wait_ge(st_free, EXPERTS + 1)
            for e in range(EXPERTS):
                for b in range(4):
                    for half in range(2):
                        rows = slice(CAP * half, CAP * (half + 1))
                        mm = pe.matmul(ps[:, 4 * half + b, :], ye[rows, e, b * P:(b + 1) * P], ohT[rows, e, :], start=(e == 0), stop=(e == EXPERTS - 1))
            mm.then_inc(out_done, 1)

        @block.scalar
        def _(act):
            step = Steps(act, a_step)
            row = 0
            for name, n in (("norm1_g", KT), ("norm2_g", KT), ("b_ada", N_MOD * KT), ("q_latent_g", 2), ("kv_latent_g", 1),
                            ("conv_b", CT), ("conv_norm_g", CT), ("conv_norm_b", CT)):
                act.dma_start(rowsA[row:row + n, :], at(name).rearrange("a (k p) -> (a k) p", p=P)).then_inc(rows_in, 16)
                row += n
            act.dma_start(rowsA[QHG:QHG + 1, :], at("q_head_g")[:, 0:NOPE]).then_inc(rows_in, 16)
            act.dma_start(rowsA[KHG:KHG + 1, :], at("k_head_g")[:, 0:NOPE]).then_inc(rows_in, 16)
            for r, name in ((QRG, "q_head_g"), (KRG, "k_head_g")):
                act.dma_start(rowsA[r:r + 1, :].rearrange("p (a n) -> p a n", a=2),
                              at(name)[:, NOPE:QK].unsqueeze(1).to_broadcast([1, 2, ROPE])).then_inc(rows_in, 16)
            act.dma_start(rowsB[0:TAPS * CT, :], at("conv_w").rearrange("a t (c p) -> (a t c) p", p=P)).then_inc(rows_in, 16)

            def norm(k, shift):
                for kt in range(KT):
                    if KT * k + kt >= 4:
                        act.wait_ge(n_ss, KT * k + kt - 3)
                    if k == 1:
                        act.wait_ge(x1_ready, kt + 1)
                    act.activation(scr[:, kt % 4, :], xT[:, kt, :], ACT.Square).then_inc(n_sq, 1)
                act.wait_ge(n_ss, KT * (k + 1))
                act.activation(krg[:], ps[:, 6 - 6 * k, :], ACT.Sqrt, bias=eps, scale=1.0 / D).then_inc(n_root, 1)

            def modulate(k, shift):
                for kt in range(KT):
                    act.wait_ge(n_xn, KT * k + kt + 1)
                    act.activation(hT[:, kt, :], hT[:, kt, :], ACT.Identity, bias=mod[:, shift + kt:shift + kt + 1],
                                   scale=smod[:, KT * k + kt:KT * k + kt + 1]).then_inc(h_ready, 1)

            norm(0, SHIFT1)
            for r in range(3):
                act.wait_ge(ada_used, 2 * r + 2)
                act.activation(sqs[:, r, :], ps[:, r, :], ACT.Copy).then_inc(ada_rows, 1)
            act.wait_ge(mod_ready, 1)
            modulate(0, SHIFT1)
            for c in range(CT):
                act.wait_ge(proj, 2 * c + 1)
                if c >= 1:
                    act.wait_ge(dve_proj, c)
                act.activation(sig, ps[:, (2 * c) % 6, :], ACT.Sigmoid).then_inc(act_proj, 1)
            for i in range(3):
                act.wait_ge(proj, 9 + i)
                bank = (8 + i) % 6
                act.activation(scr[:, i, :], ps[:, bank, :], ACT.Square).then_inc(lat_sq, 1)
                act.activation(cq[:, i, :] if i < 2 else ckv, ps[:, bank, :], ACT.Copy).then_inc(act_proj, 1)
            act.wait_ge(proj, 12)
            act.activation(sqs[:, 10, :], ps[:, 5, :], ACT.Square)
            act.activation(krg[:], ps[:, 5, :], ACT.Identity, scale=vec[:, KRG:KRG + 1]).then_inc(act_proj, 1)
            for i, width in enumerate((Q_RANK, KV_RANK)):
                act.wait_ge(lat_ss, 2 + i)
                act.activation(rin[:, i, :], ps[:, 6 + i, :], ACT.Sqrt, bias=eps, scale=1.0 / width).then_inc(lat_root, 1)
            for i in range(14):
                act.wait_ge(qk_mm, i + 1)
                src = ps[:, i % 6, :]
                if i < 6 and i % 3 < 2:
                    h = 2 * (i // 3) + i % 3
                    act.activation(sqs[:, h, :], src, ACT.Square)
                    act.activation(qn[:, h, :], src, ACT.Identity, scale=vec[:, QHG:QHG + 1]).then_inc(qk_ev, 1)
                elif i < 6:
                    act.activation(sqs[:, 4 + i // 3, :], src, ACT.Square)
                    act.activation(qr[:, i // 3, :], src, ACT.Identity, scale=vec[:, QRG:QRG + 1]).then_inc(qk_ev, 1)
                elif i < 10:
                    act.activation(sqs[:, i, :], src, ACT.Square)
                    act.activation(kn[:, i - 6, :], src, ACT.Identity, scale=vec[:, KHG:KHG + 1]).then_inc(qk_ev, 1)
                else:
                    act.activation(V[:, i - 10, :], src, ACT.Copy).then_inc(qk_ev, 1)
            for s in range(2 * HEADS):
                h, key = s // 2, s % 2
                act.wait_ge(head_ss, s + 1)
                act.activation(rin[:, HEADS * key + h, :], ps[:, 6 + key, :], ACT.Sqrt, bias=eps, scale=1.0 / QK).then_inc(head_root, 1)
            for i in range(4 * HEADS + 3):
                if i < 4 * HEADS:
                    act.wait_ge(nm_ready, i + 1)
                    if i >= 2:
                        act.wait_ge(t_done, i - 1)
                    act.activation(prob[:, i % 2, :], ps[:, i % 3, :], ACT.Exp, bias=nmx[:, i:i + 1], scale=QSCALE,
                                   accum_out=rsum[:, i:i + 1]).then_inc(exp_done, 1)
                j = i - 1
                if 0 <= j < 4 * HEADS:
                    act.wait_ge(t_done, j + 1)
                    if j >= TT and j % TT == 0:
                        act.wait_ge(pv_done, j // TT)
                    act.activation(PT[:, :, (j % TT) * P:(j % TT + 1) * P], ps[:, 3 + j % 2, :].rearrange("p (c n) -> p c n", c=TT), ACT.Copy).then_inc(pt_ev, 1)
                if i >= 6 and i % TT == 2:
                    h = (i - 6) // TT
                    act.wait_ge(pv_done, h + 1)
                    act.activation(mix[:, h, :], ps[:, 5, :], ACT.Copy).then_inc(pv_ev, 1)
            for c in range(CT):
                act.wait_ge(cdev, c + 1)
                act.activation(scr[:, c, :], acc[:, c, :], ACT.Square).then_inc(csq, 1)
            act.wait_ge(cvar, 1)
            act.activation(rin[:, 0, :], ps[:, 7, :], ACT.Sqrt, bias=eps, scale=1.0 / CONV_CH).then_inc(croot, 1)
            for c in range(CT):
                act.wait_ge(cnorm, c + 1)
                act.activation(mix[:, HEADS + c, :], acc[:, c, :], ACT.Silu, bias=vec[:, CNB + c:CNB + c + 1], scale=vec[:, CNG + c:CNG + c + 1]).then_inc(cmix, 1)
            norm(1, SHIFT2)
            modulate(1, SHIFT2)
            act.wait_ge(r_sub, 1)
            act.activation(lg[:], lg[:], ACT.Exp).then_inc(r_exp, 1)
            for i in range(2 * TT):
                act.wait_ge(htok_mm, i + 1)
                act.activation(h_tok3[:, i // 2, (i % 2) * HALF:(i % 2 + 1) * HALF], ps[:, 2 + i % 4, :], ACT.Copy).then_inc(htok_ev, 1)
            act.activation(stat[:, 0:1], stat[:, 0:1], ACT.Copy).then_inc(ye_free, 1)
            with act.Fori(0, EXPERTS) as e:
                act.wait_ge(xe_mm, e + 1)
                act.activation(x_e, ps[:, 0, :], ACT.Copy).then_inc(xe_ready, 1)
                act.wait_ge(chunk_used, 6 * e + 2)
                act.activation(sg, ps[:, 1, :], ACT.Silu).then_inc(sg_ready, 1)
                act.wait_ge(hidT_mm, e + 1)
                act.activation(hidT, ps[:, 3, :], ACT.Copy).then_inc(hidT_ready, 1)
                act.wait_ge(chunk_used, 6 * e + 6)
                act.wait_ge(st_free, e + 2)
                act.activation(ye[:, bass.ds(e, 1), :].rearrange("p a n -> p (a n)"), ps[:, 4, :], ACT.Identity, scale=gcol[:]).then_inc(ye_free, 1)

        @block.vector
        def _(dve):
            step = Steps(dve, d_step)
            dve.wait_ge(rowsT_done, 1)
            dve.tensor_copy(vec[:], ps[:, 5, 0:NVEC]).then_inc(vec_ready, 1)
            dve.wait_ge(rowsT_done, 2)
            dve.tensor_copy(convw[:], ps[:, 7, 0:TAPS * CT]).then_inc(vec_ready, 1)

            def norm(k):
                dve.wait_ge(n_root, k + 1)
                step(dve.reciprocal(krg[:], krg[:]))
                step.settle()
                for kt in range(KT):
                    dve.tensor_tensor(hT[:, kt, :], xT[:, kt, :], krg[:], ALU.mult).then_inc(n_xn, 1)

            norm(0)
            dve.wait_ge(vec_ready, 2)
            for r in range(3):
                dve.wait_ge(ada_cols, r + 1)
                step(dve.tensor_tensor(mod[:, 16 * r:16 * r + 16].rearrange("p (g b) -> p b g", g=4),
                                       ps[:, 3 + r, :].rearrange("p (b g k) -> p b g k", b=4, g=4)[:, :, :, 0],
                                       vec[:, ADA + 16 * r:ADA + 16 * r + 16].rearrange("p (g b) -> p b g", g=4), ALU.add))
            step.settle()
            step(dve.scalar_tensor_tensor(smod[:, 0:KT], mod[:, SCALE1:SCALE1 + KT], 1.0, vec[:, N1G:N1G + KT], ALU.add, ALU.mult))
            dve.scalar_tensor_tensor(smod[:, KT:2 * KT], mod[:, SCALE2:SCALE2 + KT], 1.0, vec[:, N2G:N2G + KT], ALU.add, ALU.mult).then_inc(mod_ready, 1)

            def taps():
                for c in range(CT):
                    for t in range(TAPS):
                        w, src = convw[:, t * CT + c:t * CT + c + 1], ypad[:, c, t:t + S]
                        if t == 0:
                            dve.wait_ge(dve_proj, c + 1)
                            op = dve.tensor_scalar(acc[:, c, :], src, w, vec[:, CB + c:CB + c + 1], ALU.mult, ALU.add)
                        else:
                            step.settle()
                            op = dve.scalar_tensor_tensor(acc[:, c, :], src, w, acc[:, c, :], ALU.mult, ALU.add)
                        if t == TAPS - 1:
                            op.then_inc(conv_done, 1)
                        else:
                            step(op)
                        yield
            conv = taps()

            def convolve(n):
                for _ in range(n):
                    next(conv, None)

            dve.wait_ge(pad_zero, 1)
            for c in range(CT):
                dve.wait_ge(act_proj, c + 1)
                dve.wait_ge(proj, 2 * c + 2)
                dve.tensor_tensor(ypad[:, c, PAD:PAD + S], ps[:, (2 * c + 1) % 6, :], sig, ALU.mult).then_inc(dve_proj, 1)
                convolve(14)
            for i in range(2):
                dve.wait_ge(lat_root, i + 1)
                step(dve.reciprocal(rin[:, i, :], rin[:, i, :]))
            step.settle()
            dve.wait_ge(act_proj, 7)
            for i in range(2):
                dve.scalar_tensor_tensor(cq[:, i, :], cq[:, i, :], vec[:, QLG + i:QLG + i + 1], rin[:, 0, :], ALU.mult, ALU.mult).then_inc(lat_ready, 1)
            dve.scalar_tensor_tensor(ckv, ckv, vec[:, KVG:KVG + 1], rin[:, 1, :], ALU.mult, ALU.mult).then_inc(lat_ready, 1)
            convolve(8)
            dve.wait_ge(uq_in, 48)
            ropes = (krg[:], qr[:, 0, :], qr[:, 1, :])
            for i, x in enumerate(ropes):
                dve.wait_ge(rot_mm, i + 1)
                step(dve.tensor_tensor(scr[:, 3, :], ps[:, 2 + i, :], sin, ALU.mult))
                step(dve.tensor_tensor(x, x, cos, ALU.mult))
                step.settle()
                step(dve.tensor_tensor(x, x, scr[:, 3, :], ALU.add))
                step.settle()
            for h in range(HEADS):
                half = slice(ROPE * (h % 2), ROPE * (h % 2 + 1))
                dve.wait_ge(head_root, 2 * h + 2)
                step(dve.reciprocal(rin[:, h, :], rin[:, h, :]))
                step(dve.reciprocal(rin[:, HEADS + h, :], rin[:, HEADS + h, :]))
                step.settle()
                dve.tensor_tensor(qn[:, h, :], qn[:, h, :], rin[:, h, :], ALU.mult)
                dve.tensor_tensor(kn[:, h, :], kn[:, h, :], rin[:, HEADS + h, :], ALU.mult)
                dve.tensor_tensor(qr[half, h // 2, :], qr[half, h // 2, :], rin[half, h, :], ALU.mult)
                dve.tensor_tensor(kr[half, h // 2, :], krg[half, :], rin[half, HEADS + h, :], ALU.mult).then_inc(qk_ready, 1)
            for i in range(4 * HEADS + 1):
                if i < 4 * HEADS:
                    dve.wait_ge(s_done, i + 1)
                    step(dve.reduce_max(mx[:, i:i + 1], ps[:, i % 3, :], AX_X))
                    step.settle()
                    dve.tensor_scalar(nmx[:, i:i + 1], mx[:, i:i + 1], -QSCALE, None, ALU.mult).then_inc(nm_ready, 1)
                j = i - 1
                if j >= 0:
                    dve.wait_ge(exp_done, j + 1)
                    step(dve.reciprocal(rrs[:, j:j + 1], rsum[:, j:j + 1]))
                    step.settle()
                    if j >= 2:
                        dve.wait_ge(t_done, j - 1)
                    dve.tensor_scalar(diag[:, j % 2, :], ident, rrs[:, j:j + 1], None, ALU.mult).then_inc(diag_ready, 1)
                convolve(4)
            convolve(CT * TAPS)
            dve.wait_ge(cmean, 1)
            for c in range(CT):
                dve.scalar_tensor_tensor(acc[:, c, :], ps[:, 6, :], -1.0 / CONV_CH, acc[:, c, :], ALU.mult, ALU.add).then_inc(cdev, 1)
            dve.wait_ge(croot, 1)
            step(dve.reciprocal(rin[:, 0, :], rin[:, 0, :]))
            step.settle()
            dve.wait_ge(csq, CT)
            dve.wait_ge(cdev, CT)
            for c in range(CT):
                dve.tensor_tensor(acc[:, c, :], acc[:, c, :], rin[:, 0, :], ALU.mult).then_inc(cnorm, 1)
            for dt in range(KT):
                dve.wait_ge(wout_done, dt + 1)
                dve.scalar_tensor_tensor(xT[:, dt, :], ps[:, dt, :], mod[:, GATE1 + dt:GATE1 + dt + 1], xT[:, dt, :], ALU.mult, ALU.add).then_inc(x1_ready, 1)
            dve.wait_ge(x1_ready, KT)
            norm(1)
            dve.wait_ge(r_done, 1)
            logits = ps[:, 0, 0:TT * EXPERTS].rearrange("p (t e) -> p t e", t=TT)
            step(dve.reduce_max(mx[:, 0:TT], logits, AX_X))
            step.settle()
            dve.tensor_tensor(lg[:], logits, mx[:, 0:TT].unsqueeze(2).to_broadcast([P, TT, EXPERTS]), ALU.subtract).then_inc(r_sub, 1)
            dve.wait_ge(r_exp, 1)
            step(dve.reduce_sum(rsum[:, 0:TT], lg[:], AX_X))
            step.settle()
            step(dve.reciprocal(rrs[:, 0:TT], rsum[:, 0:TT]))
            step.settle()
            dve.tensor_tensor(aff[:], lg[:], rrs[:, 0:TT].unsqueeze(2).to_broadcast([P, TT, EXPERTS]), ALU.mult).then_inc(aff_ready, 1)
            dve.wait_ge(affT_done, 1)
            step(dve.tensor_copy(work, ps[0:EXPERTS, 1, :]))
            for _ in range(CAP // 8):
                step.settle()
                step(dve.max(top8[:], work))
                step.settle()
                step(dve.match_replace(work, top8[:], work, -1.0))
            step.settle()
            step(dve.tensor_scalar(affT, work, 0.0, None, ALU.is_lt))
            step.settle()
            step(dve.tensor_tensor_scan(rank, affT, affT, 0.0, ALU.add, ALU.max))
            step.settle()
            step(dve.tensor_tensor(rank, rank, affT, ALU.mult))
            step.settle()
            dve.tensor_scalar(rankm, rank, -1.0, None, ALU.add).then_inc(rank_ready, 1)
            dve.wait_ge(rankT_done, 1)
            step(dve.tensor_copy(rankT[:].rearrange("p t e -> p (t e)"), ps[:, 6, 0:TT * EXPERTS]))
            step.settle()
            dve.memset(gcol[:], 0.0).then_inc(st_free, 1)

            def build(e):
                for t in range(TT):
                    dve.tensor_scalar(s_e[:, t, :], slot_row, rankT[:, t, bass.ds(e, 1)], None, ALU.is_equal)
                dve.tensor_scalar(sel_e[:], ones[0:EXPERTS, :], const[0:EXPERTS, bass.ds(e, 1)], None, ALU.mult).then_inc(s_built, 1)

            with dve.Fori(0, EXPERTS) as e:
                dve.wait_ge(st_free, e + 1)
                build(e)
                dve.wait_ge(st_mm, e + 1)
                dve.wait_ge(ye_free, e + 1)
                dve.tensor_copy(gcol[:], ps[:, 7, 0:1])
                dve.tensor_scalar(ohT[:, bass.ds(e, 1), :].rearrange("p a n -> p (a n)"), ps[:, 6, :], slot_col, None, ALU.is_equal).then_inc(st_free, 1)
                dve.wait_ge(sg_ready, e + 1)
                dve.wait_ge(chunk_used, 6 * e + 4)
                dve.tensor_tensor(hid, sg, ps[:, 2, :], ALU.mult).then_inc(hid_ready, 1)
            dve.wait_ge(out_done, 1)
            for dt in range(KT):
                dve.scalar_tensor_tensor(xT[:, dt, :], ps[:, dt, :], mod[:, GATE2 + dt:GATE2 + dt + 1], xT[:, dt, :], ALU.mult, ALU.add).then_inc(x2_ready, 1)


def memory(nc, ctx):
    def sb(name, shape, dt=F32):
        return ctx.enter_context(nc.sbuf_tensor(name, shape, dt))
    M = dict(ps=ctx.enter_context(nc.psum_tensor("ps", [P, 8, 512], F32)))
    for name, shape in dict(
        const=[P, C_ALL], ones=[P, P], xT=[P, KT, S],
    ).items():
        M[name] = sb(name, shape)
    return M


def memory1(nc, ctx, M):
    M = dict(M)
    for name, shape in dict(
        hy=[P, 2 * KT * S], h_tok=[P, TT * D], one_hot_T=[P, EXPERTS * S], ring=[P, 6 * TT * D], scr=[P, 4, S],
        krg=[P, S], c_rep=[P, KT, 32], vec=[P, NVEC], convw=[P, TAPS * CT],
        mod=[P, N_MOD * KT], smod=[P, 2 * KT], stat=[P, 64],
        lg=[P, TT, EXPERTS], aff=[P, TT, EXPERTS], rankT=[P, TT, EXPERTS], top8=[EXPERTS, 8],
        sel_e=[EXPERTS, P], gcol=[P, 1],
    ).items():
        M[name] = ctx.enter_context(nc.sbuf_tensor(name, shape, F32))
    return M

MEM = 256
MT = MEM // P
GROUPS_A = 8
B_W, B_HEADS, TAPS_B = 1280, 10, 4
C_HEADS, C_DIM = 4, 256
A_W, C_W = 1024, C_HEADS * C_DIM
EXP_GROUPS, PER_GROUP, FF2 = 4, 4, 256
ALPHA = 2.0 ** 0.25
CSCALE = C_DIM ** -0.5
LRU_C = 8.0
Z_U, Z_V, Z_X, Z_G, Z_Q, Z_M = 0, A_W, 2 * A_W, 2 * A_W + B_W, 2 * A_W + 2 * B_W, 2 * A_W + 2 * B_W + C_W
IN_W2 = Z_M + 3 * D
LIFT = 2.0 ** 60
V_BIN, V_CB, V_BA, V_BX, V_LAM, NV1 = 0, 68, 78, 88, 98, 108
V_CW, V_BO, V_LIG, V_LIB, V_LMG, V_LMB, V_L1G, V_L1B, V_L2G, V_L2B, NV2 = (108 + n for n in (0, 40, 48, 56, 64, 72, 80, 88, 96, 104, 112))


def second(nc, A, sem, M):
    ps, const, xT, ones = M["ps"], M["const"], M["xT"], M["ones"]
    ident = const[:, C_IDENT:C_IDENT + P]
    eps = const[:, C_EPS5:C_EPS5 + 1]
    ring, flat, u, v, ob, wT, vec, lru = (M[n] for n in ("ring2", "tmp", "u", "v", "ob", "wT", "vec2", "lru"))
    tmp = flat[:, 0:10 * S].rearrange("p (k n) -> p k n", k=10)
    y, small = M["y"], M["small"]
    slot = [ring[:, i * 4096:(i + 1) * 4096].rearrange("p (k n) -> p k n", k=KT) for i in range(6)]
    rows1, rows2 = u[:, 0, 0:P], u[:, 1, 0:P]
    v3 = v[:].rearrange("p (t d) -> p t d", t=TT)
    wab = v[:, 0:2 * B_HEADS * P].rearrange("p (h n) -> p h n", h=2 * B_HEADS)
    row_in_y = y[:].rearrange("p k n -> p (k n)")
    bv_row, lvg_row, lvb_row, bs_row = (row_in_y[:, i * D:(i + 1) * D] for i in range(4))
    w_s = ob[:, 0:2, :].rearrange("p a n -> p (a n)").rearrange("p (g s) -> p g s", g=GROUPS_A)
    padded = S + TAPS_B - 1
    xpad = [flat[:, 8 * S + i * padded:8 * S + (i + 1) * padded] for i in range(2)]
    xc, gt = [tmp[:, i, :] for i in range(2)], [tmp[:, 2 + i, :] for i in range(2)]
    rr, ii, aa, th = (tmp[:, 4 + i, :] for i in range(4))
    gate_sg = [tmp[:, 8 + i, :] for i in range(2)]
    mem_tok = flat[:, 0:MT * D].rearrange("p (t d) -> p t d", t=MT)
    memT = flat[:, 2048:2048 + KT * MEM].rearrange("p (k m) -> p k m", k=KT)
    kT = v[:, 0:KT * MEM].rearrange("p (k m) -> p k m", k=KT)
    vm = v[:, 2048:2048 + MT * C_W].rearrange("p (t d) -> p t d", t=MT)
    prob = flat[:, 0:512].rearrange("p (i m) -> p i m", i=2)
    PT = flat[:, 512:1536].rearrange("p (c n) -> p c n", c=MT)
    diag = flat[:, 1536:1792].rearrange("p (i n) -> p i n", i=2)
    obf = ob[:].rearrange("p k n -> p (k n)")
    w_g = obf[:, 0:KT * 20].rearrange("p (k n) -> p k n", k=KT)
    bg_row = obf[:, 160:180]
    gl = obf[:, 256:256 + TT * 20].rearrange("p (t n) -> p t n", t=TT)
    gw = [obf[:, 512 + 64 * i:512 + 64 * (i + 1)].rearrange("p (t n) -> p t n", t=TT) for i in range(6)]
    gateT = obf[0:EXPERTS, 1024:1536]
    sel = obf[0:EXPERTS, 1536:2048].rearrange("p (j n) -> p j n", j=PER_GROUP)
    prio = small[:, 0:4]

    rows_in2, rows_turned, vec2_ready, bc_in, wab_in, ws_in, wg_in, mem_in = (
        sem(n) for n in ("rows_in2", "rows_turned", "vec2_ready", "bc_in", "wab_in", "ws_in", "wg_in", "mem_in"))
    slot_in = [sem(f"slot_in{i}") for i in range(6)]
    l_sum, l_dev, l_sq, l_ss, l_root, l_norm, l_ready = (sem(n) for n in ("l_sum", "l_dev", "l_sq", "l_ss", "l_root", "l_norm", "l_ready"))
    bz_mm, bz_ev, xc_ready, bg_mm, bg_ev, at_ready, m2_ready, mult_ready, ob_ready, lru_ready, pads_zero = (
        sem(n) for n in ("bz_mm", "bz_ev", "xc_ready", "bg_mm", "bg_ev", "at_ready", "m2_ready", "mult_ready", "ob_ready", "lru_ready", "pads_zero"))
    lru_exp = sem("lru_exp")
    ws_turned, ws_kept, wT_ready = sem("ws_turned"), sem("ws_kept"), sem("wT_ready")
    v_mm, v_biased, v_gelu, v_var, v_root, v_ready, u_mm, u_ready, sp_mm, oa_ready = (
        sem(n) for n in ("v_mm", "v_biased", "v_gelu", "v_var", "v_root", "v_ready", "u_mm", "u_ready", "sp_mm", "oa_ready"))
    m_mm, m_sg, m_y = sem("m_mm"), sem("m_sg"), sem("m_y")
    mem_var, mem_root, mem_norm, memT_mm, memT_ready, kv_mm, kv_ready, q_mm, q_ready = (
        sem(n) for n in ("mem_var", "mem_root", "mem_norm", "memT_mm", "memT_ready", "kv_mm", "kv_ready", "q_mm", "q_ready"))
    cs_done, cnm_ready, cexp_done, cdiag_ready, ct_done, cpt_ev, cpv_done, oc_ready = (
        sem(n) for n in ("cs_done", "cnm_ready", "cexp_done", "cdiag_ready", "ct_done", "cpt_ev", "cpv_done", "oc_ready"))
    ax_ready, wo_mm, wo_used = sem("ax_ready"), sem("wo_mm"), sem("wo_used")
    g_mm, g_sub, g_exp, e_sub, e_exp, gate_ready, gate_turned, gateT_ready, prio_ready, f_init = (
        sem(n) for n in ("g_mm", "g_sub", "g_exp", "e_sub", "e_exp", "gate_ready", "gate_turned", "gateT_ready", "prio_ready", "f_init"))
    sel_ready, bc_mm, up_mm, sg2_ready, hid2_ready, dn_mm, dn_used = (
        sem(n) for n in ("sel_ready", "bc_mm", "up_mm", "sg2_ready", "hid2_ready", "dn_mm", "dn_used"))
    o_mm, o_kept, stored, d2_step, a2_step, m_loop = (sem(n) for n in ("o_mm", "o_kept", "stored", "d2_step", "a2_step", "m_loop"))

    def half(name, n):
        return [(slice(0, HALF), A[name][0].rearrange("(k p) n -> p k n", p=P)[:, :, n * HALF:(n + 1) * HALF])]

    def z_cols(c0):
        return [(slice(0, HALF), A["w_in_2"][0].rearrange("(k p) n -> p k n", p=P)[:, :, c0:c0 + HALF])]

    w_z = A["w_in_2"][0].rearrange("(k p) n -> p k n", p=P)
    chunks = [[(slice(0, 256), w_z[:, :, Z_X + 256 * k:Z_X + 256 * (k + 1)]), (slice(256, 512), w_z[:, :, Z_G + 256 * k:Z_G + 256 * (k + 1)])] for k in range(B_HEADS // 2)]
    CH_V = len(chunks); chunks += [z_cols(Z_V), z_cols(Z_V + HALF)]
    CH_U = len(chunks); chunks += [z_cols(Z_U), z_cols(Z_U + HALF)]
    CH_MA = len(chunks); chunks += [z_cols(Z_M), half("p_a_2", 0), z_cols(Z_M + HALF), half("p_a_2", 1)]
    CH_MB = len(chunks); chunks += [z_cols(Z_M + D), z_cols(Z_M + D + HALF), "p_b", "p_b", "p_b"]
    CH_K = len(chunks); chunks += [half("w_kv_2", n) for n in range(4)]
    CH_Q = len(chunks); chunks += [z_cols(Z_Q), z_cols(Z_Q + HALF)]
    CH_MC = len(chunks); chunks += [z_cols(Z_M + 2 * D), half("p_c_2", 0), z_cols(Z_M + 2 * D + HALF), half("p_c_2", 1)]
    CH_O = len(chunks); chunks += [half("w_o_2", 0), half("w_o_2", 1)]
    CH_E = len(chunks)
    assert CH_E % 6 == 0
    last_use = [(bz_mm, 4 * k + 4) for k in range(B_HEADS // 2)] + [(v_mm, 4), (v_mm, 8), (u_mm, 4), (u_mm, 8)]
    last_use += [(m_mm, 4), (m_mm, 4), (m_mm, 8), (m_mm, 8), (m_mm, 12), (m_mm, 16), (m_mm, 16), (m_mm, 16), (m_mm, 16)]
    last_use += [(kv_mm, 4), (kv_mm, 8), (kv_mm, 10), (kv_mm, 12), (q_mm, 4), (q_mm, 8), (m_mm, 20), (m_mm, 20), (m_mm, 24), (m_mm, 24), (wo_mm, 4), (wo_mm, 8)]
    landed, arrived = [0] * 6, []
    for i, c in enumerate(chunks):
        landed[i % 6] += 16 * (1 if c == "p_b" else len(c))
        arrived.append(landed[i % 6])
    p_b = [slot[i % 6].rearrange("p k n -> p (k n)").rearrange("p (k n) -> p k n", k=4) for i in range(CH_MB + 2, CH_MB + 5)]
    w_dn = [slot[4], slot[5]]

    with nc.Block() as block:
        @block.sync
        def _(sp):
            for i, c in enumerate(chunks):
                if i >= 6:
                    sp.wait_ge(*last_use[i - 6])
                if c == "p_b":
                    n = i - CH_MB - 2
                    k = min(4, B_HEADS - 4 * n)
                    sp.dma_start(p_b[n][:, 0:k], A["p_b_2"][0].rearrange("(k p) n -> p k n", p=P)[:, 4 * n:4 * n + k]).then_inc(slot_in[i % 6], 16)
                else:
                    for cols, src in c:
                        sp.dma_start(slot[i % 6][:, :, cols], src).then_inc(slot_in[i % 6], 16)

            def experts(g):
                for j in range(PER_GROUP):
                    if g is None:
                        sp.wait_ge(*last_use[CH_E - 6 + j])
                    else:
                        sp.wait_ge(up_mm, 16 * g + (4 * j - 12))
                    sp.dma_start(slot[j], A["w_up_2"][0, bass.ds((0 if g is None else PER_GROUP * g) + j, 1)].rearrange("e (k p) n -> p (e k) n", p=P)).then_inc(slot_in[j], 16)
                for j in range(2):
                    if g is None:
                        sp.wait_ge(*last_use[CH_E - 2 + j])
                    else:
                        sp.wait_ge(dn_mm, 8 * g + (4 * j - 4))
                    sp.dma_start(w_dn[j], A["w_down_2"][0, bass.ds(0 if g is None else PER_GROUP * g, PER_GROUP), :, j * HALF:(j + 1) * HALF]
                                 .rearrange("e (i p) n -> p (e i) n", p=P)).then_inc(slot_in[4 + j], 16)

            experts(None)
            with sp.Fori(1, EXP_GROUPS) as g:
                experts(g)
            out = A["out"][0].rearrange("(t p) d -> p t d", p=P)
            for t in range(TT):
                sp.wait_ge(o_kept, 2 * t + 2)
                sp.dma_start(out[:, t], v3[:, t]).then_inc(stored, 16)
            sp.wait_ge(stored, 16 * TT)

        @block.gpsimd
        def _(pool):
            for i in range(2):
                zero = pool.memset(xpad[i][:, 0:TAPS_B - 1], 0.0)
            zero.then_inc(pads_zero, 1)
            for n in range(4):
                last = pool.memset(prio[:, n:n + 1], float(4 - n))
            last.then_inc(prio_ready, 1)
            for dst, src in ((bv_row, A["b_in_2"][:, Z_V:Z_V + A_W]), (lvg_row, A["ln_v_g_2"]), (lvb_row, A["ln_v_b_2"]),
                             (bs_row, A["b_s_2"].rearrange("a g t -> a (g t)"))):
                pool.dma_start(dst, src.to_broadcast([P, D])).then_inc(bc_in, 16)
            pool.wait_ge(ws_kept, 2)
            pool.affine_select(out=wT[:], in_=wT[:], compare_op=ALU.is_ge, fill=0.0, base=0, pattern=[[0, GROUPS_A], [1, P]], channel_multiplier=-1).then_inc(wT_ready, 1)
            pool.wait_ge(m_y, 2 * KT)
            pool.dma_start(w_g[:, :, 0:4], A["w_rg_2"][0].rearrange("(k p) n -> p k n", p=P)).then_inc(wg_in, 16)
            pool.dma_start(w_g[:, :, 4:20], A["w_re_2"][0].rearrange("(k p) n -> p k n", p=P)).then_inc(wg_in, 16)
            pool.dma_start(bg_row[:, 0:4], A["b_rg_2"].to_broadcast([P, 4])).then_inc(wg_in, 16)
            pool.dma_start(bg_row[:, 4:20], A["b_re_2"].to_broadcast([P, 16])).then_inc(wg_in, 16)

        @block.tensor
        def _(pe):
            def chunk_in(i):
                pe.wait_ge(slot_in[i % 6], arrived[i])

            def layer_norm(k, x):
                for kt in range(KT):
                    mm = pe.matmul(ps[:, 0, :], ones[:], x[:, kt, :], start=(kt == 0), stop=(kt == KT - 1))
                mm.then_inc(l_sum, 1)
                for kt in range(KT):
                    pe.wait_ge(l_sq, KT * k + kt + 1)
                    pe.matmul(ps[:, 1, :], ones[:], tmp[:, kt % 4, :], start=(kt == 0), stop=(kt == KT - 1)).then_inc(l_ss, 1)

            def z_tile(bank, i, n):
                for kt in range(KT):
                    mm = pe.matmul(ps[:, bank, :], slot[i % 6][:, kt, n * P:(n + 1) * P], xT[:, kt, :], start=(kt == 0), stop=(kt == KT - 1))
                return mm

            pe.wait_ge(rows_in2, 16 * 15)
            pe.transpose(ps[:, 6, 0:NV1], rows1[0:NV1, :], ident[0:NV1, 0:NV1]).then_inc(rows_turned, 1)
            pe.transpose(ps[:, 7, 0:NV2 - NV1], rows2[0:NV2 - NV1, :], ident[0:NV2 - NV1, 0:NV2 - NV1]).then_inc(rows_turned, 1)
            pe.wait_ge(ws_in, 16)
            for g in range(GROUPS_A):
                mm = pe.transpose(ps[:, 2 + g // 4, (g % 4) * P:(g % 4 + 1) * P], w_s[:, g, :], ident)
                if g % 4 == 3:
                    mm.then_inc(ws_turned, 1)
            layer_norm(0, xT)
            pe.wait_ge(l_ready, KT)
            pe.wait_ge(ws_kept, 2)
            pe.wait_ge(vec2_ready, 2)
            pe.wait_ge(wab_in, 32)
            for h in range(B_HEADS + 1):
                if h < B_HEADS:
                    chunk_in(h // 2)
                    for part in range(2):
                        i = 2 * h + part
                        if i >= 4:
                            pe.wait_ge(bz_ev, i - 3)
                        z_tile(2 + i % 4, h // 2, 2 * part + h % 2).then_inc(bz_mm, 1)
                if h >= 1:
                    pe.wait_ge(xc_ready, h)
                    if h >= 2:
                        pe.wait_ge(bg_ev, h - 1)
                    pe.matmul(ps[:, 6, :], wab[:, h - 1, :], xc[(h - 1) % 2], start=True, stop=True)
                    pe.matmul(ps[:, 7, :], wab[:, B_HEADS + h - 1, :], xc[(h - 1) % 2], start=True, stop=True).then_inc(bg_mm, 1)
            pe.wait_ge(bz_ev, 2 * B_HEADS)
            for i in range(2 * TT):
                n, t = i // TT, i % TT
                chunk_in(CH_V + n)
                if i >= 4:
                    pe.wait_ge(v_biased, i - 3)
                for kt in range(KT):
                    mm = pe.matmul(ps[:, 2 + i % 4, :], xT[:, kt, t * P:(t + 1) * P], slot[(CH_V + n) % 6][:, kt, :], start=(kt == 0), stop=(kt == KT - 1))
                mm.then_inc(v_mm, 1)
            for i in range(KT):
                chunk_in(CH_U + i // 4)
                pe.wait_ge(v_biased, min(i + 5, 8))
                if i >= 4:
                    pe.wait_ge(u_ready, i - 3)
                z_tile(2 + i % 4, CH_U + i // 4, i % 4).then_inc(u_mm, 1)
            pe.wait_ge(wT_ready, 1)
            pe.wait_ge(v_ready, TT)
            pe.wait_ge(u_ready, KT)
            for g in range(GROUPS_A):
                if g >= 4:
                    pe.wait_ge(oa_ready, g - 3)
                for c in range(TT):
                    mm = pe.matmul(ps[:, 2 + g % 4, c * P:(c + 1) * P], v3[:, c, g * P:(g + 1) * P], wT[:, g, :], start=True, stop=True)
                mm.then_inc(sp_mm, 1)

            def merge_dense(branch, first, src):
                for dt in range(KT):
                    n, zc = KT * branch + dt, first + 2 * (dt // 4)
                    a = 2 + 2 * (n % 2)
                    if n >= 2:
                        pe.wait_ge(m_y, n - 1)
                    chunk_in(zc)
                    z_tile(a, zc, dt % 4)
                    chunk_in(zc + 1)
                    for kt in range(KT):
                        mm = pe.matmul(ps[:, a + 1, :], slot[(zc + 1) % 6][:, kt, (dt % 4) * P:(dt % 4 + 1) * P], src[:, kt, :], start=(kt == 0), stop=(kt == KT - 1))
                    mm.then_inc(m_mm, 1)

            pe.wait_ge(oa_ready, GROUPS_A)
            merge_dense(0, CH_MA, u)
            pe.wait_ge(ob_ready, B_HEADS)
            for dt in range(KT):
                n, zc = KT + dt, CH_MB + dt // 4
                a = 2 + 2 * (n % 2)
                pe.wait_ge(m_y, n - 1)
                chunk_in(zc)
                z_tile(a, zc, dt % 4)
                for kt in range(B_HEADS):
                    if dt == 0 and kt % 4 == 0:
                        chunk_in(CH_MB + 2 + kt // 4)
                    mm = pe.matmul(ps[:, a + 1, :], p_b[kt // 4][:, kt % 4, dt * P:(dt + 1) * P], ob[:, kt, :], start=(kt == 0), stop=(kt == B_HEADS - 1))
                mm.then_inc(m_mm, 1)
            for kt in range(KT):
                if kt < MT:
                    pe.wait_ge(mem_norm, MT)
                if kt >= 2:
                    pe.wait_ge(memT_ready, kt - 1)
                for t in range(MT):
                    mm = pe.transpose(ps[:, 6 + kt % 2, t * P:(t + 1) * P], mem_tok[:, t, kt * P:(kt + 1) * P], ident)
                mm.then_inc(memT_mm, 1)
            pe.wait_ge(memT_ready, KT)
            for i in range(KT + 2 * MT):
                c = CH_K + i // 4 if i < KT else CH_K + 2 + (i - KT) // MT
                chunk_in(c)
                if i >= 2:
                    pe.wait_ge(kv_ready, i - 1)
                for kt in range(KT):
                    go = dict(start=(kt == 0), stop=(kt == KT - 1))
                    if i < KT:
                        mm = pe.matmul(ps[:, 6 + i % 2, 0:MEM], slot[c % 6][:, kt, (i % 4) * P:(i % 4 + 1) * P], memT[:, kt, :], **go)
                    else:
                        t = (i - KT) % MT
                        mm = pe.matmul(ps[:, 6 + i % 2, :], memT[:, kt, t * P:(t + 1) * P], slot[c % 6][:, kt, :], **go)
                mm.then_inc(kv_mm, 1)
            pe.wait_ge(m_y, 2 * KT)
            for i in range(KT):
                chunk_in(CH_Q + i // 4)
                if i >= 4:
                    pe.wait_ge(q_ready, i - 3)
                z_tile(2 + i % 4, CH_Q + i // 4, i % 4).then_inc(q_mm, 1)
            pe.wait_ge(q_ready, KT)
            pe.wait_ge(kv_ready, KT + 2 * MT)
            N = C_HEADS * TT
            for i in range(N + 2):
                if i < N:
                    h, q0 = i // TT, (i % TT) * P
                    if i >= 3:
                        pe.wait_ge(cexp_done, i - 2)
                    for k in range(2):
                        mm = pe.matmul(ps[:, i % 3, 0:MEM], u[:, 2 * h + k, q0:q0 + P], kT[:, 2 * h + k, :], start=(k == 0), stop=(k == 1))
                    mm.then_inc(cs_done, 1)
                j = i - 1
                if 0 <= j < N:
                    pe.wait_ge(cdiag_ready, j + 1)
                    if j >= 2:
                        pe.wait_ge(cpt_ev, j - 1)
                    for c in range(MT):
                        mm = pe.matmul(ps[:, 3 + j % 2, c * P:(c + 1) * P], prob[:, j % 2, c * P:(c + 1) * P], diag[:, j % 2, :], start=True, stop=True)
                    mm.then_inc(ct_done, 1)
                if i >= 5 and i % TT == 1:
                    h = (i - 5) // TT
                    pe.wait_ge(cpt_ev, TT * (h + 1))
                    if h >= 1:
                        pe.wait_ge(oc_ready, h)
                    for d in range(2):
                        for c in range(MT):
                            mm = pe.matmul(ps[:, 5 + d, :], vm[:, c, h * C_DIM + d * P:h * C_DIM + (d + 1) * P], PT[:, c, :], start=(c == 0), stop=(c == MT - 1))
                    mm.then_inc(cpv_done, 1)
            pe.wait_ge(oc_ready, C_HEADS)
            merge_dense(2, CH_MC, u)
            pe.wait_ge(m_y, 3 * KT)
            for dt in range(KT):
                c = CH_O + dt // 4
                chunk_in(c)
                if dt >= 4:
                    pe.wait_ge(wo_used, dt - 3)
                for kt in range(KT):
                    mm = pe.matmul(ps[:, 2 + dt % 4, :], slot[c % 6][:, kt, (dt % 4) * P:(dt % 4 + 1) * P], y[:, kt, :], start=(kt == 0), stop=(kt == KT - 1))
                mm.then_inc(wo_mm, 1)
            pe.wait_ge(wo_used, KT)
            layer_norm(1, xT)
            pe.wait_ge(l_ready, 2 * KT)
            pe.wait_ge(wg_in, 64)
            for t in range(TT):
                for kt in range(KT):
                    mm = pe.matmul(ps[:, 7, t * 20:(t + 1) * 20], xT[:, kt, t * P:(t + 1) * P], w_g[:, kt, :], start=(kt == 0), stop=(kt == KT - 1))
            mm.then_inc(g_mm, 1)
            pe.wait_ge(gate_ready, 1)
            for t in range(TT):
                mm = pe.transpose(ps[0:EXPERTS, 6, t * P:(t + 1) * P], gw[0][:, t, :], ident)
            mm.then_inc(gate_turned, 1)
            pe.wait_ge(gateT_ready, 1)
            with pe.Fori(0, EXP_GROUPS) as g:
                pe.wait_ge(sel_ready, g + 1)
                for j in range(PER_GROUP):
                    pe.wait_ge(slot_in[j], 16 * g + landed[j] + 16)
                    pe.wait_ge(hid2_ready, 8 * g + max(1, 2 * j - 1))
                    pe.matmul(ps[:, 4 + j % 2, :], sel[:, j, :], gateT, start=True, stop=True).then_inc(bc_mm, 1)
                    for i in range(2):
                        if j > 0:
                            pe.wait_ge(hid2_ready, 8 * g + 2 * j + i)
                        for part in range(2):
                            for kt in range(KT):
                                mm = pe.matmul(ps[:, 2 * i + part, :], slot[j][:, kt, part * FF2 + i * P:part * FF2 + (i + 1) * P], xT[:, kt, :], start=(kt == 0), stop=(kt == KT - 1))
                            mm.then_inc(up_mm, 1)
                pe.wait_ge(hid2_ready, 8 * g + 9)
                for dt in range(KT):
                    pe.wait_ge(slot_in[4 + dt // 4], 16 * g + landed[4 + dt // 4] + 16)
                    pe.wait_ge(dn_used, 8 * g + dt + 1)
                    for kt in range(2 * PER_GROUP):
                        mm = pe.matmul(ps[:, 6 + dt % 2, :], w_dn[dt // 4][:, kt, (dt % 4) * P:(dt % 4 + 1) * P], u[:, kt, :], start=(kt == 0), stop=(kt == 2 * PER_GROUP - 1))
                    mm.then_inc(dn_mm, 1)
            pe.wait_ge(dn_used, 8 * EXP_GROUPS + 2)
            layer_norm(2, y)
            pe.wait_ge(l_ready, 3 * KT)
            for i in range(2 * TT):
                t, n = i // 2, i % 2
                if i >= 4:
                    pe.wait_ge(o_kept, i - 3)
                for b in range(4):
                    mm = pe.transpose(ps[:, 2 + i % 4, b * P:(b + 1) * P], y[:, 4 * n + b, t * P:(t + 1) * P], ident)
                mm.then_inc(o_mm, 1)

        @block.scalar
        def _(act):
            step = Steps(act, a2_step)
            row = 0
            for name, n in (("b_in_2", 68), ("conv_b_2", 10), ("b_a_2", 10), ("b_x_2", 10), ("lam_2", 10)):
                act.dma_start(rows1[row:row + n, :], A[name].rearrange("a (k p) -> (a k) p", p=P)).then_inc(rows_in2, 16)
                row += n
            act.dma_start(rows2[0:40, :], A["conv_w_2"].rearrange("a t (c p) -> (a t c) p", p=P)).then_inc(rows_in2, 16)
            row = 40
            for name in ("b_o_2", "ln_in_g_2", "ln_in_b_2", "ln_mem_g_2", "ln_mem_b_2", "ln1_g_2", "ln1_b_2", "ln2_g_2", "ln2_b_2"):
                src = A[name] if len(A[name].shape) == 1 else A[name].rearrange("a d -> (a d)")
                act.dma_start(rows2[row:row + KT, :], src.rearrange("(k p) -> k p", p=P)).then_inc(rows_in2, 16)
                row += KT
            act.dma_start(w_s, A["w_s_2"][0].rearrange("g t s -> t g s")).then_inc(ws_in, 16)
            act.dma_start(wab[:, 0:B_HEADS], A["w_a_2"][0].rearrange("h i j -> i h j")).then_inc(wab_in, 16)
            act.dma_start(wab[:, B_HEADS:], A["w_x_2"][0].rearrange("h i j -> i h j")).then_inc(wab_in, 16)

            def col(n):
                return vec[:, n:n + 1]

            def layer_norm(k, x, gain, bias, last=None):
                for kt in range(KT):
                    act.wait_ge(l_dev, KT * k + kt + 1)
                    if kt >= 4:
                        act.wait_ge(l_ss, KT * k + kt - 3)
                    act.activation(tmp[:, kt % 4, :], x[:, kt, :], ACT.Square).then_inc(l_sq, 1)
                act.wait_ge(l_ss, KT * (k + 1))
                act.activation(tmp[:, 4, :], ps[:, 1, :], ACT.Sqrt, bias=eps, scale=1.0 / D).then_inc(l_root, 1)
                for kt in range(KT):
                    act.wait_ge(l_norm, KT * k + kt + 1)
                    act.activation(x[:, kt, :], x[:, kt, :], ACT.Identity, bias=col(bias + kt), scale=col(gain + kt)).then_inc(l_ready, 1)

            for i in range(2):
                act.wait_ge(ws_turned, i + 1)
                act.activation(wT[:, 4 * i:4 * i + 4, :], ps[:, 2 + i, :].rearrange("p (g t) -> p g t", g=4), ACT.Copy).then_inc(ws_kept, 1)
            act.wait_ge(vec2_ready, 2)
            layer_norm(0, xT, V_LIG, V_LIB)
            act.wait_ge(lru_ready, 1)
            act.activation(lru[:, 1, :], lru[:, 0, :], ACT.Exp, scale=-1.0).then_inc(lru_exp, 1)
            act.wait_ge(pads_zero, 1)
            for h in range(B_HEADS + 1):
                if h < B_HEADS:
                    act.wait_ge(bz_mm, 2 * h + 1)
                    if h >= 2:
                        act.wait_ge(xc_ready, h - 1)
                    act.activation(xpad[h % 2][:, TAPS_B - 1:], ps[:, 2 + (2 * h) % 4, :], ACT.Identity, bias=col(V_BIN + Z_X // P + h)).then_inc(bz_ev, 1)
                    act.wait_ge(bz_mm, 2 * h + 2)
                    if h >= 2:
                        act.wait_ge(ob_ready, h - 1)
                    act.activation(gt[h % 2], ps[:, 2 + (2 * h + 1) % 4, :], ACT.Gelu_apprx_tanh, bias=col(V_BIN + Z_G // P + h)).then_inc(bz_ev, 1)
                if h >= 1:
                    k = h - 1
                    act.wait_ge(bg_mm, k + 1)
                    if k >= 1:
                        act.wait_ge(ob_ready, k)
                    step(act.activation(rr, ps[:, 6, :], ACT.Sigmoid, bias=col(V_BA + k)))
                    act.activation(ii, ps[:, 7, :], ACT.Sigmoid, bias=col(V_BX + k)).then_inc(bg_ev, 1)
                    step.settle()
                    act.wait_ge(lru_ready, 2)
                    act.activation(aa, rr, ACT.Exp, scale=lru[:, 2, k:k + 1])
                    act.activation(th, rr, ACT.Tanh, scale=lru[:, 3, k:k + 1]).then_inc(at_ready, 1)
                    act.wait_ge(m2_ready, k + 1)
                    act.activation(th, rr, ACT.Sqrt, scale=LIFT).then_inc(mult_ready, 1)
            for i in range(2 * TT):
                n, t = i // TT, i % TT
                act.wait_ge(v_biased, i + 1)
                part = v3[:, t, n * HALF:(n + 1) * HALF]
                act.activation(part, part, ACT.Gelu_apprx_tanh).then_inc(v_gelu, 1)
            for i in range(KT):
                act.wait_ge(u_mm, i + 1)
                act.activation(u[:, i, :], ps[:, 2 + i % 4, :], ACT.Gelu_apprx_tanh, bias=col(V_BIN + i)).then_inc(u_ready, 1)
            act.wait_ge(v_var, TT)
            act.activation(small[:, 16:20], small[:, 8:16].rearrange("p (t s) -> p t s", s=2)[:, :, 1], ACT.Sqrt, bias=eps).then_inc(v_root, 1)

            def merge(branch):
                for dt in range(KT):
                    n = KT * branch + dt
                    act.wait_ge(m_mm, n + 1)
                    if n >= 2:
                        act.wait_ge(m_y, n - 1)
                    act.activation(gate_sg[n % 2], ps[:, 2 + 2 * (n % 2), :], ACT.Sigmoid, bias=col(V_BIN + Z_M // P + n)).then_inc(m_sg, 1)

            merge(0)
            act.wait_ge(ob_ready, B_HEADS)
            act.dma_start(mem_tok, A["mem_2"][0].rearrange("(t p) d -> p t d", p=P)).then_inc(mem_in, 16)
            merge(1)
            act.wait_ge(mem_var, MT)
            act.activation(small[:, 16:18], small[:, 8:12].rearrange("p (t s) -> p t s", s=2)[:, :, 1], ACT.Sqrt, bias=eps).then_inc(mem_root, 1)
            for kt in range(KT):
                act.wait_ge(memT_mm, kt + 1)
                act.activation(memT[:, kt, :], ps[:, 6 + kt % 2, 0:MEM], ACT.Identity, bias=col(V_LMB + kt), scale=col(V_LMG + kt)).then_inc(memT_ready, 1)
            for i in range(KT + 2 * MT):
                act.wait_ge(kv_mm, i + 1)
                if i < KT:
                    act.activation(kT[:, i, :], ps[:, 6 + i % 2, 0:MEM], ACT.Copy).then_inc(kv_ready, 1)
                else:
                    n, t = (i - KT) // MT, (i - KT) % MT
                    act.activation(vm[:, t, n * HALF:(n + 1) * HALF], ps[:, 6 + i % 2, :], ACT.Copy).then_inc(kv_ready, 1)
            for i in range(KT):
                act.wait_ge(q_mm, i + 1)
                act.activation(u[:, i, :], ps[:, 2 + i % 4, :], ACT.Identity, bias=col(V_BIN + Z_Q // P + i)).then_inc(q_ready, 1)
            N = C_HEADS * TT
            for i in range(N + 3):
                if i < N:
                    act.wait_ge(cnm_ready, i + 1)
                    if i >= 2:
                        act.wait_ge(ct_done, i - 1)
                    act.activation(prob[:, i % 2, :], ps[:, i % 3, 0:MEM], ACT.Exp, bias=small[:, 64 + i:65 + i], scale=CSCALE, accum_out=small[:, 32 + i:33 + i]).then_inc(cexp_done, 1)
                j = i - 1
                if 0 <= j < N:
                    act.wait_ge(ct_done, j + 1)
                    if j >= TT and j % TT == 0:
                        act.wait_ge(cpv_done, j // TT)
                    act.activation(PT[:, :, (j % TT) * P:(j % TT + 1) * P], ps[:, 3 + j % 2, 0:MEM].rearrange("p (c n) -> p c n", c=MT), ACT.Copy).then_inc(cpt_ev, 1)
                if i >= 6 and i % TT == 2:
                    h = (i - 6) // TT
                    act.wait_ge(cpv_done, h + 1)
                    act.activation(u[:, 2 * h, :], ps[:, 5, :], ACT.Copy)
                    act.activation(u[:, 2 * h + 1, :], ps[:, 6, :], ACT.Copy).then_inc(oc_ready, 1)
            merge(2)
            act.wait_ge(m_mm, 3 * KT)
            for kt in range(KT):
                act.activation(xT[:, kt, :], xT[:, kt, :], ACT.Copy, scale=ALPHA).then_inc(ax_ready, 1)
            layer_norm(1, xT, V_L1G, V_L1B)
            act.wait_ge(l_ready, 2 * KT)
            act.wait_ge(wo_mm, KT)
            for kt in range(KT):
                act.activation(y[:, kt, :], xT[:, kt, :], ACT.Copy, scale=ALPHA).then_inc(f_init, 1)
            act.wait_ge(g_sub, 1)
            act.activation(gw[0][:, :, 0:4], gw[0][:, :, 0:4], ACT.Exp).then_inc(g_exp, 1)
            act.wait_ge(e_sub, 1)
            act.activation(gw[3][:, :, 0:4], gw[3][:, :, 0:4], ACT.Exp).then_inc(e_exp, 1)
            with act.Fori(0, EXP_GROUPS) as g:
                for j in range(PER_GROUP):
                    for i in range(2):
                        act.wait_ge(up_mm, 16 * g + 4 * j + 2 * i + 1)
                        act.wait_ge(hid2_ready, 8 * g + 2 * j + i + 1)
                        act.activation(tmp[:, i, :], ps[:, 2 * i, :], ACT.Silu).then_inc(sg2_ready, 1)
            layer_norm(2, y, V_L2G, V_L2B)
            for i in range(2 * TT):
                t, n = i // 2, i % 2
                act.wait_ge(o_mm, i + 1)
                act.activation(v3[:, t, n * HALF:(n + 1) * HALF], ps[:, 2 + i % 4, :], ACT.Copy).then_inc(o_kept, 1)

        @block.vector
        def _(dve):
            step = Steps(dve, d2_step)

            def col(n):
                return vec[:, n:n + 1]

            dve.wait_ge(rows_turned, 1)
            dve.tensor_copy(vec[:, 0:NV1], ps[:, 6, 0:NV1]).then_inc(vec2_ready, 1)
            dve.wait_ge(rows_turned, 2)
            dve.tensor_copy(vec[:, NV1:NV2], ps[:, 7, 0:NV2 - NV1]).then_inc(vec2_ready, 1)
            dve.wait_ge(vec2_ready, 2)
            lam = vec[:, V_LAM:V_LAM + B_HEADS]
            step(dve.tensor_scalar(lru[:, 4, :], lam, -1.0, None, ALU.mult))
            step.settle()
            dve.tensor_tensor(lru[:, 0, :], lam, lru[:, 4, :], ALU.max).then_inc(lru_ready, 1)

            def layer_norm(k, x):
                dve.wait_ge(l_sum, k + 1)
                for kt in range(KT):
                    dve.scalar_tensor_tensor(x[:, kt, :], ps[:, 0, :], -1.0 / D, x[:, kt, :], ALU.mult, ALU.add).then_inc(l_dev, 1)
                dve.wait_ge(l_root, k + 1)
                step(dve.reciprocal(tmp[:, 4, :], tmp[:, 4, :]))
                step.settle()
                for kt in range(KT):
                    dve.tensor_tensor(x[:, kt, :], x[:, kt, :], tmp[:, 4, :], ALU.mult).then_inc(l_norm, 1)

            layer_norm(0, xT)
            e, s, s2, acc = lru[:, 1, :], lru[:, 2, :], lru[:, 3, :], lru[:, 5, :]
            dve.wait_ge(lru_exp, 1)
            step(dve.tensor_scalar(s, e, 2.0, None, ALU.add))
            step.settle()
            step(dve.reciprocal(s, s))
            step.settle()
            step(dve.tensor_tensor(s, s, e, ALU.mult))
            step.settle()
            step(dve.tensor_tensor(s2, s, s, ALU.mult))
            step(dve.memset(acc, 2.0 / 19))
            for n in range(17, 0, -2):
                step.settle()
                step(dve.tensor_tensor(acc, acc, s2, ALU.mult))
                step.settle()
                step(dve.tensor_scalar(acc, acc, 2.0 / n, None, ALU.add))
            step.settle()
            step(dve.tensor_tensor(acc, acc, s, ALU.mult))
            step.settle()
            step(dve.scalar_tensor_tensor(acc, lru[:, 4, :], 0.0, acc, ALU.max, ALU.add))
            step.settle()
            step(dve.tensor_scalar(s, acc, -LRU_C, None, ALU.mult))
            dve.tensor_scalar(s2, acc, LRU_C, None, ALU.mult).then_inc(lru_ready, 1)

            for h in range(B_HEADS + 1):
                if h < B_HEADS:
                    dve.wait_ge(bz_ev, 2 * h + 1)
                    if h >= 2:
                        dve.wait_ge(bg_mm, h - 1)
                    x, src = xc[h % 2], xpad[h % 2]
                    for t in range(TAPS_B):
                        w = col(V_CW + t * B_HEADS + h)
                        if t == 0:
                            step(dve.tensor_scalar(x, src[:, 0:S], w, col(V_CB + h), ALU.mult, ALU.add))
                        else:
                            step.settle()
                            op = dve.scalar_tensor_tensor(x, src[:, t:t + S], w, x, ALU.mult, ALU.add)
                            if t < TAPS_B - 1:
                                step(op)
                            else:
                                op.then_inc(xc_ready, 1)
                if h >= 1:
                    k = h - 1
                    dve.wait_ge(at_ready, k + 1)
                    step(dve.tensor_tensor(rr, aa, aa, ALU.mult))
                    step(dve.tensor_tensor(ii, ii, xc[k % 2], ALU.mult))
                    step.settle()
                    dve.scalar_tensor_tensor(rr, rr, 1.0, th, ALU.add, ALU.mult).then_inc(m2_ready, 1)
                    dve.wait_ge(mult_ready, k + 1)
                    step(dve.scalar_tensor_tensor(ii, th, LIFT ** -0.5, ii, ALU.mult, ALU.mult))
                    step.settle()
                    step(dve.tensor_tensor_scan(rr, aa, ii, 0.0, ALU.mult, ALU.add))
                    step.settle()
                    dve.tensor_tensor(ob[:, k, :], rr, gt[k % 2], ALU.mult).then_inc(ob_ready, 1)

            dve.wait_ge(bc_in, 64)
            for i in range(2 * TT):
                n, t = i // TT, i % TT
                dve.wait_ge(v_mm, i + 1)
                dve.tensor_tensor(v3[:, t, n * HALF:(n + 1) * HALF], ps[:, 2 + i % 4, :], bv_row[:, n * HALF:(n + 1) * HALF], ALU.add).then_inc(v_biased, 1)

            def row_stats(x, t, done):
                for n in range(2):
                    step(dve.bn_stats(small[:, 100 + 6 * n:106 + 6 * n], x[:, t, n * HALF:(n + 1) * HALF]))
                step.settle()
                dve.bn_aggr(small[:, 8 + 2 * t:10 + 2 * t], small[:, 100:112]).then_inc(done, 1)
                dve.wait_ge(done, t + 1)

            for t in range(TT):
                dve.wait_ge(v_gelu, TT + t + 1)
                row_stats(v3, t, v_var)
            dve.wait_ge(v_root, 1)
            step(dve.reciprocal(small[:, 16:20], small[:, 16:20]))
            step.settle()
            for t in range(TT):
                step(dve.tensor_scalar(v3[:, t], v3[:, t], small[:, 8 + 2 * t:9 + 2 * t], small[:, 16 + t:17 + t], ALU.subtract, ALU.mult))
                step.settle()
                step(dve.tensor_tensor(v3[:, t], v3[:, t], lvg_row, ALU.mult))
                step.settle()
                dve.tensor_tensor(v3[:, t], v3[:, t], lvb_row, ALU.add).then_inc(v_ready, 1)
            for g in range(GROUPS_A):
                dve.wait_ge(sp_mm, g + 1)
                s = tmp[:, 4 + g % 2, :]
                step(dve.tensor_tensor(s.rearrange("p (c t) -> p c t", c=TT), ps[:, 2 + g % 4, :].rearrange("p (c t) -> p c t", c=TT),
                                       bs_row[:, g * P:(g + 1) * P].unsqueeze(1).to_broadcast([P, TT, P]), ALU.add))
                step.settle()
                dve.tensor_tensor(u[:, g, :], u[:, g, :], s, ALU.mult).then_inc(oa_ready, 1)

            def merge(branch):
                for dt in range(KT):
                    n = KT * branch + dt
                    dve.wait_ge(m_sg, n + 1)
                    sg, out = gate_sg[n % 2], ps[:, 3 + 2 * (n % 2), :]
                    if branch == 0:
                        dve.tensor_tensor(y[:, dt, :], sg, out, ALU.mult).then_inc(m_y, 1)
                    else:
                        step(dve.tensor_tensor(sg, sg, out, ALU.mult))
                        step.settle()
                        dve.tensor_tensor(y[:, dt, :], y[:, dt, :], sg, ALU.add).then_inc(m_y, 1)

            merge(0)
            dve.wait_ge(mem_in, 16)
            for t in range(MT):
                row_stats(mem_tok, t, mem_var)
            merge(1)
            dve.wait_ge(mem_root, 1)
            step(dve.reciprocal(small[:, 16:18], small[:, 16:18]))
            step.settle()
            for t in range(MT):
                dve.tensor_scalar(mem_tok[:, t], mem_tok[:, t], small[:, 8 + 2 * t:9 + 2 * t], small[:, 16 + t:17 + t], ALU.subtract, ALU.mult).then_inc(mem_norm, 1)
            N = C_HEADS * TT
            for i in range(N + 1):
                if i < N:
                    dve.wait_ge(cs_done, i + 1)
                    step(dve.reduce_max(small[:, 48 + i:49 + i], ps[:, i % 3, 0:MEM], AX_X))
                    step.settle()
                    dve.tensor_scalar(small[:, 64 + i:65 + i], small[:, 48 + i:49 + i], -CSCALE, None, ALU.mult).then_inc(cnm_ready, 1)
                j = i - 1
                if j >= 0:
                    dve.wait_ge(cexp_done, j + 1)
                    step(dve.reciprocal(small[:, 80 + j:81 + j], small[:, 32 + j:33 + j]))
                    step.settle()
                    if j >= 2:
                        dve.wait_ge(ct_done, j - 1)
                    dve.tensor_scalar(diag[:, j % 2, :], ident, small[:, 80 + j:81 + j], None, ALU.mult).then_inc(cdiag_ready, 1)
            merge(2)
            for dt in range(KT):
                dve.wait_ge(ax_ready, dt + 1)
                dve.wait_ge(wo_mm, dt + 1)
                dve.scalar_tensor_tensor(xT[:, dt, :], ps[:, 2 + dt % 4, :], col(V_BO + dt), xT[:, dt, :], ALU.add, ALU.add).then_inc(wo_used, 1)
            layer_norm(1, xT)
            dve.wait_ge(g_mm, 1)
            dve.wait_ge(prio_ready, 1)
            dve.wait_ge(wg_in, 64)

            def op(instruction):
                step(instruction)
                step.settle()

            def wide(x, n=4):
                return x.unsqueeze(2).to_broadcast([P, TT, n])

            def first_best(out, x, top, rest):
                op(dve.tensor_tensor(out, x, wide(top), ALU.is_equal))
                op(dve.tensor_tensor(out, out, prio.unsqueeze(1).to_broadcast([P, TT, 4]), ALU.mult))
                op(dve.reduce_max(rest, out, AX_X))
                op(dve.tensor_tensor(out, out, wide(rest), ALU.is_equal))

            top, rest, ptop = small[:, 8:12], small[:, 12:16], small[:, 16:20]
            op(dve.tensor_tensor(gl, ps[:, 7, 0:TT * 20].rearrange("p (t n) -> p t n", t=TT), bg_row.unsqueeze(1).to_broadcast([P, TT, 20]), ALU.add))
            op(dve.reduce_max(top, gl[:, :, 0:4], AX_X))
            dve.tensor_tensor(gw[0][:, :, 0:4], gl[:, :, 0:4], wide(top), ALU.subtract).then_inc(g_sub, 1)
            group = gw[1][:, :, 0:4]
            first_best(group, gl[:, :, 0:4], top, rest)
            dve.wait_ge(g_exp, 1)
            op(dve.reduce_sum(ptop, gw[0][:, :, 0:4], AX_X))
            op(dve.reciprocal(ptop, ptop))
            per = gw[2].rearrange("p t (g j) -> p t g j", g=4)
            op(dve.tensor_tensor(per, gl[:, :, 4:20].rearrange("p t (g j) -> p t g j", g=4), group.unsqueeze(3).to_broadcast([P, TT, 4, 4]), ALU.mult))
            inside = gw[3][:, :, 0:4]
            op(dve.reduce_sum(inside, per.rearrange("p t g j -> p t j g"), AX_X))
            op(dve.reduce_max(top, inside, AX_X))
            dve.tensor_tensor(inside, inside, wide(top), ALU.subtract).then_inc(e_sub, 1)
            dve.wait_ge(e_exp, 1)
            one, two = gw[4][:, :, 0:4], gw[5][:, :, 0:4]
            op(dve.reduce_max(top, inside, AX_X))
            first_best(one, inside, top, rest)
            op(dve.scalar_tensor_tensor(gw[4][:, :, 4:8], one, -2.0, inside, ALU.mult, ALU.add))
            op(dve.reduce_max(top, gw[4][:, :, 4:8], AX_X))
            first_best(two, gw[4][:, :, 4:8], top, rest)
            op(dve.tensor_tensor(one, one, two, ALU.add))
            op(dve.tensor_tensor(one, one, inside, ALU.mult))
            op(dve.reduce_sum(rest, one, AX_X))
            op(dve.reciprocal(rest, rest))
            op(dve.tensor_tensor(rest, rest, ptop, ALU.mult))
            op(dve.tensor_tensor(one, one, wide(rest), ALU.mult))
            dve.tensor_tensor(gw[0].rearrange("p t (g j) -> p t g j", g=4), group.unsqueeze(3).to_broadcast([P, TT, 4, 4]),
                              one.unsqueeze(2).to_broadcast([P, TT, 4, 4]), ALU.mult).then_inc(gate_ready, 1)
            dve.wait_ge(gate_turned, 1)
            dve.tensor_copy(gateT, ps[0:EXPERTS, 6, :]).then_inc(gateT_ready, 1)
            dve.wait_ge(f_init, KT)
            dve.memset(small[:, 20:21], 0.0).then_inc(hid2_ready, 1)
            dve.memset(small[:, 21:22], 0.0).then_inc(dn_used, 2)
            with dve.Fori(0, EXP_GROUPS) as g:
                for j in range(PER_GROUP):
                    last = dve.tensor_scalar(sel[:, j, :], ones[0:EXPERTS, :], const[0:EXPERTS, bass.ds(PER_GROUP * g + j, 1)], None, ALU.mult)
                last.then_inc(sel_ready, 1)
                for j in range(PER_GROUP):
                    for i in range(2):
                        n = 2 * j + i
                        dve.wait_ge(up_mm, 16 * g + 2 * n + 2)
                        dve.wait_ge(sg2_ready, 8 * g + n + 1)
                        dve.tensor_tensor(tmp[:, 2 + i, :], tmp[:, i, :], ps[:, 2 * i + 1, :], ALU.mult).then_inc(m_loop, 1)
                        dve.wait_ge(m_loop, 8 * g + n + 1)
                        dve.wait_ge(bc_mm, 4 * g + j + 1)
                        dve.tensor_tensor(u[:, n, :], tmp[:, 2 + i, :], ps[:, 4 + j % 2, :], ALU.mult).then_inc(hid2_ready, 1)
                for dt in range(KT):
                    dve.wait_ge(dn_mm, 8 * g + dt + 1)
                    dve.tensor_tensor(y[:, dt, :], y[:, dt, :], ps[:, 6 + dt % 2, :], ALU.add).then_inc(dn_used, 1)
            layer_norm(2, y)


def memory2(nc, ctx, M):
    M = dict(M)
    for name, shape in dict(
        ring2=[P, 6 * 4096], y=[P, KT, S], u=[P, KT, S], v=[P, TT * D], ob=[P, B_HEADS, S], tmp=[P, 8 * S + 2 * (S + TAPS_B - 1)],
        wT=[P, GROUPS_A, P], vec2=[P, NV2], lru=[P, 6, B_HEADS], small=[P, 128],
    ).items():
        M[name] = ctx.enter_context(nc.sbuf_tensor(name, shape, F32))
    return M


def program(nc, A):
    with ExitStack() as ctx:
        M = memory(nc, ctx)
        with ExitStack() as first:
            M1 = memory1(nc, first, M)
            prologue(nc, A, lambda name: ctx.enter_context(nc.semaphore(name)), M1)
            layer_sems = []

            def layer_sem(name):
                layer_sems.append(first.enter_context(nc.semaphore(name)))
                return layer_sems[-1]

            with nc.Fori(0, DEPTH) as l:
                layer(nc, A, layer_sem, M1, l)
                nc.gpsimd.sem_clear(range(layer_sems[0].num, layer_sems[-1].num + 1))
                nc.all_engine_barrier()
        with ExitStack() as last:
            second(nc, A, lambda name: ctx.enter_context(nc.semaphore(name)), memory2(nc, last, M))


def constants():
    import numpy as np

    c = np.zeros((P, C_ALL), np.float32)
    part = np.arange(P)
    c[:, C_IDENT:C_IDENT + P] = np.eye(P)
    half = ROPE // 2
    for m in range(P):
        first = m % ROPE < half
        c[m + half if first else m - half, C_ROT + m] = -1.0 if first else 1.0
    c[:, C_SLOT:C_SLOT + P] = part % CAP
    c[:, C_PSLOT] = part % CAP
    freq = np.float32(1.0) / np.float32(10000.0) ** (np.arange(0, ROPE, 2, dtype=np.float32) / np.float32(ROPE))
    c[:, C_FREQ] = freq[part % half]
    c[:, C_EPS6], c[:, C_EPS5] = EPS, 1e-5
    return c


def kernel(**inputs):
    import numpy as _np
    import concourse.bacc as _bacc
    from concourse import mybir as _mybir
    from concourse.bass_utils import run_bass_kernel_spmd as _run

    nc = _bacc.Bacc("TRN2", target_bir_lowering=False, num_devices=1)
    arrays, A = {}, {}
    for name, value in [*inputs.items(), ("const", constants())]:
        a = _np.ascontiguousarray(value)
        arrays[f"in_{name}"] = a
        A[name] = nc.dram_tensor(f"in_{name}", a.shape, _mybir.dt.from_np(a.dtype), kind="ExternalInput").ap()
    A["rope"] = nc.dram_tensor("rope_tables", (P, 2 * S), F32, kind="Internal").ap()
    A["out"] = nc.dram_tensor("out_0", (1, S, D), F32, kind="ExternalOutput").ap()
    program(nc, A)
    return _run(nc, [arrays], core_ids=[0]).results[0]["out_0"]
```

```python
import math
from contextlib import ExitStack

import concourse.bass as bass
from concourse import mybir

F32 = mybir.dt.float32
I32 = mybir.dt.int32
ALU = mybir.AluOpType
ACT = mybir.ActivationFunctionType
AX_X = mybir.AxisListType.X

P = 128
D = 1024
KT = D // P
S = 512
TT = S // P
DEPTH = 2
N_MOD = 6
HEADS, NOPE, ROPE, VD = 4, 128, 64, 128
QK = NOPE + ROPE
Q_RANK, KV_RANK = 256, 128
CONV_CH, TAPS = 512, 31
CT = CONV_CH // P
PAD = TAPS // 2
YW = S + 2 * PAD
IN_W = Q_RANK + KV_RANK + ROPE + 2 * CONV_CH
EXPERTS, CAP, FF = 16, 64, 1024
PAIRS = EXPERTS // 2
POOL_TAPS = {1: TAPS, 3: 6}
TAPS_A_TILE = 5
DVE_TAPS = (0, 11, 11, 9, 0, 10, 11, 10, 0)
HALF = 512
EPS = 1e-6
TABLES = 5 * TT * D + 2 * HEADS * QK + HEADS * (NOPE + VD)
QSCALE = 1.0 / math.sqrt(QK)
PI = 3.141592653589793
TWO_PI_A = 6.28125
TWO_PI_B = 0.0019350051879882812
TWO_PI_C = 2 * PI - TWO_PI_A - TWO_PI_B
ROUND = 1.5 * 2.0 ** 23

N1G, N2G, ADA, QLG, KVG, CB, CNG, CNB, QHG, KHG, QRG, KRG, NVEC = 0, 8, 16, 64, 66, 67, 71, 75, 79, 80, 81, 82, 83
SHIFT1, SCALE1, GATE1, SHIFT2, SCALE2, GATE2 = (m * KT for m in range(N_MOD))
C_IDENT, C_ROT, C_SLOT, C_PAIR, C_FREQ, C_PSLOT, C_EPS6, C_EPS5, C_ALL = 0, 128, 256, 384, 432, 433, 434, 435, 436
GROUP = 32
FR = mybir.dt.float32r


class Steps:

    def __init__(self, engine, semaphore):
        self.engine, self.semaphore, self.count = engine, semaphore, 0

    def __call__(self, instruction):
        self.count += 1
        instruction.then_inc(self.semaphore, 1)

    def settle(self):
        self.engine.wait_ge(self.semaphore, self.count)


def prologue(nc, A, sem, M):
    ps, const, xT = M["ps"], M["const"], M["xT"]
    ident = const[:, C_IDENT:C_IDENT + P]
    x_tok, scr = M["ring"][:, 0:TT * D].rearrange("p (t d) -> p t d", t=TT), M["scr"]
    c_rows, ones = M["one_hot_T"][:, 0:P], M["ones"]
    cos, sin = M["ring"][:, TABLES:TABLES + S], M["ring"][:, TABLES + S:TABLES + 2 * S]
    pos_i = M["ring"][:, TT * D:TT * D + S].bitcast(I32)
    const_in, x_in, pos_in, c_in = (sem(n) for n in ("const_in", "x_in", "pos_in", "c_in"))
    x_turned, c_turned, x_kept, c_raw, c_act, ones_set = (
        sem(n) for n in ("x_turned", "c_turned", "x_kept", "c_raw", "c_act", "ones_set"))
    angle_ready, p_step, p_act, tables_out = sem("angle_ready"), sem("p_step"), sem("p_act"), sem("tables_out")
    with nc.Block() as block:
        @block.sync
        def _(sp):
            sp.dma_start(const[:], A["const"]).then_inc(const_in, 16)
            sp.dma_start(x_tok, A["x"][0].rearrange("(t p) d -> p t d", p=P)).then_inc(x_in, 16)
            sp.dma_start(c_rows[0:KT, :], A["c"].rearrange("a (t p) -> (a t) p", p=P)).then_inc(c_in, 16)
            sp.dma_start(pos_i, A["positions"].to_broadcast([P, S])).then_inc(pos_in, 16)
            sp.wait_ge(p_act, 2)
            sp.dma_start(A["rope"], M["ring"][:, TABLES:TABLES + 2 * S]).then_inc(tables_out, 16)
            sp.wait_ge(tables_out, 16)

        @block.tensor
        def _(pe):
            pe.wait_ge(const_in, 16)
            pe.wait_ge(c_in, 16)
            pe.transpose(ps[:, 7, 0:KT], c_rows[0:KT, :], ident[0:KT, 0:KT]).then_inc(c_turned, 1)
            pe.wait_ge(x_in, 16)
            for kt in range(KT):
                if kt == 7:
                    pe.wait_ge(c_act, 1)
                for t in range(TT):
                    turn = pe.transpose(ps[:, kt, t * P:(t + 1) * P], x_tok[:, t, kt * P:(kt + 1) * P], ident)
                turn.then_inc(x_turned, 1)

        @block.scalar
        def _(act):
            act.wait_ge(c_turned, 1)
            act.activation(M["c_col"][:], ps[:, 7, 0:KT], ACT.Silu).then_inc(c_act, 1)
            act.wait_ge(angle_ready, 1)
            act.activation(sin, sin, ACT.Sin).then_inc(p_act, 1)
            act.wait_ge(angle_ready, 2)
            act.activation(cos, cos, ACT.Sin).then_inc(p_act, 1)

        @block.vector
        def _(dve):
            step = Steps(dve, p_step)
            dve.memset(ones[:], 1.0).then_inc(ones_set, 1)
            ang, turns = scr[:, 1, :], scr[:, 2, :]
            dve.wait_ge(pos_in, 16)
            dve.wait_ge(const_in, 16)
            step(dve.tensor_copy(ang, pos_i))
            step.settle()
            step(dve.tensor_scalar(ang, ang, const[:, C_FREQ:C_FREQ + 1], None, ALU.mult))
            step.settle()
            step(dve.tensor_scalar(turns, ang, 1.0 / (2 * PI), ROUND, ALU.mult, ALU.add))
            step.settle()
            step(dve.tensor_scalar(turns, turns, ROUND, None, ALU.subtract))
            for part in (TWO_PI_A, TWO_PI_B, TWO_PI_C):
                step.settle()
                step(dve.scalar_tensor_tensor(ang, turns, -part, ang, ALU.mult, ALU.add))
            step.settle()
            dve.tensor_scalar(sin, ang, -3.1415925, 3.1415925, ALU.max, ALU.min).then_inc(angle_ready, 1)
            step(dve.tensor_scalar(turns, ang, -1.0, None, ALU.mult))
            step.settle()
            step(dve.tensor_tensor(turns, turns, ang, ALU.max))
            step.settle()
            dve.tensor_scalar(cos, turns, -1.0, PI / 2, ALU.mult, ALU.add).then_inc(angle_ready, 1)
            for kt in range(KT):
                dve.wait_ge(x_turned, kt + 1)
                dve.tensor_copy(xT[:, kt, :], ps[:, kt, :]).then_inc(x_kept, 1)

        @block.gpsimd
        def _(pool):
            pass


def layer(nc, A, sem, M, l):
    ps, const, xT, ring, scr = M["ps"], M["const"], M["xT"], M["ring"], M["scr"]
    ident, rot = const[:, C_IDENT:C_IDENT + P], const[:, C_ROT:C_ROT + P]
    eps = const[:, C_EPS6:C_EPS6 + 1]
    slot_row, slot_col = const[:, C_SLOT:C_SLOT + P], const[:, C_PSLOT:C_PSLOT + 1]
    ones = M["ones"]
    pair = const[:, C_PAIR:C_PAIR + 3 * GROUP // 2]
    cos, sin = ring[:, TABLES:TABLES + S], ring[:, TABLES + S:TABLES + 2 * S]
    hy, h_tok, one_hot_T = M["hy"], M["h_tok"], M["one_hot_T"]
    hT = hy[:, 0:KT * S].rearrange("p (k n) -> p k n", k=KT)
    mix = hT
    ye = hy[:, 0:PAIRS * D].rearrange("p (e n) -> p e n", e=PAIRS)
    ye_lo = M["hy_r"][:, 0:PAIRS * D].rearrange("p (e n) -> p e n", e=PAIRS)
    ye_hi = M["ring_r"][:, 0:PAIRS * D].rearrange("p (e n) -> p e n", e=PAIRS)
    rin = hy[:, KT * S:2 * KT * S].rearrange("p (k n) -> p k n", k=2 * HEADS)
    vec, convw, mod, smod = (M[n] for n in ("vec", "convw", "mod", "smod"))
    CHUNK = TT * D
    ada = [ring[:, i * CHUNK:(i + 1) * CHUNK].rearrange("p (k n) -> p k n", k=KT) for i in (3, 4, 5)]
    ada_row = [one_hot_T[:, CHUNK + i * P:CHUNK + (i + 1) * P] for i in range(4)]
    c_rep = one_hot_T[:, CHUNK + 4 * P:CHUNK + 4 * P + KT * GROUP].rearrange("p (k n) -> p k n", k=KT)
    w_in, w_in_low = (M[n][:, 0:KT * IN_W].rearrange("p (k n) -> p k n", k=KT) for n in ("ring", "ring_r"))
    w_in_high = [M["one_hot_T_r"][:, i * KT * P:(i + 1) * KT * P].rearrange("p (k n) -> p k n", k=KT) for i in range(3)]
    h_low = M["hy_r"][:, 0:KT * S].rearrange("p (k n) -> p k n", k=KT)
    h_high = M["hy_r"][:, KT * S:2 * KT * S].rearrange("p (k n) -> p k n", k=KT)
    products = [one_hot_T[:, 3 * KT * P + i * S:3 * KT * P + (i + 1) * S] for i in range(2)] + [scr[:, 3, :]]
    first = Q_RANK + KV_RANK + ROPE
    in_cols = [c0 + c * P for c in range(CT) for c0 in (first + CONV_CH, first)] + [0, P, Q_RANK, Q_RANK + KV_RANK]
    IN_TILES = len(in_cols)
    POOL_ADDS = sum(taps - 1 for taps in POOL_TAPS.values())
    w_out = ring[:, 3 * CHUNK:5 * CHUNK].rearrange("p (k n) -> p k n", k=KT)
    w_out_low = M["ring2_r"][:, 0:2 * CHUNK].rearrange("p (k n) -> p k n", k=KT)
    w_out_high = [M[n][:, a:a + CHUNK].rearrange("p (k n) -> p k n", k=4)[:, k, :] for n, a in (("ring2_r", 2 * CHUNK), ("one_hot_T_r", 0)) for k in range(4)]
    mix_low, mix_high = h_low, h_high
    MIX_ORDER = (0, 1, 2, 4, 5, 6, 7, 3)
    w_uq = ring[:, 5 * CHUNK:5 * CHUNK + 2 * HEADS * QK].rearrange("p (k n) -> p k n", k=2)
    w_ukv = ring[:, 5 * CHUNK + 2 * HEADS * QK:5 * CHUNK + 2 * HEADS * QK + HEADS * (NOPE + VD)]
    chunk = [ring[:, i * CHUNK:(i + 1) * CHUNK].rearrange("p (k n) -> p k n", k=4) for i in range(6)]
    def cut(region, at, n):
        return region[:, at * HALF:(at + n) * HALF].rearrange("p (k n) -> p k n", k=n)
    qn, qr, kn, kr = cut(ring, 0, 4), cut(ring, 4, 2), cut(ring, 6, 4), cut(ring, 10, 2)
    V, PT, prob = cut(ring, 12, 4), cut(ring, 16, 4), cut(ring, 20, 3)
    ypad = h_tok[:, 0:CT * YW].rearrange("p (c n) -> p c n", c=CT)
    w_r = h_tok[:, CT * YW:CT * YW + KT * EXPERTS].rearrange("p (k n) -> p k n", k=KT)
    cq = h_tok[:, 2560:2560 + 1024].rearrange("p (k n) -> p k n", k=2)
    ckv = h_tok[:, 3584:4096]
    sqs, acc, sig, krg = cut(one_hot_T, 0, 11), cut(one_hot_T, 11, 4), one_hot_T[:, 15 * HALF:16 * HALF], M["krg"]
    h_tok3 = h_tok[:].rearrange("p (t d) -> p t d", t=TT)
    ohT = M["one_hot_T_r"][:, 0:PAIRS * S].rearrange("p (e n) -> p e n", e=PAIRS)
    stat = M["stat"]
    mx, nmx, rsum, rrs, rqs, rqk = (stat[:, a:b] for a, b in ((0, 16), (16, 32), (32, 48), (48, 64), (64, 80), (80, 112)))
    root, head_rms, kd = M["krg"][:, 0:P], rin[:, 2, :], rin[:, 3, :]
    root2 = rin[:, 0, 0:2 * P]
    rowsA, rowsB = one_hot_T[:, 12 * S:12 * S + P], one_hot_T[:, 13 * S:13 * S + P]
    diag = ring[:, 23 * HALF:23 * HALF + 3 * P].rearrange("p (i n) -> p i n", i=3)
    lg, aff, top8, rankT = (M[n] for n in ("lg", "aff", "top8", "rankT"))
    work, affT, rank, lgT = (one_hot_T[0:EXPERTS, i * S:(i + 1) * S] for i in range(4))
    rankm = M["krg"][0:EXPERTS, :]
    sel_e, gcol = M["sel_e"], M["gcol"]
    x_e, sg, hid = scr[:, 0, :], scr[:, 1, :], scr[:, 2, :]
    hidT = x_e
    s_e = scr[:, 3, :].rearrange("p (t n) -> p t n", t=TT)

    rows_in, rowsT_done, vec_ready = sem("rows_in"), sem("rowsT_done"), sem("vec_ready")
    ada_in = [sem(f"ada_in{i}") for i in range(3)]
    c_spread, ada_used, ada_rows, ada_cols, mod_ready = (sem(n) for n in ("c_spread", "ada_used", "ada_rows", "ada_cols", "mod_ready"))
    w_in_in = [sem(f"w_in_in{i}") for i in range(CT + 1)]
    uq_in, w_out_in, w_r_in = sem("uq_in"), sem("w_out_in"), sem("w_r_in")
    w_in_split, w_in_ready, h_split, h_low_ready, prod_ready, prod_used, w_out_split, w_out_ready, mix_split, mix_ready = (
        sem(n) for n in ("w_in_split", "w_in_ready", "h_split", "h_low_ready", "prod_ready", "prod_used", "w_out_split", "w_out_ready", "mix_split", "mix_ready"))
    n_sq, n_ss, n_root, n_inv, n_bc, n_xn, h_ready = (sem(n) for n in ("n_sq", "n_ss", "n_root", "n_inv", "n_bc", "n_xn", "h_ready"))
    pad_zero, proj, act_proj, dve_proj, sig_ready, y_ready = (sem(n) for n in ("pad_zero", "proj", "act_proj", "dve_proj", "sig_ready", "y_ready"))
    lat_sq, lat_ss, lat_root, lat_inv, lat_bc, lat_ready = (sem(n) for n in ("lat_sq", "lat_ss", "lat_root", "lat_inv", "lat_bc", "lat_ready"))
    qk_mm, qk_ev, rot_mm, roped, head_ss, head_root, head_cols, kd_ready, kb_mm, qk_ready = (
        sem(n) for n in ("qk_mm", "qk_ev", "rot_mm", "roped", "head_ss", "head_root", "head_cols", "kd_ready", "kb_mm", "qk_ready"))
    s_done, nm_ready, exp_done, diag_ready, t_done, pt_ev, pv_done, pv_ev = (
        sem(n) for n in ("s_done", "nm_ready", "exp_done", "diag_ready", "t_done", "pt_ev", "pv_done", "pv_ev"))
    conv_dve, cmean, cdev, csq, cvar, croot, cinv, cbc, cnorm, cmix = (
        sem(n) for n in ("conv_dve", "cmean", "cdev", "csq", "cvar", "croot", "cinv", "cbc", "cnorm", "cmix"))
    wout_done, x1_ready = sem("wout_done"), sem("x1_ready")
    r_mm, rT_kept, r_done, r_sub, r_exp, aff_ready, affT_done, htok_mm, htok_ev, rank_ready, rankT_done = (
        sem(n) for n in ("r_mm", "rT_kept", "r_done", "r_sub", "r_exp", "aff_ready", "affT_done", "htok_mm", "htok_ev", "rank_ready", "rankT_done"))
    chunk_in = [sem(f"chunk_in{i}") for i in range(6)]
    chunk_used, s_built, xe_mm, xe_ready, st_mm, st_free, sg_ready, hid_ready, hidT_mm, hidT_ready, ye_free = (
        sem(n) for n in ("chunk_used", "s_built", "xe_mm", "xe_ready", "st_mm", "st_free", "sg_ready", "hid_ready", "hidT_mm", "hidT_ready", "ye_free"))
    ye_hi_ready, ye_lo_ready, out_done, x2_ready = (sem(n) for n in ("ye_hi_ready", "ye_lo_ready", "out_done", "x2_ready"))
    d_step = sem("d_step")

    def at(name):
        return A[name][bass.ds(l, 1)]

    with nc.Block() as block:
        @block.sync
        def _(sp):
            w_ada = at("w_ada").rearrange("a (k p) n -> p (a k) n", p=P)
            w = at("w_in").rearrange("a (k p) n -> p (a k) n", p=P)

            def ada_chunk(c):
                if c >= 3:
                    sp.wait_ge(ada_used, c - 2)
                sp.dma_start(ada[c % 3], w_ada[:, :, HALF * c:HALF * (c + 1)]).then_inc(ada_in[c % 3], 16)

            ada_chunk(0)
            row = 0
            for name, n in (("norm1_g", KT), ("norm2_g", KT), ("b_ada", N_MOD * KT), ("q_latent_g", 2), ("kv_latent_g", 1),
                            ("conv_b", CT), ("conv_norm_g", CT), ("conv_norm_b", CT)):
                sp.dma_start(rowsA[row:row + n, :], at(name).rearrange("a (k p) -> (a k) p", p=P)).then_inc(rows_in, 16)
                row += n
            ada_chunk(1)
            ada_chunk(2)
            for piece in range(CT + 1):
                if piece == 1:
                    ada_chunk(3)
                for c0 in in_cols[2 * piece:2 * piece + 2] if piece < CT else [0]:
                    width = P if piece < CT else first
                    sp.dma_start(w_in[:, :, c0:c0 + width], w[:, :, c0:c0 + width]).then_inc(w_in_in[piece], 16)
            for c in range(4, 12):
                ada_chunk(c)
            sp.wait_ge(ada_used, 12)
            sp.dma_start(w_uq, at("w_uq").rearrange("a (k p) n -> p (a k) n", p=P)).then_inc(uq_in, 16)
            sp.dma_start(w_ukv, at("w_ukv").rearrange("a p n -> p (a n)")).then_inc(uq_in, 16)
            sp.dma_start(ring[:, TABLES:TABLES + 2 * S], A["rope"]).then_inc(uq_in, 16)
            sp.dma_start(w_r, at("w_router").rearrange("a (k p) n -> p (a k) n", p=P)).then_inc(w_r_in, 16)
            w = at("w_out").rearrange("a (k p) n -> p (a k) n", p=P)
            for k in range(0, KT, 4):
                sp.dma_start(w_out[:, k:k + 4], w[:, k:k + 4]).then_inc(w_out_in, 16)

            def expert(e):
                for j in range(6):
                    if e is None and j in (0, 3):
                        sp.wait_ge(*((pv_done, HEADS) if j == 0 else (wout_done, KT)))
                    name, k = ("w_gate", "w_up", "w_down")[j // 2], 4 * (j % 2)
                    if e is not None:
                        sp.wait_ge(chunk_used, 6 * e + (j - 5))
                    w = A[name][bass.ds(l, 1), bass.ds(0 if e is None else e, 1)].rearrange("a e (k p) n -> p (a e k) n", p=P)
                    sp.dma_start(chunk[j], w[:, k:k + 4]).then_inc(chunk_in[j], 16)

            expert(None)
            with sp.Fori(1, EXPERTS) as e:
                expert(e)

        @block.gpsimd
        def _(pool):
            pool.memset(ypad[:, :, 0:PAD], 0.0)
            pool.memset(ypad[:, :, PAD + S:YW], 0.0).then_inc(pad_zero, 1)
            n = 0
            for c, taps in POOL_TAPS.items():
                for t in range(1, taps):
                    pool.wait_ge(prod_ready, n + 1)
                    if n >= 1:
                        pool.wait_ge(prod_used, n)
                    pool.tensor_tensor(acc[:, c, :], acc[:, c, :], products[n % 3], ALU.add).then_inc(prod_used, 1)
                    n += 1
            for kt in range(KT):
                pool.wait_ge(w_out_split, kt + 1)
                pool.tensor_tensor(w_out_low[:, kt, :], w_out[:, kt, :], w_out_high[kt].bitcast(F32), ALU.subtract).then_inc(w_out_ready, 1)

        @block.tensor
        def _(pe):
            def grouped_sum(bank, col, x, start, stop):
                for g in range(TT):
                    mm = pe.matmul(ps[GROUP * g:GROUP * (g + 1), bank, col:col + P], ones[:, 0:GROUP], x[:, g * P:(g + 1) * P], start=start, stop=stop)
                return mm

            def broadcast(bank, x):
                for g in range(TT):
                    first = ident[:, GROUP * g:GROUP * g + 1].to_broadcast([P, P])
                    mm = pe.matmul(ps[:, bank, g * P:(g + 1) * P], first, x, start=True, stop=True)
                return mm

            def norm(k):
                for kt in range(KT):
                    pe.wait_ge(n_sq, KT * k + kt + 1)
                    grouped_sum(6 - 6 * k, 0, scr[:, kt % 4, :], kt == 0, kt == KT - 1).then_inc(n_ss, 1)
                pe.wait_ge(n_inv, k + 1)
                if k == 0:
                    pe.wait_ge(vec_ready, 2)
                broadcast(7 - 6 * k, root).then_inc(n_bc, 1)

            pe.wait_ge(rows_in, 16 * 13)
            pe.transpose(ps[:, 5, 0:NVEC], rowsA[0:NVEC, :], ident[0:NVEC, 0:NVEC]).then_inc(rowsT_done, 1)
            pe.transpose(ps[:, 7, 0:TAPS * CT], rowsB[0:TAPS * CT, :], ident[0:TAPS * CT, 0:TAPS * CT]).then_inc(rowsT_done, 1)
            norm(0)

            def ada_chunk(c, bank):
                pe.wait_ge(ada_in[c % 3], 16 * (c // 3 + 1))
                for kt in range(KT):
                    for g in range(4):
                        mm = pe.matmul(ps[GROUP * g:GROUP * (g + 1), bank, 0:P], c_rep[:, kt, :], ada[c % 3][:, kt, g * P:(g + 1) * P],
                                       start=(kt == 0), stop=(kt == KT - 1))
                mm.then_inc(ada_used, 1)

            def ada_turn(c, bank):
                pe.wait_ge(ada_rows, c + 1)
                pe.transpose(ps[:, bank, (c % 4) * P:(c % 4 + 1) * P], ada_row[c % 4], ident).then_inc(ada_cols, 1)

            pe.wait_ge(c_spread, 1)
            for c in range(4):
                ada_chunk(c, c)
            for c in range(4):
                ada_turn(c, 4)
            pe.wait_ge(vec_ready, 2)
            for i, c0 in enumerate(in_cols):
                if i in (6, 8, 10):
                    pe.wait_ge(act_proj, (i - 6) // 2 + 1)
                if i in (7, 9, 11):
                    pe.wait_ge(dve_proj, (i - 7) // 2 + 1)
                pe.wait_ge(w_in_ready, i + 1)
                w_high = w_in_high[i % 3]
                w_low = w_in_low[:, :, c0:c0 + P] if i < IN_TILES - 1 else w_in_low[:, :, 0:P]
                for kt in range(KT):
                    if i == 0:
                        pe.wait_ge(h_low_ready, kt + 1)
                    pe.matmul(ps[:, i % 6, :], w_high[:, kt, :], h_high[:, kt, :], start=(kt == 0), stop=False)
                    pe.matmul(ps[:, i % 6, :], w_high[:, kt, :], h_low[:, kt, :], start=False, stop=False)
                    mm = pe.matmul(ps[:, i % 6, :], w_low[:, kt, :], h_high[:, kt, :], start=False, stop=(kt == KT - 1))
                mm.then_inc(proj, 1)
                c = 4 + i
                if 5 <= c <= 12:
                    if c == 5:
                        pe.wait_ge(n_xn, KT)
                    if c == 9:
                        pe.wait_ge(mod_ready, 2)
                    ada_turn(c - 1, 7)
                if c < 12:
                    ada_chunk(c, 6)
            pe.wait_ge(ada_rows, 12)
            for i in range(3):
                pe.wait_ge(lat_sq, i + 1)
                grouped_sum(6, P * (i // 2), scr[:, i, :], i != 1, i != 0).then_inc(lat_ss, 1)
            pe.wait_ge(mod_ready, 3)
            pe.wait_ge(lat_inv, 1)
            broadcast(7, root2[:, 0:P]).then_inc(lat_bc, 1)
            broadcast(6, root2[:, P:2 * P]).then_inc(lat_bc, 1)
            pe.wait_ge(uq_in, 48)
            pe.wait_ge(lat_ready, 3)
            for i in range(14):
                if i == 5:
                    pe.wait_ge(act_proj, 8)
                if i >= 6:
                    pe.wait_ge(qk_ev, i - 5)
                out = ps[:, i % 6, :]
                if i < 6:
                    for k in range(2):
                        go = dict(start=(k == 0), stop=(k == 1))
                        if i % 3 < 2:
                            h = 2 * (i // 3) + i % 3
                            mm = pe.matmul(out, w_uq[:, k, h * QK:h * QK + NOPE], cq[:, k, :], **go)
                        else:
                            for half in range(2):
                                h = 2 * (i // 3) + half
                                mm = pe.matmul(ps[ROPE * half:ROPE * (half + 1), i % 6, :], w_uq[:, k, h * QK + NOPE:(h + 1) * QK], cq[:, k, :], **go)
                elif i < 10:
                    h = i - 6
                    mm = pe.matmul(out, w_ukv[:, h * 2 * P:h * 2 * P + P], ckv, start=True, stop=True)
                else:
                    t = i - 10
                    mm = pe.matmul(out, ckv[:, t * P:(t + 1) * P], w_ukv.rearrange("p (h c) -> p h c", h=HEADS)[:, :, NOPE:NOPE + VD],
                                   start=True, stop=True)
                mm.then_inc(qk_mm, 1)
            for i in range(3):
                pe.wait_ge(qk_ev, 9 + i)
                pe.matmul(ps[:, 2 + i, :], rot, krg[:] if i == 0 else qr[:, i - 1, :], start=True, stop=True).then_inc(rot_mm, 1)
            query, key = pair[:, GROUP // 2:], pair[:, 0:GROUP]
            for n in range(4):
                for h in range(HEADS):
                    out, half = ps[GROUP * h:GROUP * (h + 1), 6, :], slice(ROPE * (h % 2), ROPE * (h % 2 + 1))
                    if n == 0:
                        pe.matmul(out, query, sqs[:, h, :], start=True, stop=False)
                    elif n == 1:
                        pe.matmul(out, key, sqs[:, 6 + h, :], start=False, stop=False)
                    elif n == 2:
                        pe.matmul(out, query[half, :], sqs[half, 4 + h // 2, :], start=False, stop=False)
                    else:
                        mm = pe.matmul(out, key[half, :], sqs[half, 10, :], start=False, stop=True)
            mm.then_inc(head_ss, 1)
            pe.wait_ge(head_root, 1)
            for t in range(TT):
                mm = pe.transpose(ps[:, 7, t * P:(t + 1) * P], head_rms[:, t * P:(t + 1) * P], ident)
            mm.then_inc(head_cols, 1)

            def key_factor(h):
                pe.wait_ge(kd_ready, h + 1)
                if h >= 1:
                    pe.wait_ge(qk_ready, h)
                pe.matmul(ps[:, 6, :], ones[:], kd, start=True, stop=True).then_inc(kb_mm, 1)

            key_factor(0)
            pe.wait_ge(qk_ev, 14)
            pe.wait_ge(prod_used, POOL_ADDS)
            pe.wait_ge(conv_dve, CT - 1)
            for c in range(CT):
                mm = pe.matmul(ps[:, 5, :], ones[:], acc[:, c, :], start=(c == 0), stop=(c == CT - 1))
            mm.then_inc(cmean, 1)
            pe.wait_ge(roped, 3)
            for i in range(4 * HEADS + 3):
                if i < 4 * HEADS:
                    h, q0 = i // TT, (i % TT) * P
                    pe.wait_ge(qk_ready, h + 1)
                    if i >= 3:
                        pe.wait_ge(exp_done, i - 2)
                    half = slice(ROPE * (h % 2), ROPE * (h % 2 + 1))
                    pe.matmul(ps[:, i % 3, :], qn[:, h, q0:q0 + P], kn[:, h, :], start=True, stop=False)
                    pe.matmul(ps[:, i % 3, :], qr[half, h // 2, q0:q0 + P], kr[half, h // 2, :], start=False, stop=True).then_inc(s_done, 1)
                    if i % TT == 1 and h + 1 < HEADS:
                        key_factor(h + 1)
                j = i - 2
                if 0 <= j < 4 * HEADS:
                    pe.wait_ge(diag_ready, j + 1)
                    if j >= 2:
                        pe.wait_ge(pt_ev, j - 1)
                    for kc in range(TT):
                        mm = pe.matmul(ps[:, 3 + j % 2, kc * P:(kc + 1) * P], prob[:, j % 3, kc * P:(kc + 1) * P], diag[:, j % 3, :], start=True, stop=True)
                    mm.then_inc(t_done, 1)
                if i >= 6 and i % TT == 2:
                    h = (i - 6) // TT
                    pe.wait_ge(pt_ev, TT * (h + 1))
                    if h == 0:
                        pe.wait_ge(cdev, CT)
                    if h >= 1:
                        pe.wait_ge(pv_ev, h)
                    for kc in range(TT):
                        mm = pe.matmul(ps[:, 5, :], V[:, kc, h * VD:(h + 1) * VD], PT[:, kc, :], start=(kc == 0), stop=(kc == TT - 1))
                    mm.then_inc(pv_done, 1)
                if i == 5:
                    pe.wait_ge(csq, CT)
                    for c in range(CT):
                        mm = grouped_sum(7, 0, scr[:, c, :], c == 0, c == CT - 1)
                    mm.then_inc(cvar, 1)
                if i == 8:
                    pe.wait_ge(cinv, 1)
                    broadcast(7, scr[:, 0, 0:P]).then_inc(cbc, 1)
            for dt in range(KT):
                tile = slice(dt * P, (dt + 1) * P)
                for n, kt in enumerate(MIX_ORDER):
                    if dt == 0:
                        pe.wait_ge(w_out_ready, kt + 1)
                        pe.wait_ge(mix_ready, n + 1)
                    pe.matmul(ps[:, dt, :], w_out_high[kt][:, tile], mix_high[:, kt, :], start=(n == 0), stop=False)
                    pe.matmul(ps[:, dt, :], w_out_high[kt][:, tile], mix_low[:, kt, :], start=False, stop=False)
                    mm = pe.matmul(ps[:, dt, :], w_out_low[:, kt, tile], mix_high[:, kt, :], start=False, stop=(n == KT - 1))
                mm.then_inc(wout_done, 1)
            norm(1)
            pe.wait_ge(w_r_in, 16)
            for kt in range(KT):
                pe.wait_ge(h_ready, KT + kt + 1)
                mm = pe.matmul(ps[0:EXPERTS, 0, :], w_r[:, kt, :], hT[:, kt, :], start=(kt == 0), stop=(kt == KT - 1))
            mm.then_inc(r_mm, 1)
            pe.wait_ge(rT_kept, 1)
            pe.wait_ge(n_xn, 2 * KT)
            for t in range(TT):
                mm = pe.transpose(ps[:, 1, t * EXPERTS:(t + 1) * EXPERTS], lgT[:, t * P:(t + 1) * P], ident[0:EXPERTS, 0:EXPERTS])
            mm.then_inc(r_done, 1)
            for i in range(2 * TT):
                t, g = i // 2, i % 2
                if i >= 4:
                    pe.wait_ge(htok_ev, i - 3)
                for b in range(4):
                    kt = 4 * g + b
                    mm = pe.transpose(ps[:, 2 + i % 4, b * P:(b + 1) * P], hT[:, kt, t * P:(t + 1) * P], ident)
                mm.then_inc(htok_mm, 1)
            pe.wait_ge(aff_ready, 1)
            for t in range(TT):
                mm = pe.transpose(ps[0:EXPERTS, 6, t * P:(t + 1) * P], aff[:, t, :], ident)
            mm.then_inc(affT_done, 1)
            pe.wait_ge(rank_ready, 1)
            for t in range(TT):
                mm = pe.transpose(ps[:, 7, t * EXPERTS:(t + 1) * EXPERTS], rankm[:, t * P:(t + 1) * P], ident[0:EXPERTS, 0:EXPERTS])
            mm.then_inc(rankT_done, 1)
            pe.wait_ge(htok_ev, 2 * TT)
            with pe.Fori(0, EXPERTS) as e:
                pe.wait_ge(s_built, e + 1)
                for kt in range(KT):
                    for t in range(TT):
                        mm = pe.matmul(ps[:, 0, kt * CAP:(kt + 1) * CAP], h_tok3[:, t, kt * P:(kt + 1) * P], s_e[:, t, 0:CAP], start=(t == 0), stop=(t == TT - 1))
                mm.then_inc(xe_mm, 1)
                pe.wait_ge(st_free, e + 1)
                for t in range(TT):
                    pe.matmul(ps[:, 7, 0:1], s_e[:, t, :], aff[:, t, bass.ds(e, 1)], start=(t == 0), stop=(t == TT - 1))
                pe.matmul(ps[:, 6, :], sel_e[:], rankm, start=True, stop=True).then_inc(st_mm, 1)
                pe.wait_ge(xe_ready, e + 1)
                for j in range(4):
                    pe.wait_ge(chunk_in[j], 16 * e + 16)
                    for k in range(4):
                        kt = 4 * (j % 2) + k
                        for half in range(2):
                            mm = pe.matmul(ps[CAP * half:CAP * (half + 1), 1 + j // 2, :], x_e[:, kt * CAP:(kt + 1) * CAP],
                                           chunk[j][:, k, half * HALF:(half + 1) * HALF], start=(kt == 0), stop=(kt == KT - 1))
                    mm.then_inc(chunk_used, 1)
                pe.wait_ge(hid_ready, e + 1)
                for b in range(4):
                    mm = pe.transpose(ps[:, 3, b * P:(b + 1) * P], hid[:, b * P:(b + 1) * P], ident)
                mm.then_inc(hidT_mm, 1)
                pe.wait_ge(hidT_ready, e + 1)
                pe.wait_ge(ye_free, e + 1)
                for j in range(4, 6):
                    pe.wait_ge(chunk_in[j], 16 * e + 16)
                    for k in range(4):
                        at_f = k * P + CAP * (j - 4)
                        for half in range(2):
                            mm = pe.matmul(ps[CAP * half:CAP * (half + 1), 4, :], hidT[:, at_f:at_f + CAP],
                                           chunk[j][:, k, half * HALF:(half + 1) * HALF], start=(j == 4 and k == 0), stop=(j == 5 and k == 3))
                    mm.then_inc(chunk_used, 1)
            pe.wait_ge(ye_free, EXPERTS + 1)
            pe.wait_ge(st_free, EXPERTS + 1)
            for n in range(PAIRS):
                for dt in range(KT):
                    tile = slice(dt * P, (dt + 1) * P)
                    pe.wait_ge(ye_hi_ready, n + 1)
                    pe.matmul(ps[:, dt, :], ye_hi[:, n, tile], ohT[:, n, :], start=(n == 0), stop=False)
                for dt in range(KT):
                    tile = slice(dt * P, (dt + 1) * P)
                    pe.wait_ge(ye_lo_ready, n + 1)
                    mm = pe.matmul(ps[:, dt, :], ye_lo[:, n, tile], ohT[:, n, :], start=False, stop=(n == PAIRS - 1))
            mm.then_inc(out_done, 1)

        @block.scalar
        def _(act):
            act.dma_start(rowsA[QHG:QHG + 1, :], at("q_head_g")[:, 0:NOPE]).then_inc(rows_in, 16)
            act.dma_start(rowsA[KHG:KHG + 1, :], at("k_head_g")[:, 0:NOPE]).then_inc(rows_in, 16)
            for r, name in ((QRG, "q_head_g"), (KRG, "k_head_g")):
                act.dma_start(rowsA[r:r + 1, :].rearrange("p (a n) -> p a n", a=2),
                              at(name)[:, NOPE:QK].unsqueeze(1).to_broadcast([1, 2, ROPE])).then_inc(rows_in, 16)
            act.dma_start(rowsB[0:TAPS * CT, :], at("conv_w").rearrange("a t (c p) -> (a t c) p", p=P)).then_inc(rows_in, 16)

            def norm(k, shift):
                for kt in range(KT):
                    if KT * k + kt >= 4:
                        act.wait_ge(n_ss, KT * k + kt - 3)
                    if k == 1:
                        act.wait_ge(x1_ready, kt + 1)
                    act.activation(scr[:, kt % 4, :], xT[:, kt, :], ACT.Square).then_inc(n_sq, 1)
                act.wait_ge(n_ss, KT * (k + 1))
                act.activation(root, ps[:, 6 - 6 * k, 0:P], ACT.Sqrt, bias=eps, scale=1.0 / D).then_inc(n_root, 1)

            def modulate(k, shift):
                for kt in range(KT):
                    act.wait_ge(n_xn, KT * k + kt + 1)
                    act.activation(hT[:, kt, :], hT[:, kt, :], ACT.Identity, bias=mod[:, shift + kt:shift + kt + 1],
                                   scale=smod[:, KT * k + kt:KT * k + kt + 1]).then_inc(h_ready, 1)
                    if k == 0:
                        act.wait_ge(h_ready, kt + 1)
                        act.activation(h_high[:, kt, :], hT[:, kt, :], ACT.Copy).then_inc(h_split, 1)

            norm(0, SHIFT1)

            def ada_kept(c, bank):
                act.wait_ge(ada_used, c + 1)
                if c >= 4:
                    act.wait_ge(ada_cols, c - 3)
                act.activation(ada_row[c % 4], ps[:, bank, 0:P], ACT.Copy).then_inc(ada_rows, 1)

            def w_in_split_tile(i):
                if i % 2 == 0 and i <= 2 * CT:
                    act.wait_ge(w_in_in[i // 2], 32 if i < 2 * CT else 16)
                if i >= 3:
                    act.wait_ge(proj, i - 2)
                c0 = in_cols[i]
                if i < IN_TILES - 1:
                    act.activation(w_in_high[i % 3], w_in[:, :, c0:c0 + P], ACT.Copy).then_inc(w_in_split, 1)
                else:
                    act.activation(w_in_high[i % 3].rearrange("p k (a n) -> p k a n", a=2),
                                   w_in[:, :, c0:c0 + ROPE].unsqueeze(2).to_broadcast([P, KT, 2, ROPE]), ACT.Copy).then_inc(w_in_split, 1)

            def conv_products():
                n = 0
                for c, taps in POOL_TAPS.items():
                    for t in range(taps):
                        w, src = convw[:, t * CT + c:t * CT + c + 1], ypad[:, c, t:t + S]
                        if t == 0:
                            act.wait_ge(dve_proj, c + 1)
                            act.activation(acc[:, c, :], src, ACT.Identity, bias=vec[:, CB + c:CB + c + 1], scale=w)
                        else:
                            if n >= 3:
                                act.wait_ge(prod_used, n - 2)
                            act.activation(products[n % 3], src, ACT.Copy, scale=w).then_inc(prod_ready, 1)
                            n += 1
                        yield

            for c in range(3):
                ada_kept(c, c)
            for i in range(2):
                w_in_split_tile(i)
            ada_kept(3, 3)
            act.wait_ge(mod_ready, 1)
            modulate(0, SHIFT1)
            w_in_split_tile(2)
            conv = conv_products()
            for i in range(IN_TILES):
                act.wait_ge(proj, i + 1)
                bank = i % 6
                if i < 2 * CT:
                    if i % 2 == 0:
                        if i >= 2:
                            act.wait_ge(dve_proj, i // 2)
                        act.activation(sig, ps[:, bank, :], ACT.Sigmoid).then_inc(act_proj, 1)
                    ada_kept(4 + i, 6)
                elif i < 11:
                    n = i - 2 * CT
                    act.activation(scr[:, n, :], ps[:, bank, :], ACT.Square).then_inc(lat_sq, 1)
                    act.activation(cq[:, n, :] if n < 2 else ckv, ps[:, bank, :], ACT.Copy).then_inc(act_proj, 1)
                else:
                    act.activation(sqs[:, 10, :], ps[:, bank, :], ACT.Square)
                    act.activation(krg[:], ps[:, bank, :], ACT.Identity, scale=vec[:, KRG:KRG + 1]).then_inc(act_proj, 1)
                if i + 3 < IN_TILES:
                    w_in_split_tile(i + 3)
                for _ in range(TAPS_A_TILE if i >= 3 else 0):
                    next(conv, None)
            for i, width in enumerate((Q_RANK, KV_RANK)):
                act.wait_ge(lat_ss, 3)
                act.activation(root2[:, i * P:(i + 1) * P], ps[:, 6, i * P:(i + 1) * P], ACT.Sqrt, bias=eps, scale=1.0 / width).then_inc(lat_root, 1)
            for i in range(14):
                act.wait_ge(qk_mm, i + 1)
                src = ps[:, i % 6, :]
                if i == 6:
                    act.wait_ge(prod_used, POOL_ADDS)
                if i < 6 and i % 3 < 2:
                    h = 2 * (i // 3) + i % 3
                    act.activation(sqs[:, h, :], src, ACT.Square)
                    act.activation(qn[:, h, :], src, ACT.Identity, scale=vec[:, QHG:QHG + 1]).then_inc(qk_ev, 1)
                elif i < 6:
                    act.activation(sqs[:, 4 + i // 3, :], src, ACT.Square)
                    act.activation(qr[:, i // 3, :], src, ACT.Identity, scale=vec[:, QRG:QRG + 1]).then_inc(qk_ev, 1)
                elif i < 10:
                    act.activation(sqs[:, i, :], src, ACT.Square)
                    act.activation(kn[:, i - 6, :], src, ACT.Identity, scale=vec[:, KHG:KHG + 1]).then_inc(qk_ev, 1)
                else:
                    act.activation(V[:, i - 10, :], src, ACT.Copy).then_inc(qk_ev, 1)
            act.wait_ge(head_ss, 1)
            act.activation(head_rms, ps[:, 6, :], ACT.Sqrt, bias=eps, scale=1.0 / QK).then_inc(head_root, 1)
            for i in range(4 * HEADS + 4):
                if i < 4 * HEADS:
                    act.wait_ge(nm_ready, i + 1)
                    if i >= 3:
                        act.wait_ge(t_done, i - 2)
                    act.activation(prob[:, i % 3, :], ps[:, i % 3, :], ACT.Exp, bias=nmx[:, i:i + 1], scale=rqs[:, i:i + 1],
                                   accum_out=rsum[:, i:i + 1]).then_inc(exp_done, 1)
                j = i - 2
                if 0 <= j < 4 * HEADS:
                    act.wait_ge(t_done, j + 1)
                    if j >= TT and j % TT == 0:
                        act.wait_ge(pv_done, j // TT)
                    act.activation(PT[:, :, (j % TT) * P:(j % TT + 1) * P], ps[:, 3 + j % 2, :].rearrange("p (c n) -> p c n", c=TT), ACT.Copy).then_inc(pt_ev, 1)
                if 1 <= i <= CT:
                    act.wait_ge(cdev, i)
                    act.activation(scr[:, i - 1, :], acc[:, i - 1, :], ACT.Square).then_inc(csq, 1)
                if i == 6:
                    act.wait_ge(cvar, 1)
                    act.activation(scr[:, 0, 0:P], ps[:, 7, 0:P], ACT.Sqrt, bias=eps, scale=1.0 / CONV_CH).then_inc(croot, 1)
                if 3 <= i < 3 + KT:
                    kt = i - 3
                    act.wait_ge(w_out_in, 32)
                    act.wait_ge(roped, 3)
                    act.activation(w_out_high[kt], w_out[:, kt, :], ACT.Copy).then_inc(w_out_split, 1)
                if i == 4 * HEADS + 1:
                    for c in range(CT):
                        act.wait_ge(cnorm, c + 1)
                        act.activation(mix[:, HEADS + c, :], acc[:, c, :], ACT.Silu, bias=vec[:, CNB + c:CNB + c + 1], scale=vec[:, CNG + c:CNG + c + 1]).then_inc(cmix, 1)
                        act.wait_ge(cmix, c + 1)
                        act.activation(mix_high[:, HEADS + c, :], mix[:, HEADS + c, :], ACT.Copy).then_inc(mix_split, 1)
                if i >= 7 and i % TT == 3:
                    h = (i - 7) // TT
                    act.wait_ge(pv_done, h + 1)
                    act.activation(mix_high[:, h, :], ps[:, 5, :], ACT.Copy).then_inc(mix_split, 1)
                    act.activation(mix[:, h, :], ps[:, 5, :], ACT.Copy).then_inc(pv_ev, 1)
            norm(1, SHIFT2)
            modulate(1, SHIFT2)
            act.wait_ge(r_mm, 1)
            act.activation(lgT, ps[0:EXPERTS, 0, :], ACT.Copy).then_inc(rT_kept, 1)
            act.wait_ge(r_sub, 1)
            act.activation(lg[:], lg[:], ACT.Exp).then_inc(r_exp, 1)
            for i in range(2 * TT):
                act.wait_ge(htok_mm, i + 1)
                act.activation(h_tok3[:, i // 2, (i % 2) * HALF:(i % 2 + 1) * HALF], ps[:, 2 + i % 4, :], ACT.Copy).then_inc(htok_ev, 1)
            act.activation(stat[:, 0:1], stat[:, 0:1], ACT.Copy).then_inc(ye_free, 1)
            with act.Fori(0, PAIRS) as n:
                for r in range(2):
                    act.wait_ge(xe_mm, 2 * n + r + 1)
                    act.activation(x_e, ps[:, 0, :], ACT.Copy).then_inc(xe_ready, 1)
                    act.wait_ge(chunk_used, 12 * n + (6 * r + 2))
                    act.activation(sg, ps[:, 1, :], ACT.Silu).then_inc(sg_ready, 1)
                    act.wait_ge(hidT_mm, 2 * n + r + 1)
                    act.activation(hidT, ps[:, 3, :], ACT.Copy).then_inc(hidT_ready, 1)
                    act.wait_ge(chunk_used, 12 * n + (6 * r + 6))
                    act.wait_ge(st_free, 2 * n + r + 2)
                    out = ye[CAP * r:CAP * (r + 1), bass.ds(n, 1), :].rearrange("p a n -> p (a n)")
                    for half in range(2):
                        rows = slice(CAP * half, CAP * (half + 1))
                        last = act.activation(out[:, half * HALF:(half + 1) * HALF], ps[rows, 4, :], ACT.Identity, scale=gcol[rows, :])
                    last.then_inc(ye_free, 1)
            act.wait_ge(ye_free, EXPERTS + 1)
            act.wait_ge(chunk_used, 6 * EXPERTS)
            for n in range(PAIRS):
                act.activation(ye_hi[:, n, :], ye[:, n, :], ACT.Copy).then_inc(ye_hi_ready, 1)

        @block.vector
        def _(dve):
            step = Steps(dve, d_step)
            dve.wait_ge(rowsT_done, 1)
            dve.tensor_copy(vec[:], ps[:, 5, 0:NVEC]).then_inc(vec_ready, 1)
            dve.wait_ge(rowsT_done, 2)
            dve.tensor_copy(convw[:], ps[:, 7, 0:TAPS * CT]).then_inc(vec_ready, 1)

            dve.tensor_copy(c_rep, M["c_col"][:].unsqueeze(2).to_broadcast([P, KT, GROUP])).then_inc(c_spread, 1)

            def norm(k):
                dve.wait_ge(n_root, k + 1)
                dve.reciprocal(root, root).then_inc(n_inv, 1)
                dve.wait_ge(n_bc, k + 1)
                for kt in range(KT):
                    dve.tensor_tensor(hT[:, kt, :], xT[:, kt, :], ps[:, 7 - 6 * k, :], ALU.mult).then_inc(n_xn, 1)

            norm(0)
            dve.wait_ge(vec_ready, 2)

            def modulation(r):
                dve.wait_ge(ada_cols, 4 * r + 4)
                return dve.tensor_tensor(mod[:, 16 * r:16 * (r + 1)], ps[:, 4 if r == 0 else 7, :].rearrange("p (n k) -> p n k", k=GROUP)[:, :, 0],
                                         vec[:, ADA + 16 * r:ADA + 16 * (r + 1)], ALU.add)

            step(modulation(0))
            step.settle()
            dve.scalar_tensor_tensor(smod[:, 0:KT], mod[:, SCALE1:SCALE1 + KT], 1.0, vec[:, N1G:N1G + KT], ALU.add, ALU.mult).then_inc(mod_ready, 1)

            def convolve():
                for c in [c for c in range(CT) if c not in POOL_TAPS] + [c for c in POOL_TAPS if POOL_TAPS[c] < TAPS]:
                    for t in range(POOL_TAPS.get(c, 0), TAPS):
                        w, src = convw[:, t * CT + c:t * CT + c + 1], ypad[:, c, t:t + S]
                        if t == 0:
                            dve.wait_ge(dve_proj, c + 1)
                            step(dve.tensor_scalar(acc[:, c, :], src, w, vec[:, CB + c:CB + c + 1], ALU.mult, ALU.add))
                        else:
                            if c in POOL_TAPS:
                                dve.wait_ge(prod_used, POOL_ADDS)
                            step.settle()
                            op = dve.scalar_tensor_tensor(acc[:, c, :], src, w, acc[:, c, :], ALU.mult, ALU.add)
                            if t == TAPS - 1:
                                op.then_inc(conv_dve, 1)
                            else:
                                step(op)
                        yield

            def w_in_rest(i):
                dve.wait_ge(w_in_split, i + 1)
                c0, high = in_cols[i], w_in_high[i % 3].bitcast(F32)
                if i < IN_TILES - 1:
                    dve.tensor_tensor(w_in_low[:, :, c0:c0 + P], w_in[:, :, c0:c0 + P], high, ALU.subtract).then_inc(w_in_ready, 1)
                else:
                    dve.wait_ge(proj, 2 * CT + 1)
                    dve.tensor_tensor(w_in_low[:, :, 0:P].rearrange("p k (a n) -> p k a n", a=2), w_in[:, :, c0:c0 + ROPE].unsqueeze(2).to_broadcast([P, KT, 2, ROPE]),
                                      high.rearrange("p k (a n) -> p k a n", a=2), ALU.subtract).then_inc(w_in_ready, 1)

            for i in range(2):
                w_in_rest(i)
            for kt in range(KT):
                dve.wait_ge(h_split, kt + 1)
                dve.tensor_tensor(h_low[:, kt, :], hT[:, kt, :], h_high[:, kt, :].bitcast(F32), ALU.subtract).then_inc(h_low_ready, 1)
            w_in_rest(2)
            dve.wait_ge(pad_zero, 1)
            conv = convolve()
            for i in range(IN_TILES - 3):
                if i == 4:
                    modulation(1).then_inc(mod_ready, 1)
                if i % 2 == 1 and i < 2 * CT:
                    c = i // 2
                    dve.wait_ge(act_proj, c + 1)
                    dve.wait_ge(proj, i + 1)
                    dve.tensor_tensor(ypad[:, c, PAD:PAD + S], ps[:, i % 6, :], sig, ALU.mult).then_inc(dve_proj, 1)
                w_in_rest(i + 3)
                for _ in range(DVE_TAPS[i]):
                    next(conv, None)
            step(modulation(2))
            step.settle()
            dve.scalar_tensor_tensor(smod[:, KT:2 * KT], mod[:, SCALE2:SCALE2 + KT], 1.0, vec[:, N2G:N2G + KT], ALU.add, ALU.mult).then_inc(mod_ready, 1)
            dve.wait_ge(lat_root, 2)
            dve.reciprocal(root2, root2).then_inc(lat_inv, 1)
            dve.wait_ge(act_proj, 7)
            dve.wait_ge(lat_bc, 2)
            for i in range(2):
                dve.scalar_tensor_tensor(cq[:, i, :], cq[:, i, :], vec[:, QLG + i:QLG + i + 1], ps[:, 7, :], ALU.mult, ALU.mult).then_inc(lat_ready, 1)
            dve.scalar_tensor_tensor(ckv, ckv, vec[:, KVG:KVG + 1], ps[:, 6, :], ALU.mult, ALU.mult).then_inc(lat_ready, 1)
            for _ in conv:
                pass
            dve.wait_ge(uq_in, 48)
            ropes = (krg[:], qr[:, 0, :], qr[:, 1, :])
            for i, x in enumerate(ropes):
                dve.wait_ge(rot_mm, i + 1)
                step(dve.tensor_tensor(rin[:, 6, :], ps[:, 2 + i, :], sin, ALU.mult))
                step(dve.tensor_tensor(x, x, cos, ALU.mult))
                step.settle()
                dve.tensor_tensor(x, x, rin[:, 6, :], ALU.add).then_inc(roped, 1)
                dve.wait_ge(roped, i + 1)
            dve.wait_ge(head_cols, 1)
            step(dve.reciprocal(rqk, ps[:, 7, :].rearrange("p (n k) -> p n k", k=GROUP // 2)[:, :, 0]))
            step.settle()
            factors = rqk.rearrange("p (t h k) -> p t h k", t=TT, h=HEADS)
            step(dve.tensor_scalar(rqs.rearrange("p (h t) -> p t h", h=HEADS), factors[:, :, :, 0], QSCALE, None, ALU.mult))

            def key_diag(h):
                dve.tensor_tensor(kd.rearrange("p (t n) -> p t n", t=TT), ident.unsqueeze(1).to_broadcast([P, TT, P]),
                                  factors[:, :, h, 1].unsqueeze(2).to_broadcast([P, TT, P]), ALU.mult).then_inc(kd_ready, 1)

            def key_norm(h):
                half = slice(ROPE * (h % 2), ROPE * (h % 2 + 1))
                dve.wait_ge(kb_mm, h + 1)
                dve.tensor_tensor(kn[:, h, :], kn[:, h, :], ps[:, 6, :], ALU.mult)
                dve.tensor_tensor(kr[half, h // 2, :], krg[half, :], ps[half, 6, :], ALU.mult).then_inc(qk_ready, 1)

            key_diag(0)
            key_norm(0)
            step.settle()
            def mix_rest(n):
                kt = MIX_ORDER[n]
                dve.wait_ge(mix_split, n + 1)
                if kt < HEADS:
                    dve.wait_ge(pv_ev, kt + 1)
                dve.tensor_tensor(mix_low[:, kt, :], mix[:, kt, :], mix_high[:, kt, :].bitcast(F32), ALU.subtract).then_inc(mix_ready, 1)

            for i in range(4 * HEADS + 1):
                if i < 4 * HEADS:
                    dve.wait_ge(s_done, i + 1)
                    step(dve.reduce_max(mx[:, i:i + 1], ps[:, i % 3, :], AX_X))
                    step.settle()
                    dve.tensor_scalar(nmx[:, i:i + 1], mx[:, i:i + 1], rqs[:, i:i + 1], -1.0, ALU.mult, ALU.mult).then_inc(nm_ready, 1)
                    if i // TT + 1 < HEADS:
                        if i % TT == 0:
                            key_diag(i // TT + 1)
                        if i % TT == 2:
                            key_norm(i // TT + 1)
                j = i - 1
                if j >= 0:
                    dve.wait_ge(exp_done, j + 1)
                    step(dve.reciprocal(rrs[:, j:j + 1], rsum[:, j:j + 1]))
                    step.settle()
                    if j >= 3:
                        dve.wait_ge(t_done, j - 2)
                    dve.tensor_scalar(diag[:, j % 3, :], ident, rrs[:, j:j + 1], None, ALU.mult).then_inc(diag_ready, 1)
                if i >= 8 and i % TT == 0:
                    mix_rest(i // TT - 2)
                if i < CT:
                    dve.wait_ge(cmean, 1)
                    dve.scalar_tensor_tensor(acc[:, i, :], ps[:, 5, :], -1.0 / CONV_CH, acc[:, i, :], ALU.mult, ALU.add).then_inc(cdev, 1)
                if i == 7:
                    dve.wait_ge(croot, 1)
                    dve.reciprocal(scr[:, 0, 0:P], scr[:, 0, 0:P]).then_inc(cinv, 1)
                if 9 <= i < 9 + CT:
                    dve.wait_ge(cbc, 1)
                    dve.wait_ge(csq, CT)
                    dve.tensor_tensor(acc[:, i - 9, :], acc[:, i - 9, :], ps[:, 7, :], ALU.mult).then_inc(cnorm, 1)
            for n in range(HEADS - 1, KT):
                mix_rest(n)
            for dt in range(KT):
                dve.wait_ge(wout_done, dt + 1)
                dve.scalar_tensor_tensor(xT[:, dt, :], ps[:, dt, :], mod[:, GATE1 + dt:GATE1 + dt + 1], xT[:, dt, :], ALU.mult, ALU.add).then_inc(x1_ready, 1)
            dve.wait_ge(x1_ready, KT)
            norm(1)
            dve.wait_ge(r_done, 1)
            logits = ps[:, 1, 0:TT * EXPERTS].rearrange("p (t e) -> p t e", t=TT)
            step(dve.reduce_max(mx[:, 0:TT], logits, AX_X))
            step.settle()
            dve.tensor_tensor(lg[:], logits, mx[:, 0:TT].unsqueeze(2).to_broadcast([P, TT, EXPERTS]), ALU.subtract).then_inc(r_sub, 1)
            dve.wait_ge(r_exp, 1)
            step(dve.reduce_sum(rsum[:, 0:TT], lg[:], AX_X))
            step.settle()
            step(dve.reciprocal(rrs[:, 0:TT], rsum[:, 0:TT]))
            step.settle()
            dve.tensor_tensor(aff[:], lg[:], rrs[:, 0:TT].unsqueeze(2).to_broadcast([P, TT, EXPERTS]), ALU.mult).then_inc(aff_ready, 1)
            dve.wait_ge(affT_done, 1)
            step(dve.tensor_copy(work, ps[0:EXPERTS, 6, :]))
            for _ in range(CAP // 8):
                step.settle()
                step(dve.max(top8[:], work))
                step.settle()
                step(dve.match_replace(work, top8[:], work, -1.0))
            step.settle()
            step(dve.tensor_scalar(affT, work, 0.0, None, ALU.is_lt))
            step.settle()
            step(dve.tensor_tensor_scan(rank, affT, affT, 0.0, ALU.add, ALU.max))
            step.settle()
            step(dve.tensor_tensor(rank, rank, affT, ALU.mult))
            step.settle()
            dve.tensor_scalar(rankm, rank, -1.0, None, ALU.add).then_inc(rank_ready, 1)
            dve.wait_ge(rankT_done, 1)
            step(dve.tensor_copy(rankT[:].rearrange("p t e -> p (t e)"), ps[:, 7, 0:TT * EXPERTS]))
            step.settle()
            dve.memset(gcol[:], 0.0).then_inc(st_free, 1)

            def build(e):
                for t in range(TT):
                    dve.tensor_scalar(s_e[:, t, :], slot_row, rankT[:, t, bass.ds(e, 1)], None, ALU.is_equal)
                dve.tensor_scalar(sel_e[:], ones[0:EXPERTS, :], const[0:EXPERTS, bass.ds(e, 1)], None, ALU.mult).then_inc(s_built, 1)

            with dve.Fori(0, PAIRS) as n:
                for r in range(2):
                    e = 2 * n + r
                    dve.wait_ge(st_free, e + 1)
                    build(e)
                    dve.wait_ge(st_mm, e + 1)
                    dve.wait_ge(ye_free, e + 1)
                    dve.tensor_copy(gcol[:], ps[:, 7, 0:1])
                    rows = slice(CAP * r, CAP * (r + 1))
                    dve.tensor_scalar(ohT[rows, bass.ds(n, 1), :].rearrange("p a n -> p (a n)"), ps[rows, 6, :], slot_col[rows, :], None, ALU.is_equal).then_inc(st_free, 1)
                    dve.wait_ge(sg_ready, e + 1)
                    dve.wait_ge(chunk_used, 12 * n + (6 * r + 4))
                    dve.tensor_tensor(hid, sg, ps[:, 2, :], ALU.mult).then_inc(hid_ready, 1)
            for n in range(PAIRS):
                dve.wait_ge(ye_hi_ready, n + 1)
                dve.tensor_tensor(ye_lo[:, n, :], ye[:, n, :], ye_hi[:, n, :].bitcast(F32), ALU.subtract).then_inc(ye_lo_ready, 1)
            dve.wait_ge(out_done, 1)
            for dt in range(KT):
                dve.scalar_tensor_tensor(xT[:, dt, :], ps[:, dt, :], mod[:, GATE2 + dt:GATE2 + dt + 1], xT[:, dt, :], ALU.mult, ALU.add).then_inc(x2_ready, 1)


def memory(nc, ctx):
    M = dict(ps=ctx.enter_context(nc.psum_tensor("ps", [P, 8, 512], F32)))
    with nc.sbuf_tensor("xT_r", [P, KT, S], FR) as rounded:
        M["xT_r"] = rounded
    for name, shape in dict(xT=[P, KT, S], const=[P, C_ALL], ones=[P, P]).items():
        M[name] = ctx.enter_context(nc.sbuf_tensor(name, shape, F32))
    return M


def memory1(nc, ctx, M):
    M = dict(M)
    shared = dict(hy=[P, 2 * KT * S], h_tok=[P, TT * D], one_hot_T=[P, EXPERTS * S], ring=[P, 6 * TT * D])
    with ExitStack() as rounded:
        halves = dict(ring=[P, 3 * TT * D], ring2=[P, 3 * TT * D])
        for name, shape in {**shared, **halves}.items():
            M[name + "_r"] = rounded.enter_context(nc.sbuf_tensor(name + "_r", shape, FR))
    for name, shape in dict(
        **shared, scr=[P, 4, S],
        krg=[P, S], c_col=[P, KT], vec=[P, NVEC], convw=[P, TAPS * CT],
        mod=[P, N_MOD * KT], smod=[P, 2 * KT], stat=[P, 112],
        lg=[P, TT, EXPERTS], aff=[P, TT, EXPERTS], rankT=[P, TT, EXPERTS], top8=[EXPERTS, 8],
        sel_e=[EXPERTS, P], gcol=[P, 1],
    ).items():
        M[name] = ctx.enter_context(nc.sbuf_tensor(name, shape, F32))
    return M

MEM = 256
MT = MEM // P
GROUPS_A = 8
B_W, B_HEADS, TAPS_B = 1280, 10, 4
C_HEADS, C_DIM = 4, 256
A_W, C_W = 1024, C_HEADS * C_DIM
EXP_GROUPS, PER_GROUP, FF2 = 4, 4, 256
ALPHA = 2.0 ** 0.25
CSCALE = C_DIM ** -0.5
LRU_C = 8.0
Z_U, Z_V, Z_X, Z_G, Z_Q, Z_M = 0, A_W, 2 * A_W, 2 * A_W + B_W, 2 * A_W + 2 * B_W, 2 * A_W + 2 * B_W + C_W
IN_W2 = Z_M + 3 * D
SLOTS, SLOT = 4, KT * 2 * P
GROUP_CHUNKS = 3 * PER_GROUP
AHEAD = 2
LIFT = 2.0 ** 60
V_BIN, V_CB, V_BA, V_BX, V_LAM, NV1 = 0, 68, 78, 88, 98, 108
V_CW, V_BO, V_LIG, V_LIB, V_LMG, V_LMB, V_L1G, V_L1B, V_L2G, V_L2B, NV2 = (108 + n for n in (0, 40, 48, 56, 64, 72, 80, 88, 96, 104, 112))


def second(nc, A, sem, M):
    ps, const, xT, ones = M["ps"], M["const"], M["xT"], M["ones"]
    ident = const[:, C_IDENT:C_IDENT + P]
    eps = const[:, C_EPS5:C_EPS5 + 1]
    flat, u, v, ob, wT, vec, lru = (M[n] for n in ("tmp", "u", "v", "ob", "wT", "vec2", "lru"))
    tmp = flat[:, 0:10 * S].rearrange("p (k n) -> p k n", k=10)
    y, small = M["y"], M["small"]
    raw, w_low, w_high = ([M[name][:, i * SLOT:(i + 1) * SLOT] for i in range(SLOTS)] for name in ("raw", "raw_r", "w_high"))
    x_high, x_low = M["x_high"], M["xT_r"]
    act_high, u_low, ob_low, y_low, v_high = M["act_high"], M["u_r"], M["ob_r"], M["y_r"], M["v_r"]
    y_high = v_high[:].rearrange("p (k n) -> p k n", k=KT)
    ob_high = [act_high[:, k, :] for k in range(KT)] + [u_low[:, k, :] for k in range(B_HEADS - KT)]
    memT_high = act_high[:].rearrange("p k n -> p (k n)")[:, 0:KT * MEM].rearrange("p (k m) -> p k m", k=KT)
    memT_low = M["tmp_r"][:, 2048:2048 + KT * MEM].rearrange("p (k m) -> p k m", k=KT)
    rows1, rows2 = u[:, 0, 0:P], u[:, 1, 0:P]
    v3 = v[:].rearrange("p (t d) -> p t d", t=TT)
    wab = v[:, 0:2 * B_HEADS * P].rearrange("p (h n) -> p h n", h=2 * B_HEADS)
    row_in_y = y[:].rearrange("p k n -> p (k n)")
    bv_row, lvg_row, lvb_row, bs_row = (row_in_y[:, i * D:(i + 1) * D] for i in range(4))
    w_s = ob[:, 0:2, :].rearrange("p a n -> p (a n)").rearrange("p (g s) -> p g s", g=GROUPS_A)
    padded = S + TAPS_B - 1
    xpad = [flat[:, 8 * S + i * padded:8 * S + (i + 1) * padded] for i in range(2)]
    xc, gt = [tmp[:, i, :] for i in range(2)], [tmp[:, 2 + i, :] for i in range(2)]
    rr, ii, aa, th = (tmp[:, 4 + i, :] for i in range(4))
    gate_sg = [tmp[:, 8 + i, :] for i in range(2)]
    mem_tok = flat[:, 0:MT * D].rearrange("p (t d) -> p t d", t=MT)
    memT = flat[:, 2048:2048 + KT * MEM].rearrange("p (k m) -> p k m", k=KT)
    kT = v[:, 0:KT * MEM].rearrange("p (k m) -> p k m", k=KT)
    vm = v[:, 2048:2048 + MT * C_W].rearrange("p (t d) -> p t d", t=MT)
    prob = flat[:, 0:768].rearrange("p (i m) -> p i m", i=3)
    PT = flat[:, 768:1792].rearrange("p (c n) -> p c n", c=MT)
    diag = flat[:, 2048:2432].rearrange("p (i n) -> p i n", i=3)
    obf = ob[:].rearrange("p k n -> p (k n)")
    w_g = obf[:, 0:KT * 20].rearrange("p (k n) -> p k n", k=KT)
    bg_row = obf[:, 160:180]
    gl = obf[:, 256:256 + TT * 20].rearrange("p (t n) -> p t n", t=TT)
    gw = [obf[:, 512 + 64 * i:512 + 64 * (i + 1)].rearrange("p (t n) -> p t n", t=TT) for i in range(6)]
    gateT = obf[0:EXPERTS, 1024:1536]
    sel = obf[0:EXPERTS, 1536:2048].rearrange("p (j n) -> p j n", j=PER_GROUP)
    prio = small[:, 0:4]
    w_g_high, w_g_low = (M["ob_r"][:].rearrange("p k n -> p (k n)")[:, a:a + KT * 20].rearrange("p (k n) -> p k n", k=KT) for a in (2048, 2304))
    glT = obf[0:20, 2560:2560 + S]

    rows_in2, rows_turned, vec2_ready, bc_in, wab_in, ws_in, wg_in, mem_in = (
        sem(n) for n in ("rows_in2", "rows_turned", "vec2_ready", "bc_in", "wab_in", "ws_in", "wg_in", "mem_in"))
    slot_in = [sem(f"slot_in{i}") for i in range(SLOTS)]
    w_split, w_ready, x_split, x_ready, u_split, u_low_ready, ob_split, ob_low_ready, y_split, y_low_ready, x_whole = (
        sem(n) for n in ("w_split", "w_ready", "x_split", "x_ready", "u_split", "u_low_ready", "ob_split", "ob_low_ready", "y_split", "y_low_ready", "x_whole"))
    memT_split, memT_low_ready, hid_split, hid_low, wg_split, wg_ready, glT_kept = (
        sem(n) for n in ("memT_split", "memT_low_ready", "hid_split", "hid_low", "wg_split", "wg_ready", "glT_kept"))
    l_inv, l_bc = sem("l_inv"), sem("l_bc")
    l_sum, l_dev, l_sq, l_ss, l_root, l_norm, l_ready = (sem(n) for n in ("l_sum", "l_dev", "l_sq", "l_ss", "l_root", "l_norm", "l_ready"))
    bz_mm, bz_ev, xc_ready, bg_mm, bg_ev, at_ready, m2_ready, mult_ready, ob_ready, lru_ready, pads_zero = (
        sem(n) for n in ("bz_mm", "bz_ev", "xc_ready", "bg_mm", "bg_ev", "at_ready", "m2_ready", "mult_ready", "ob_ready", "lru_ready", "pads_zero"))
    lru_exp = sem("lru_exp")
    ws_turned, ws_kept, wT_ready = sem("ws_turned"), sem("ws_kept"), sem("wT_ready")
    v_mm, v_biased, v_gelu, v_var, v_root, v_ready, u_mm, u_ready, sp_mm, oa_ready = (
        sem(n) for n in ("v_mm", "v_biased", "v_gelu", "v_var", "v_root", "v_ready", "u_mm", "u_ready", "sp_mm", "oa_ready"))
    mz_mm, m_mm, m_sg, m_y = sem("mz_mm"), sem("m_mm"), sem("m_sg"), sem("m_y")
    mem_var, mem_root, mem_norm, memT_mm, memT_ready, kv_mm, kv_ready, q_mm, q_ready = (
        sem(n) for n in ("mem_var", "mem_root", "mem_norm", "memT_mm", "memT_ready", "kv_mm", "kv_ready", "q_mm", "q_ready"))
    cs_done, cnm_ready, cexp_done, cdiag_ready, ct_done, cpt_ev, cpv_done, oc_ready = (
        sem(n) for n in ("cs_done", "cnm_ready", "cexp_done", "cdiag_ready", "ct_done", "cpt_ev", "cpv_done", "oc_ready"))
    ax_ready, wo_mm, wo_used, gl_mm = sem("ax_ready"), sem("wo_mm"), sem("wo_used"), sem("gl_mm")
    g_mm, g_sub, g_exp, e_sub, e_exp, gate_ready, gate_turned, gateT_ready, prio_ready, f_init = (
        sem(n) for n in ("g_mm", "g_sub", "g_exp", "e_sub", "e_exp", "gate_ready", "gate_turned", "gateT_ready", "prio_ready", "f_init"))
    sel_ready, bc_mm, up_mm, sg2_ready, hid2_ready, dn_mm, dn_used = (
        sem(n) for n in ("sel_ready", "bc_mm", "up_mm", "sg2_ready", "hid2_ready", "dn_mm", "dn_used"))
    o_mm, o_kept, stored, d2_step, a2_step, m_loop = (sem(n) for n in ("o_mm", "o_kept", "stored", "d2_step", "a2_step", "m_loop"))

    def cols(name, c0, n=2 * P):
        w = A[name][0].rearrange("(k p) n -> p k n", p=P)
        return w[:, :, c0:c0 + n]

    def two(name, c0, step, at):
        return cols(name, c0, 2 * step).rearrange("p k (a c) -> p k a c", a=2)[:, :, :, at:at + P]

    chunks, last_use = [], []

    def chunk(src, used, count):
        chunks.append(src)
        last_use.append((used, count))

    for h in range(B_HEADS):
        chunk(two("w_in_2", Z_X, B_W, h * P), bz_mm, 2 * h + 2)
    CH_V = len(chunks)
    for n in range(4):
        chunk(cols("w_in_2", Z_V + 2 * P * n), v_mm, TT * (n + 1))
    CH_U = len(chunks)
    for n in range(4):
        chunk(cols("w_in_2", Z_U + 2 * P * n), u_mm, 2 * n + 2)

    def dense(branch, name):
        first = len(chunks)
        for n in range(4):
            chunk(cols("w_in_2", Z_M + branch * D + 2 * P * n), mz_mm, KT * branch + 2 * n + 2)
            chunk(cols(name, 2 * P * n), m_mm, KT * branch + 2 * n + 2)
        return first

    CH_MA = dense(0, "p_a_2")
    CH_MB = len(chunks)
    for n in range(4):
        chunk(cols("w_in_2", Z_M + D + 2 * P * n), mz_mm, KT + 2 * n + 2)
        for dt in (2 * n, 2 * n + 1):
            chunk(cols("p_b_2", P * dt, P), m_mm, KT + dt + 1)
    CH_K = len(chunks)
    for n in range(8):
        chunk(cols("w_kv_2", 2 * P * n), kv_mm, 2 * n + 2)
    CH_Q = len(chunks)
    for n in range(4):
        chunk(cols("w_in_2", Z_Q + 2 * P * n), q_mm, 2 * n + 2)
    CH_MC = dense(2, "p_c_2")
    CH_O = len(chunks)
    for n in range(4):
        chunk(cols("w_o_2", 2 * P * n), wo_mm, 2 * n + 2)
    CH_E = len(chunks)

    def slot_of(tensors, i):
        src = chunks[i]
        k, n = src.shape[1], math.prod(src.shape[2:])
        return tensors[i % SLOTS][:, 0:k * n].rearrange("p (k n) -> p k n", k=k)

    def group_slot(tensors, n):
        return tensors[(CH_E + n) % SLOTS].rearrange("p (k n) -> p k n", k=KT)

    sizes = [16 * (2 if len(src.shape) == 4 else 1) for src in chunks]
    group_sizes = [32] * (2 * PER_GROUP) + [16] * PER_GROUP
    per_group = sum(group_sizes[0::SLOTS])

    def landed(i):
        return sum(sizes[i % SLOTS:i + 1:SLOTS])

    def group_landed(g, n):
        return per_group * g + (sum(sizes[(CH_E + n) % SLOTS::SLOTS]) + sum(group_sizes[n % SLOTS:n + 1:SLOTS]))

    with nc.Block() as block:
        @block.sync
        def _(sp):
            row = 0
            for name, n in (("b_in_2", 68), ("conv_b_2", 10), ("b_a_2", 10), ("b_x_2", 10), ("lam_2", 10)):
                sp.dma_start(rows1[row:row + n, :], A[name].rearrange("a (k p) -> (a k) p", p=P)).then_inc(rows_in2, 16)
                row += n
            sp.dma_start(rows2[0:40, :], A["conv_w_2"].rearrange("a t (c p) -> (a t c) p", p=P)).then_inc(rows_in2, 16)
            row = 40
            for name in ("b_o_2", "ln_in_g_2", "ln_in_b_2", "ln_mem_g_2", "ln_mem_b_2", "ln1_g_2", "ln1_b_2", "ln2_g_2", "ln2_b_2"):
                src = A[name] if len(A[name].shape) == 1 else A[name].rearrange("a d -> (a d)")
                sp.dma_start(rows2[row:row + KT, :], src.rearrange("(k p) -> k p", p=P)).then_inc(rows_in2, 16)
                row += KT
            for i, src in enumerate(chunks):
                if i >= SLOTS:
                    sp.wait_ge(*last_use[i - SLOTS])
                dst = slot_of(raw, i)
                if len(src.shape) == 3:
                    sp.dma_start(dst, src).then_inc(slot_in[i % SLOTS], 16)
                else:
                    for a in range(2):
                        sp.dma_start(dst[:, :, a * P:(a + 1) * P], src[:, :, a, :]).then_inc(slot_in[i % SLOTS], 16)

            def experts(g):
                for n in range(GROUP_CHUNKS):
                    if n < SLOTS and g is None:
                        sp.wait_ge(*last_use[CH_E + n - SLOTS])
                    elif n < SLOTS:
                        sp.wait_ge(dn_mm, 8 * g + (2 * n - 6))
                    elif n < 8 + SLOTS:
                        sp.wait_ge(up_mm, (0 if g is None else 16 * g) + 2 * (n - SLOTS) + 2)
                    e = (0 if g is None else PER_GROUP * g) + n // 2
                    dst, there = group_slot(raw, n), slot_in[(CH_E + n) % SLOTS]
                    if n < 8:
                        w = A["w_up_2"][0, bass.ds(e, 1)].rearrange("e (k p) n -> p (e k) n", p=P)
                        for a in range(2):
                            c0 = FF2 * a + P * (n % 2)
                            sp.dma_start(dst[:, :, a * P:(a + 1) * P], w[:, :, c0:c0 + P]).then_inc(there, 16)
                    else:
                        cs = slice(2 * P * (n - 8), 2 * P * (n - 7))
                        w = A["w_down_2"][0, bass.ds(0 if g is None else PER_GROUP * g, PER_GROUP), :, cs]
                        sp.dma_start(dst, w.rearrange("e (i p) n -> p (e i) n", p=P)).then_inc(there, 16)

            experts(None)
            with sp.Fori(1, EXP_GROUPS) as g:
                experts(g)
            out = A["out"][0].rearrange("(t p) d -> p t d", p=P)
            for t in range(TT):
                sp.wait_ge(o_kept, 2 * t + 2)
                sp.dma_start(out[:, t], v3[:, t]).then_inc(stored, 16)
            sp.wait_ge(stored, 16 * TT)

        @block.gpsimd
        def _(pool):
            for i in range(2):
                zero = pool.memset(xpad[i][:, 0:TAPS_B - 1], 0.0)
            zero.then_inc(pads_zero, 1)
            for n in range(4):
                last = pool.memset(prio[:, n:n + 1], float(4 - n))
            last.then_inc(prio_ready, 1)
            for dst, src in ((bv_row, A["b_in_2"][:, Z_V:Z_V + A_W]), (lvg_row, A["ln_v_g_2"]), (lvb_row, A["ln_v_b_2"]),
                             (bs_row, A["b_s_2"].rearrange("a g t -> a (g t)"))):
                pool.dma_start(dst, src.to_broadcast([P, D])).then_inc(bc_in, 16)
            def low(i, dst, src, high):
                pool.wait_ge(w_split, i + 1)
                pool.tensor_tensor(dst, src, high.bitcast(F32), ALU.subtract).then_inc(w_ready, 1)

            for i in range(CH_K):
                low(i, slot_of(w_low, i), slot_of(raw, i), slot_of(w_high, i))
                if i == AHEAD:
                    pool.wait_ge(ws_kept, 2)
                    pool.affine_select(out=wT[:], in_=wT[:], compare_op=ALU.is_ge, fill=0.0, base=0, pattern=[[0, GROUPS_A], [1, P]], channel_multiplier=-1).then_inc(wT_ready, 1)
            pool.wait_ge(m_y, 2 * KT)
            pool.dma_start(w_g[:, :, 0:4], A["w_rg_2"][0].rearrange("(k p) n -> p k n", p=P)).then_inc(wg_in, 16)
            pool.dma_start(w_g[:, :, 4:20], A["w_re_2"][0].rearrange("(k p) n -> p k n", p=P)).then_inc(wg_in, 16)
            pool.dma_start(bg_row[:, 0:4], A["b_rg_2"].to_broadcast([P, 4])).then_inc(wg_in, 16)
            pool.dma_start(bg_row[:, 4:20], A["b_re_2"].to_broadcast([P, 16])).then_inc(wg_in, 16)
            for i in range(CH_K, CH_E):
                low(i, slot_of(w_low, i), slot_of(raw, i), slot_of(w_high, i))
            with pool.Fori(0, EXP_GROUPS) as g:
                for n in range(GROUP_CHUNKS):
                    low(GROUP_CHUNKS * g + (CH_E + n), group_slot(w_low, n), group_slot(raw, n), group_slot(w_high, n))

        @block.tensor
        def _(pe):
            def passes(out, terms, ready=None):
                for n, (s_high, s_low, m_high, m_low) in enumerate(terms):
                    if ready is not None:
                        pe.wait_ge(ready[0], ready[1] + (n + 1))
                    pe.matmul(out, s_high, m_high, start=(n == 0), stop=False)
                    pe.matmul(out, s_high, m_low, start=False, stop=False)
                    mm = pe.matmul(out, s_low, m_high, start=False, stop=(n == len(terms) - 1))
                return mm

            def feature_tile(bank, i, n, high, low, ready=None):
                pe.wait_ge(w_ready, i + 1)
                h, l, tile = slot_of(w_high, i), slot_of(w_low, i), slice(n * P, (n + 1) * P)
                return passes(ps[:, bank, :], [(h[:, k, tile], l[:, k, tile], high[k], low[k]) for k in range(chunks[i].shape[1])], ready)

            def tiles(x):
                return [x[:, k, :] for k in range(x.shape[1])]

            def z_tile(bank, i, n, ready=None):
                return feature_tile(bank, i, n, tiles(x_high), tiles(x_low), ready)

            def turn_vectors():
                pe.wait_ge(rows_in2, 16 * 15)
                pe.transpose(ps[:, 6, 0:NV1], rows1[0:NV1, :], ident[0:NV1, 0:NV1]).then_inc(rows_turned, 1)
                pe.transpose(ps[:, 7, 0:NV2 - NV1], rows2[0:NV2 - NV1, :], ident[0:NV2 - NV1, 0:NV2 - NV1]).then_inc(rows_turned, 1)
            def layer_norm(k, x):
                for kt in range(KT):
                    mm = pe.matmul(ps[:, 0, :], ones[:], x[:, kt, :], start=(kt == 0), stop=(kt == KT - 1))
                mm.then_inc(l_sum, 1)
                if k == 0:
                    turn_vectors()
                for kt in range(KT):
                    pe.wait_ge(l_sq, KT * k + kt + 1)
                    for g in range(TT):
                        mm = pe.matmul(ps[GROUP * g:GROUP * (g + 1), 1, 0:P], ones[:, 0:GROUP], tmp[:, kt % 4, g * P:(g + 1) * P], start=(kt == 0), stop=(kt == KT - 1))
                    mm.then_inc(l_ss, 1)
                pe.wait_ge(l_inv, k + 1)
                pe.wait_ge(l_dev, KT * (k + 1))
                for g in range(TT):
                    first = ident[:, GROUP * g:GROUP * g + 1].to_broadcast([P, P])
                    mm = pe.matmul(ps[:, 0, g * P:(g + 1) * P], first, tmp[:, 4, 0:P], start=True, stop=True)
                mm.then_inc(l_bc, 1)

            layer_norm(0, xT)
            pe.wait_ge(vec2_ready, 2)
            pe.wait_ge(wab_in, 32)
            for h in range(B_HEADS + 1):
                if h < B_HEADS:
                    for part in range(2):
                        i = 2 * h + part
                        if i >= 4:
                            pe.wait_ge(bz_ev, i - 3)
                        z_tile(2 + i % 4, h, part, (x_ready, 0) if i == 0 else None).then_inc(bz_mm, 1)
                if h == 0:
                    pe.wait_ge(ws_in, 16)
                    for g in range(GROUPS_A):
                        mm = pe.transpose(ps[:, 6 + g // 4, (g % 4) * P:(g % 4 + 1) * P], w_s[:, g, :], ident)
                        if g % 4 == 3:
                            mm.then_inc(ws_turned, 1)
                if h == 1:
                    pe.wait_ge(ws_kept, 2)
                if h >= 1:
                    pe.wait_ge(xc_ready, h)
                    if h >= 2:
                        pe.wait_ge(bg_ev, h - 1)
                    pe.matmul(ps[:, 6, :], wab[:, h - 1, :], xc[(h - 1) % 2], start=True, stop=True)
                    pe.matmul(ps[:, 7, :], wab[:, B_HEADS + h - 1, :], xc[(h - 1) % 2], start=True, stop=True).then_inc(bg_mm, 1)
            pe.wait_ge(bz_ev, 2 * B_HEADS)
            for i in range(4 * TT):
                n, t = i // TT, i % TT
                pe.wait_ge(w_ready, CH_V + n + 1)
                if i >= 4:
                    pe.wait_ge(v_biased, i - 3)
                h, l, rows = slot_of(w_high, CH_V + n), slot_of(w_low, CH_V + n), slice(t * P, (t + 1) * P)
                passes(ps[:, 2 + i % 4, 0:2 * P], [(x_high[:, k, rows], x_low[:, k, rows], h[:, k, :], l[:, k, :]) for k in range(KT)]).then_inc(v_mm, 1)
            for i in range(KT):
                pe.wait_ge(v_biased, min(i + 13, 16))
                if i >= 4:
                    pe.wait_ge(u_ready, i - 3)
                z_tile(2 + i % 4, CH_U + i // 2, i % 2).then_inc(u_mm, 1)
            pe.wait_ge(wT_ready, 1)
            pe.wait_ge(v_ready, TT)
            pe.wait_ge(u_ready, KT)
            for g in range(GROUPS_A):
                if g >= 4:
                    pe.wait_ge(oa_ready, g - 3)
                for c in range(TT):
                    mm = pe.matmul(ps[:, 2 + g % 4, c * P:(c + 1) * P], v3[:, c, g * P:(g + 1) * P], wT[:, g, :], start=True, stop=True)
                mm.then_inc(sp_mm, 1)

            def merge_dense(branch, first, high, low):
                for dt in range(KT):
                    n, zc = KT * branch + dt, first + 2 * (dt // 2)
                    a = 2 + 2 * (n % 2)
                    if n >= 2:
                        pe.wait_ge(m_y, n - 1)
                    z_tile(a, zc, dt % 2).then_inc(mz_mm, 1)
                    pe.wait_ge(u_low_ready, KT * (branch // 2 + 1))
                    feature_tile(a + 1, zc + 1, dt % 2, high, low).then_inc(m_mm, 1)

            pe.wait_ge(oa_ready, 5)
            merge_dense(0, CH_MA, tiles(act_high), tiles(u_low))
            for dt in range(KT):
                n, zc = KT + dt, CH_MB + 3 * (dt // 2)
                a = 2 + 2 * (n % 2)
                pe.wait_ge(m_y, n - 1)
                z_tile(a, zc, dt % 2).then_inc(mz_mm, 1)
                pe.wait_ge(ob_low_ready, B_HEADS)
                feature_tile(a + 1, zc + 1 + dt % 2, 0, ob_high, tiles(ob_low)).then_inc(m_mm, 1)
            for kt in range(KT):
                if kt < MT:
                    pe.wait_ge(mem_norm, MT)
                if kt >= 2:
                    pe.wait_ge(memT_ready, kt - 1)
                for t in range(MT):
                    mm = pe.transpose(ps[:, 6 + kt % 2, t * P:(t + 1) * P], mem_tok[:, t, kt * P:(kt + 1) * P], ident)
                mm.then_inc(memT_mm, 1)
            pe.wait_ge(memT_low_ready, KT)
            for i in range(KT + 4 * MT):
                if i >= 2:
                    pe.wait_ge(kv_ready, i - 1)
                bank = 6 + i % 2
                if i < KT:
                    c, tile = CH_K + i // 2, slice((i % 2) * P, (i % 2 + 1) * P)
                    pe.wait_ge(w_ready, c + 1)
                    h, l = slot_of(w_high, c), slot_of(w_low, c)
                    mm = passes(ps[:, bank, 0:MEM], [(h[:, k, tile], l[:, k, tile], memT_high[:, k, :], memT_low[:, k, :]) for k in range(KT)])
                else:
                    c, t = CH_K + 4 + (i - KT) // MT, (i - KT) % MT
                    pe.wait_ge(w_ready, c + 1)
                    h, l, rows = slot_of(w_high, c), slot_of(w_low, c), slice(t * P, (t + 1) * P)
                    mm = passes(ps[:, bank, 0:2 * P], [(memT_high[:, k, rows], memT_low[:, k, rows], h[:, k, :], l[:, k, :]) for k in range(KT)])
                mm.then_inc(kv_mm, 1)
            pe.wait_ge(m_y, 2 * KT)
            for i in range(KT):
                if i >= 4:
                    pe.wait_ge(q_ready, i - 3)
                z_tile(2 + i % 4, CH_Q + i // 2, i % 2).then_inc(q_mm, 1)
            pe.wait_ge(q_ready, KT)
            pe.wait_ge(kv_ready, KT + 4 * MT)
            N = C_HEADS * TT
            for i in range(N + 3):
                if i < N:
                    h, q0 = i // TT, (i % TT) * P
                    if i >= 3:
                        pe.wait_ge(cexp_done, i - 2)
                    for k in range(2):
                        mm = pe.matmul(ps[:, i % 3, 0:MEM], u[:, 2 * h + k, q0:q0 + P], kT[:, 2 * h + k, :], start=(k == 0), stop=(k == 1))
                    mm.then_inc(cs_done, 1)
                j = i - 2
                if 0 <= j < N:
                    pe.wait_ge(cdiag_ready, j + 1)
                    if j >= 2:
                        pe.wait_ge(cpt_ev, j - 1)
                    for c in range(MT):
                        mm = pe.matmul(ps[:, 3 + j % 2, c * P:(c + 1) * P], prob[:, j % 3, c * P:(c + 1) * P], diag[:, j % 3, :], start=True, stop=True)
                    mm.then_inc(ct_done, 1)
                if i >= 6 and i % TT == 2:
                    h = (i - 6) // TT
                    pe.wait_ge(cpt_ev, TT * (h + 1))
                    if h >= 1:
                        pe.wait_ge(oc_ready, h)
                    for d in range(2):
                        for c in range(MT):
                            mm = pe.matmul(ps[:, 5 + d, :], vm[:, c, h * C_DIM + d * P:h * C_DIM + (d + 1) * P], PT[:, c, :], start=(c == 0), stop=(c == MT - 1))
                    mm.then_inc(cpv_done, 1)
            merge_dense(2, CH_MC, tiles(act_high), tiles(u_low))
            pe.wait_ge(m_y, 3 * KT)
            pe.wait_ge(y_low_ready, KT)
            for dt in range(KT):
                if dt >= 4:
                    pe.wait_ge(wo_used, dt - 3)
                feature_tile(2 + dt % 4, CH_O + dt // 2, dt % 2, tiles(y_high), tiles(y_low)).then_inc(wo_mm, 1)
            pe.wait_ge(wo_used, KT)
            layer_norm(1, xT)
            pe.wait_ge(wg_ready, 1)
            passes(ps[0:20, 6, :], [(w_g_high[:, k, :], w_g_low[:, k, :], x_high[:, k, :], x_low[:, k, :]) for k in range(KT)], (x_ready, KT)).then_inc(gl_mm, 1)
            pe.wait_ge(glT_kept, 1)
            for t in range(TT):
                mm = pe.transpose(ps[:, 7, t * 20:(t + 1) * 20], glT[:, t * P:(t + 1) * P], ident[0:20, 0:20])
            mm.then_inc(g_mm, 1)
            pe.wait_ge(gate_ready, 1)
            for t in range(TT):
                mm = pe.transpose(ps[0:EXPERTS, 6, t * P:(t + 1) * P], gw[0][:, t, :], ident)
            mm.then_inc(gate_turned, 1)
            pe.wait_ge(gateT_ready, 1)
            with pe.Fori(0, EXP_GROUPS) as g:
                pe.wait_ge(sel_ready, g + 1)
                for n in range(2 * PER_GROUP):
                    j, i = n // 2, n % 2
                    if i == 0:
                        pe.wait_ge(hid2_ready, 8 * g + max(1, 2 * j - 1))
                        pe.matmul(ps[:, 4 + j % 2, :], sel[:, j, :], gateT, start=True, stop=True).then_inc(bc_mm, 1)
                    pe.wait_ge(w_ready, GROUP_CHUNKS * g + (CH_E + n + 1))
                    if n >= 2:
                        pe.wait_ge(hid2_ready, 8 * g + n)
                    h, l = group_slot(w_high, n), group_slot(w_low, n)
                    for part in range(2):
                        tile = slice(part * P, (part + 1) * P)
                        passes(ps[:, 2 * i + part, :], [(h[:, k, tile], l[:, k, tile], x_high[:, k, :], x_low[:, k, :]) for k in range(KT)]).then_inc(up_mm, 1)
                for dt in range(KT):
                    pe.wait_ge(w_ready, GROUP_CHUNKS * g + (CH_E + 8 + dt // 2 + 1))
                    pe.wait_ge(dn_used, 8 * g + dt + 1)
                    h, l, tile = group_slot(w_high, 8 + dt // 2), group_slot(w_low, 8 + dt // 2), slice((dt % 2) * P, (dt % 2 + 1) * P)
                    passes(ps[:, 6 + dt % 2, :], [(h[:, k, tile], l[:, k, tile], act_high[:, k, :], u_low[:, k, :]) for k in range(KT)],
                           (hid_low, 8 * g) if dt == 0 else None).then_inc(dn_mm, 1)
            pe.wait_ge(dn_used, 8 * EXP_GROUPS + 2)
            layer_norm(2, y)
            pe.wait_ge(l_ready, 3 * KT)
            for i in range(2 * TT):
                t, n = i // 2, i % 2
                if i >= 4:
                    pe.wait_ge(o_kept, i - 3)
                for b in range(4):
                    mm = pe.transpose(ps[:, 2 + i % 4, b * P:(b + 1) * P], y[:, 4 * n + b, t * P:(t + 1) * P], ident)
                mm.then_inc(o_mm, 1)

        @block.scalar
        def _(act):
            step = Steps(act, a2_step)
            act.dma_start(w_s, A["w_s_2"][0].rearrange("g t s -> t g s")).then_inc(ws_in, 16)
            act.dma_start(wab[:, 0:B_HEADS], A["w_a_2"][0].rearrange("h i j -> i h j")).then_inc(wab_in, 16)
            act.dma_start(wab[:, B_HEADS:], A["w_x_2"][0].rearrange("h i j -> i h j")).then_inc(wab_in, 16)

            def col(n):
                return vec[:, n:n + 1]

            split = [0]

            def ahead(i):
                while split[0] <= min(i + AHEAD, CH_E - 1):
                    n = split[0]
                    act.wait_ge(slot_in[n % SLOTS], landed(n))
                    act.activation(slot_of(w_high, n), slot_of(raw, n), ACT.Copy).then_inc(w_split, 1)
                    split[0] += 1

            def group_split(g, n):
                act.wait_ge(slot_in[(CH_E + n) % SLOTS], group_landed(g, n))
                act.activation(group_slot(w_high, n), group_slot(raw, n), ACT.Copy).then_inc(w_split, 1)

            def layer_norm(k, x, gain, bias, last=None):
                for kt in range(KT):
                    act.wait_ge(l_dev, KT * k + kt + 1)
                    if kt >= 4:
                        act.wait_ge(l_ss, KT * k + kt - 3)
                    act.activation(tmp[:, kt % 4, :], x[:, kt, :], ACT.Square).then_inc(l_sq, 1)
                if k == 0:
                    act.wait_ge(vec2_ready, 2)
                act.wait_ge(l_ss, KT * (k + 1))
                act.activation(tmp[:, 4, 0:P], ps[:, 1, 0:P], ACT.Sqrt, bias=eps, scale=1.0 / D).then_inc(l_root, 1)
                for kt in range(KT):
                    act.wait_ge(l_norm, KT * k + kt + 1)
                    act.activation(x[:, kt, :], x[:, kt, :], ACT.Identity, bias=col(bias + kt), scale=col(gain + kt)).then_inc(l_ready, 1)
                    if k < 2:
                        act.wait_ge(l_ready, KT * k + kt + 1)
                        act.activation(x_high[:, kt, :], x[:, kt, :], ACT.Copy).then_inc(x_split, 1)

            ahead(0)
            layer_norm(0, xT, V_LIG, V_LIB)
            act.wait_ge(lru_ready, 1)
            act.activation(lru[:, 1, :], lru[:, 0, :], ACT.Exp, scale=-1.0).then_inc(lru_exp, 1)
            act.wait_ge(pads_zero, 1)
            for h in range(B_HEADS + 1):
                if h < B_HEADS:
                    ahead(h)
                    act.wait_ge(bz_mm, 2 * h + 1)
                    if h >= 2:
                        act.wait_ge(xc_ready, h - 1)
                    act.activation(xpad[h % 2][:, TAPS_B - 1:], ps[:, 2 + (2 * h) % 4, :], ACT.Identity, bias=col(V_BIN + Z_X // P + h)).then_inc(bz_ev, 1)
                    act.wait_ge(bz_mm, 2 * h + 2)
                    if h >= 2:
                        act.wait_ge(ob_ready, h - 1)
                    act.activation(gt[h % 2], ps[:, 2 + (2 * h + 1) % 4, :], ACT.Gelu_apprx_tanh, bias=col(V_BIN + Z_G // P + h)).then_inc(bz_ev, 1)
                if h == 0:
                    for i in range(2):
                        act.wait_ge(ws_turned, i + 1)
                        act.activation(wT[:, 4 * i:4 * i + 4, :], ps[:, 6 + i, :].rearrange("p (g t) -> p g t", g=4), ACT.Copy).then_inc(ws_kept, 1)
                if h >= 1:
                    k = h - 1
                    act.wait_ge(bg_mm, k + 1)
                    if k >= 1:
                        act.wait_ge(ob_ready, k)
                    step(act.activation(rr, ps[:, 6, :], ACT.Sigmoid, bias=col(V_BA + k)))
                    act.activation(ii, ps[:, 7, :], ACT.Sigmoid, bias=col(V_BX + k)).then_inc(bg_ev, 1)
                    step.settle()
                    act.wait_ge(lru_ready, 2)
                    act.activation(aa, rr, ACT.Exp, scale=lru[:, 2, k:k + 1])
                    act.activation(th, rr, ACT.Tanh, scale=lru[:, 3, k:k + 1]).then_inc(at_ready, 1)
                    act.wait_ge(m2_ready, k + 1)
                    act.activation(th, rr, ACT.Sqrt, scale=LIFT).then_inc(mult_ready, 1)
            for i in range(4 * TT):
                n, t = i // TT, i % TT
                ahead(CH_V + n)
                act.wait_ge(v_biased, i + 1)
                part = v3[:, t, n * 2 * P:(n + 1) * 2 * P]
                act.activation(part, part, ACT.Gelu_apprx_tanh).then_inc(v_gelu, 1)
            for i in range(KT):
                ahead(CH_U + i // 2)
                if i == 1:
                    act.wait_ge(v_var, TT)
                    act.activation(small[:, 16:20], small[:, 8:16].rearrange("p (t s) -> p t s", s=2)[:, :, 1], ACT.Sqrt, bias=eps).then_inc(v_root, 1)
                act.wait_ge(u_mm, i + 1)
                act.activation(u[:, i, :], ps[:, 2 + i % 4, :], ACT.Gelu_apprx_tanh, bias=col(V_BIN + i)).then_inc(u_ready, 1)

            def merge(branch, first, per):
                for dt in range(KT):
                    n = KT * branch + dt
                    ahead(first + per * (dt // 2) + (per - 2) * (dt % 2) + 1)
                    if n == KT + 2:
                        act.wait_ge(mem_var, MT)
                        act.activation(small[:, 16:18], small[:, 8:12].rearrange("p (t s) -> p t s", s=2)[:, :, 1], ACT.Sqrt, bias=eps).then_inc(mem_root, 1)
                    act.wait_ge(mz_mm, n + 1)
                    if n >= 2:
                        act.wait_ge(m_y, n - 1)
                    act.activation(gate_sg[n % 2], ps[:, 2 + 2 * (n % 2), :], ACT.Sigmoid, bias=col(V_BIN + Z_M // P + n)).then_inc(m_sg, 1)

            for g in range(GROUPS_A):
                act.wait_ge(oa_ready, g + 1)
                act.activation(act_high[:, g, :], u[:, g, :], ACT.Copy).then_inc(u_split, 1)
            merge(0, CH_MA, 2)
            act.wait_ge(ob_ready, B_HEADS)
            act.wait_ge(m_mm, KT)
            for h in range(B_HEADS):
                act.activation(ob_high[h], ob[:, h, :], ACT.Copy).then_inc(ob_split, 1)
            act.dma_start(mem_tok, A["mem_2"][0].rearrange("(t p) d -> p t d", p=P)).then_inc(mem_in, 16)
            merge(1, CH_MB, 3)
            for kt in range(KT):
                act.wait_ge(memT_mm, kt + 1)
                act.activation(memT[:, kt, :], ps[:, 6 + kt % 2, 0:MEM], ACT.Identity, bias=col(V_LMB + kt), scale=col(V_LMG + kt)).then_inc(memT_ready, 1)
                act.wait_ge(memT_ready, kt + 1)
                act.activation(memT_high[:, kt, :], memT[:, kt, :], ACT.Copy).then_inc(memT_split, 1)
            for i in range(KT + 4 * MT):
                ahead(CH_K + i // 2)
                act.wait_ge(kv_mm, i + 1)
                if i < KT:
                    act.activation(kT[:, i, :], ps[:, 6 + i % 2, 0:MEM], ACT.Copy).then_inc(kv_ready, 1)
                else:
                    n, t = (i - KT) // MT, (i - KT) % MT
                    act.activation(vm[:, t, n * 2 * P:(n + 1) * 2 * P], ps[:, 6 + i % 2, 0:2 * P], ACT.Copy).then_inc(kv_ready, 1)
            for i in range(KT):
                ahead(CH_Q + i // 2)
                act.wait_ge(q_mm, i + 1)
                act.activation(u[:, i, :], ps[:, 2 + i % 4, :], ACT.Identity, bias=col(V_BIN + Z_Q // P + i)).then_inc(q_ready, 1)
            ahead(CH_MC)
            N = C_HEADS * TT
            for i in range(N + 4):
                if i < N:
                    act.wait_ge(cnm_ready, i + 1)
                    if i >= 3:
                        act.wait_ge(ct_done, i - 2)
                    act.activation(prob[:, i % 3, :], ps[:, i % 3, 0:MEM], ACT.Exp, bias=small[:, 64 + i:65 + i], scale=CSCALE, accum_out=small[:, 32 + i:33 + i]).then_inc(cexp_done, 1)
                j = i - 2
                if 0 <= j < N:
                    act.wait_ge(ct_done, j + 1)
                    if j >= TT and j % TT == 0:
                        act.wait_ge(cpv_done, j // TT)
                    act.activation(PT[:, :, (j % TT) * P:(j % TT + 1) * P], ps[:, 3 + j % 2, 0:MEM].rearrange("p (c n) -> p c n", c=MT), ACT.Copy).then_inc(cpt_ev, 1)
                if i >= 7 and i % TT == 3:
                    h = (i - 7) // TT
                    act.wait_ge(cpv_done, h + 1)
                    for d in range(2):
                        act.activation(u[:, 2 * h + d, :], ps[:, 5 + d, :], ACT.Copy)
                        last = act.activation(act_high[:, 2 * h + d, :], ps[:, 5 + d, :], ACT.Copy)
                    last.then_inc(oc_ready, 1)
            merge(2, CH_MC, 2)
            for kt in range(KT):
                act.wait_ge(m_y, 2 * KT + kt + 1)
                act.activation(y_high[:, kt, :], y[:, kt, :], ACT.Copy).then_inc(y_split, 1)
            ahead(CH_O)
            for kt in range(KT):
                if kt % 2 == 0:
                    ahead(CH_O + kt // 2)
                act.wait_ge(x_whole, kt + 1)
                act.activation(xT[:, kt, :], xT[:, kt, :], ACT.Identity, bias=col(V_BO + kt), scale=ALPHA).then_inc(ax_ready, 1)
            act.wait_ge(wg_in, 64)
            act.activation(w_g_high, w_g, ACT.Copy).then_inc(wg_split, 1)
            layer_norm(1, xT, V_L1G, V_L1B)
            for n in range(AHEAD):
                group_split(0, n)
            act.wait_ge(gl_mm, 1)
            act.activation(glT, ps[0:20, 6, :], ACT.Copy).then_inc(glT_kept, 1)
            act.wait_ge(g_sub, 1)
            act.activation(gw[0][:, :, 0:4], gw[0][:, :, 0:4], ACT.Exp).then_inc(g_exp, 1)
            act.wait_ge(e_sub, 1)
            act.activation(gw[3][:, :, 0:4], gw[3][:, :, 0:4], ACT.Exp).then_inc(e_exp, 1)

            def experts(g, last):
                def high(n):
                    act.wait_ge(hid2_ready, 8 * g + n + 2)
                    act.activation(act_high[:, n, :], u[:, n, :], ACT.Copy).then_inc(hid_split, 1)

                for n in range(2 * PER_GROUP):
                    group_split(g, n + AHEAD)
                    act.wait_ge(up_mm, 16 * g + 2 * n + 1)
                    act.wait_ge(hid2_ready, 8 * g + n + 1)
                    act.activation(tmp[:, n % 2, :], ps[:, 2 * (n % 2), :], ACT.Silu).then_inc(sg2_ready, 1)
                    if n >= 1:
                        high(n - 1)
                high(2 * PER_GROUP - 1)
                for n in range(2 * PER_GROUP + AHEAD, GROUP_CHUNKS):
                    group_split(g, n)
                if not last:
                    for n in range(AHEAD):
                        group_split(g + 1, n)

            with act.Fori(0, EXP_GROUPS - 1) as g:
                experts(g, False)
            experts(EXP_GROUPS - 1, True)
            layer_norm(2, y, V_L2G, V_L2B)
            for i in range(2 * TT):
                t, n = i // 2, i % 2
                act.wait_ge(o_mm, i + 1)
                act.activation(v3[:, t, n * HALF:(n + 1) * HALF], ps[:, 2 + i % 4, :], ACT.Copy).then_inc(o_kept, 1)

        @block.vector
        def _(dve):
            step = Steps(dve, d2_step)

            def col(n):
                return vec[:, n:n + 1]

            def vectors():
                dve.wait_ge(rows_turned, 1)
                dve.tensor_copy(vec[:, 0:NV1], ps[:, 6, 0:NV1]).then_inc(vec2_ready, 1)
                dve.wait_ge(rows_turned, 2)
                dve.tensor_copy(vec[:, NV1:NV2], ps[:, 7, 0:NV2 - NV1]).then_inc(vec2_ready, 1)
                dve.wait_ge(vec2_ready, 2)
                lam = vec[:, V_LAM:V_LAM + B_HEADS]
                step(dve.tensor_scalar(lru[:, 4, :], lam, -1.0, None, ALU.mult))
                step.settle()
                dve.tensor_tensor(lru[:, 0, :], lam, lru[:, 4, :], ALU.max).then_inc(lru_ready, 1)

            def layer_norm(k, x):
                dve.wait_ge(l_sum, k + 1)
                for kt in range(KT):
                    dve.scalar_tensor_tensor(x[:, kt, :], ps[:, 0, :], -1.0 / D, x[:, kt, :], ALU.mult, ALU.add).then_inc(l_dev, 1)
                if k == 0:
                    vectors()
                dve.wait_ge(l_root, k + 1)
                dve.reciprocal(tmp[:, 4, 0:P], tmp[:, 4, 0:P]).then_inc(l_inv, 1)
                dve.wait_ge(l_bc, k + 1)
                for n in range(KT + 3 if k < 2 else KT):
                    if n < KT:
                        dve.tensor_tensor(x[:, n, :], x[:, n, :], ps[:, 0, :], ALU.mult).then_inc(l_norm, 1)
                    kt = n - 3
                    if kt < 0 or k == 2:
                        continue
                    dve.wait_ge(x_split, KT * k + kt + 1)
                    if k == 1:
                        dve.tensor_scalar(y[:, kt, :], x[:, kt, :], ALPHA, None, ALU.mult).then_inc(f_init, 1)
                    dve.tensor_tensor(x_low[:, kt, :], x[:, kt, :], x_high[:, kt, :].bitcast(F32), ALU.subtract).then_inc(x_ready, 1)

            layer_norm(0, xT)
            e, s, s2, acc = lru[:, 1, :], lru[:, 2, :], lru[:, 3, :], lru[:, 5, :]
            dve.wait_ge(lru_exp, 1)
            step(dve.tensor_scalar(s, e, 2.0, None, ALU.add))
            step.settle()
            step(dve.reciprocal(s, s))
            step.settle()
            step(dve.tensor_tensor(s, s, e, ALU.mult))
            step.settle()
            step(dve.tensor_tensor(s2, s, s, ALU.mult))
            step(dve.memset(acc, 2.0 / 19))
            for n in range(17, 0, -2):
                step.settle()
                step(dve.tensor_tensor(acc, acc, s2, ALU.mult))
                step.settle()
                step(dve.tensor_scalar(acc, acc, 2.0 / n, None, ALU.add))
            step.settle()
            step(dve.tensor_tensor(acc, acc, s, ALU.mult))
            step.settle()
            step(dve.scalar_tensor_tensor(acc, lru[:, 4, :], 0.0, acc, ALU.max, ALU.add))
            step.settle()
            step(dve.tensor_scalar(s, acc, -LRU_C, None, ALU.mult))
            dve.tensor_scalar(s2, acc, LRU_C, None, ALU.mult).then_inc(lru_ready, 1)

            for h in range(B_HEADS + 1):
                if h < B_HEADS:
                    dve.wait_ge(bz_ev, 2 * h + 1)
                    if h >= 2:
                        dve.wait_ge(bg_mm, h - 1)
                    x, src = xc[h % 2], xpad[h % 2]
                    for t in range(TAPS_B):
                        w = col(V_CW + t * B_HEADS + h)
                        if t == 0:
                            step(dve.tensor_scalar(x, src[:, 0:S], w, col(V_CB + h), ALU.mult, ALU.add))
                        else:
                            step.settle()
                            op = dve.scalar_tensor_tensor(x, src[:, t:t + S], w, x, ALU.mult, ALU.add)
                            if t < TAPS_B - 1:
                                step(op)
                            else:
                                op.then_inc(xc_ready, 1)
                if h >= 1:
                    k = h - 1
                    dve.wait_ge(at_ready, k + 1)
                    step(dve.tensor_tensor(rr, aa, aa, ALU.mult))
                    step(dve.tensor_tensor(ii, ii, xc[k % 2], ALU.mult))
                    step.settle()
                    dve.scalar_tensor_tensor(rr, rr, 1.0, th, ALU.add, ALU.mult).then_inc(m2_ready, 1)
                    dve.wait_ge(mult_ready, k + 1)
                    step(dve.scalar_tensor_tensor(ii, th, LIFT ** -0.5, ii, ALU.mult, ALU.mult))
                    step.settle()
                    step(dve.tensor_tensor_scan(rr, aa, ii, 0.0, ALU.mult, ALU.add))
                    step.settle()
                    dve.tensor_tensor(ob[:, k, :], rr, gt[k % 2], ALU.mult).then_inc(ob_ready, 1)

            dve.wait_ge(bc_in, 64)
            for i in range(4 * TT):
                n, t = i // TT, i % TT
                dve.wait_ge(v_mm, i + 1)
                cs = slice(n * 2 * P, (n + 1) * 2 * P)
                dve.tensor_tensor(v3[:, t, cs], ps[:, 2 + i % 4, 0:2 * P], bv_row[:, cs], ALU.add).then_inc(v_biased, 1)

            def row_stats(x, t, done):
                for n in range(2):
                    step(dve.bn_stats(small[:, 100 + 6 * n:106 + 6 * n], x[:, t, n * HALF:(n + 1) * HALF]))
                step.settle()
                dve.bn_aggr(small[:, 8 + 2 * t:10 + 2 * t], small[:, 100:112]).then_inc(done, 1)
                dve.wait_ge(done, t + 1)

            for t in range(TT):
                dve.wait_ge(v_gelu, 3 * TT + t + 1)
                row_stats(v3, t, v_var)
            dve.wait_ge(v_root, 1)
            step(dve.reciprocal(small[:, 16:20], small[:, 16:20]))
            step.settle()
            for t in range(TT):
                step(dve.tensor_scalar(v3[:, t], v3[:, t], small[:, 8 + 2 * t:9 + 2 * t], small[:, 16 + t:17 + t], ALU.subtract, ALU.mult))
                step.settle()
                step(dve.tensor_tensor(v3[:, t], v3[:, t], lvg_row, ALU.mult))
                step.settle()
                dve.tensor_tensor(v3[:, t], v3[:, t], lvb_row, ALU.add).then_inc(v_ready, 1)
            def u_rest(use, k):
                dve.wait_ge(u_split, KT * use + k + 1)
                dve.tensor_tensor(u_low[:, k, :], u[:, k, :], act_high[:, k, :].bitcast(F32), ALU.subtract).then_inc(u_low_ready, 1)

            for g in range(GROUPS_A):
                dve.wait_ge(sp_mm, g + 1)
                s = tmp[:, 4 + g % 2, :]
                step(dve.tensor_tensor(s.rearrange("p (c t) -> p c t", c=TT), ps[:, 2 + g % 4, :].rearrange("p (c t) -> p c t", c=TT),
                                       bs_row[:, g * P:(g + 1) * P].unsqueeze(1).to_broadcast([P, TT, P]), ALU.add))
                step.settle()
                dve.tensor_tensor(u[:, g, :], u[:, g, :], s, ALU.mult).then_inc(oa_ready, 1)
                if g >= 1:
                    u_rest(0, g - 1)
            u_rest(0, GROUPS_A - 1)

            def merge(branch):
                for dt in range(KT):
                    n = KT * branch + dt
                    dve.wait_ge(m_sg, n + 1)
                    dve.wait_ge(m_mm, n + 1)
                    sg, out = gate_sg[n % 2], ps[:, 3 + 2 * (n % 2), :]
                    if branch == 0:
                        dve.tensor_tensor(y[:, dt, :], sg, out, ALU.mult).then_inc(m_y, 1)
                    else:
                        step(dve.tensor_tensor(sg, sg, out, ALU.mult))
                        step.settle()
                        dve.tensor_tensor(y[:, dt, :], y[:, dt, :], sg, ALU.add).then_inc(m_y, 1)
                    if n == KT + 3:
                        dve.wait_ge(mem_root, 1)
                        step(dve.reciprocal(small[:, 16:18], small[:, 16:18]))
                        step.settle()
                        for t in range(MT):
                            dve.tensor_scalar(mem_tok[:, t], mem_tok[:, t], small[:, 8 + 2 * t:9 + 2 * t], small[:, 16 + t:17 + t], ALU.subtract, ALU.mult).then_inc(mem_norm, 1)

            merge(0)
            for h in range(B_HEADS):
                dve.wait_ge(ob_split, h + 1)
                dve.tensor_tensor(ob_low[:, h, :], ob[:, h, :], ob_high[h].bitcast(F32), ALU.subtract).then_inc(ob_low_ready, 1)
            dve.wait_ge(mem_in, 16)
            for t in range(MT):
                row_stats(mem_tok, t, mem_var)
            merge(1)
            for kt in range(KT):
                dve.wait_ge(memT_split, kt + 1)
                dve.tensor_tensor(memT_low[:, kt, :], memT[:, kt, :], memT_high[:, kt, :].bitcast(F32), ALU.subtract).then_inc(memT_low_ready, 1)

            def oc_rest(h):
                dve.wait_ge(oc_ready, h + 1)
                for k in (2 * h, 2 * h + 1):
                    dve.tensor_tensor(u_low[:, k, :], u[:, k, :], act_high[:, k, :].bitcast(F32), ALU.subtract).then_inc(u_low_ready, 1)

            N = C_HEADS * TT
            for i in range(N + 1):
                if i < N:
                    dve.wait_ge(cs_done, i + 1)
                    step(dve.reduce_max(small[:, 48 + i:49 + i], ps[:, i % 3, 0:MEM], AX_X))
                    step.settle()
                    dve.tensor_scalar(small[:, 64 + i:65 + i], small[:, 48 + i:49 + i], -CSCALE, None, ALU.mult).then_inc(cnm_ready, 1)
                j = i - 1
                if j >= 0:
                    dve.wait_ge(cexp_done, j + 1)
                    step(dve.reciprocal(small[:, 80 + j:81 + j], small[:, 32 + j:33 + j]))
                    step.settle()
                    if j >= 3:
                        dve.wait_ge(ct_done, j - 2)
                    dve.tensor_scalar(diag[:, j % 3, :], ident, small[:, 80 + j:81 + j], None, ALU.mult).then_inc(cdiag_ready, 1)
                if i >= 9 and i % TT == 1:
                    oc_rest((i - 9) // TT)
            for h in (C_HEADS - 2, C_HEADS - 1):
                oc_rest(h)
            merge(2)
            for kt in range(KT):
                dve.wait_ge(y_split, kt + 1)
                dve.tensor_tensor(y_low[:, kt, :], y[:, kt, :], y_high[:, kt, :].bitcast(F32), ALU.subtract).then_inc(y_low_ready, 1)
            dve.wait_ge(m_mm, 3 * KT)
            for kt in range(KT):
                dve.tensor_tensor(xT[:, kt, :], x_low[:, kt, :].bitcast(F32), x_high[:, kt, :].bitcast(F32), ALU.add).then_inc(x_whole, 1)
            for dt in range(KT):
                dve.wait_ge(ax_ready, dt + 1)
                dve.wait_ge(wo_mm, dt + 1)
                dve.tensor_tensor(xT[:, dt, :], ps[:, 2 + dt % 4, :], xT[:, dt, :], ALU.add).then_inc(wo_used, 1)
            dve.wait_ge(wg_split, 1)
            dve.tensor_tensor(w_g_low, w_g, w_g_high.bitcast(F32), ALU.subtract).then_inc(wg_ready, 1)
            layer_norm(1, xT)
            dve.wait_ge(g_mm, 1)
            dve.wait_ge(prio_ready, 1)
            dve.wait_ge(wg_in, 64)

            def op(instruction):
                step(instruction)
                step.settle()

            def wide(x, n=4):
                return x.unsqueeze(2).to_broadcast([P, TT, n])

            def first_best(out, x, top, rest):
                op(dve.tensor_tensor(out, x, wide(top), ALU.is_equal))
                op(dve.tensor_tensor(out, out, prio.unsqueeze(1).to_broadcast([P, TT, 4]), ALU.mult))
                op(dve.reduce_max(rest, out, AX_X))
                op(dve.tensor_tensor(out, out, wide(rest), ALU.is_equal))

            top, rest, ptop = small[:, 8:12], small[:, 12:16], small[:, 16:20]
            op(dve.tensor_tensor(gl, ps[:, 7, 0:TT * 20].rearrange("p (t n) -> p t n", t=TT), bg_row.unsqueeze(1).to_broadcast([P, TT, 20]), ALU.add))
            op(dve.reduce_max(top, gl[:, :, 0:4], AX_X))
            dve.tensor_tensor(gw[0][:, :, 0:4], gl[:, :, 0:4], wide(top), ALU.subtract).then_inc(g_sub, 1)
            group = gw[1][:, :, 0:4]
            first_best(group, gl[:, :, 0:4], top, rest)
            dve.wait_ge(g_exp, 1)
            op(dve.reduce_sum(ptop, gw[0][:, :, 0:4], AX_X))
            op(dve.reciprocal(ptop, ptop))
            per = gw[2].rearrange("p t (g j) -> p t g j", g=4)
            op(dve.tensor_tensor(per, gl[:, :, 4:20].rearrange("p t (g j) -> p t g j", g=4), group.unsqueeze(3).to_broadcast([P, TT, 4, 4]), ALU.mult))
            inside = gw[3][:, :, 0:4]
            op(dve.reduce_sum(inside, per.rearrange("p t g j -> p t j g"), AX_X))
            op(dve.reduce_max(top, inside, AX_X))
            dve.tensor_tensor(inside, inside, wide(top), ALU.subtract).then_inc(e_sub, 1)
            dve.wait_ge(e_exp, 1)
            one, two = gw[4][:, :, 0:4], gw[5][:, :, 0:4]
            op(dve.reduce_max(top, inside, AX_X))
            first_best(one, inside, top, rest)
            op(dve.scalar_tensor_tensor(gw[4][:, :, 4:8], one, -2.0, inside, ALU.mult, ALU.add))
            op(dve.reduce_max(top, gw[4][:, :, 4:8], AX_X))
            first_best(two, gw[4][:, :, 4:8], top, rest)
            op(dve.tensor_tensor(one, one, two, ALU.add))
            op(dve.tensor_tensor(one, one, inside, ALU.mult))
            op(dve.reduce_sum(rest, one, AX_X))
            op(dve.reciprocal(rest, rest))
            op(dve.tensor_tensor(rest, rest, ptop, ALU.mult))
            op(dve.tensor_tensor(one, one, wide(rest), ALU.mult))
            dve.tensor_tensor(gw[0].rearrange("p t (g j) -> p t g j", g=4), group.unsqueeze(3).to_broadcast([P, TT, 4, 4]),
                              one.unsqueeze(2).to_broadcast([P, TT, 4, 4]), ALU.mult).then_inc(gate_ready, 1)
            dve.wait_ge(gate_turned, 1)
            dve.tensor_copy(gateT, ps[0:EXPERTS, 6, :]).then_inc(gateT_ready, 1)
            dve.wait_ge(f_init, KT)
            dve.memset(small[:, 20:21], 0.0).then_inc(hid2_ready, 1)
            dve.memset(small[:, 21:22], 0.0).then_inc(dn_used, 2)
            def select(g):
                for j in range(PER_GROUP):
                    last = dve.tensor_scalar(sel[:, j, :], ones[0:EXPERTS, :], const[0:EXPERTS, bass.ds(PER_GROUP * g + j, 1)], None, ALU.mult)
                last.then_inc(sel_ready, 1)

            select(0)
            with dve.Fori(0, EXP_GROUPS) as g:
                def rest(n):
                    dve.wait_ge(hid_split, 8 * g + n + 1)
                    dve.tensor_tensor(u_low[:, n, :], u[:, n, :], act_high[:, n, :].bitcast(F32), ALU.subtract).then_inc(hid_low, 1)

                for n in range(2 * PER_GROUP):
                    j, i = n // 2, n % 2
                    dve.wait_ge(up_mm, 16 * g + 2 * n + 2)
                    dve.wait_ge(sg2_ready, 8 * g + n + 1)
                    dve.tensor_tensor(tmp[:, 2 + i, :], tmp[:, i, :], ps[:, 2 * i + 1, :], ALU.mult).then_inc(m_loop, 1)
                    dve.wait_ge(m_loop, 8 * g + n + 1)
                    dve.wait_ge(bc_mm, 4 * g + j + 1)
                    dve.tensor_tensor(u[:, n, :], tmp[:, 2 + i, :], ps[:, 4 + j % 2, :], ALU.mult).then_inc(hid2_ready, 1)
                    if n >= 1:
                        rest(n - 1)
                rest(2 * PER_GROUP - 1)
                select(g + 1)
                for dt in range(KT):
                    dve.wait_ge(dn_mm, 8 * g + dt + 1)
                    dve.tensor_tensor(y[:, dt, :], y[:, dt, :], ps[:, 6 + dt % 2, :], ALU.add).then_inc(dn_used, 1)
            layer_norm(2, y)


def memory2(nc, ctx, M):
    M = dict(M)
    shared = dict(raw=[P, SLOTS * SLOT], u=[P, KT, S], ob=[P, B_HEADS, S], y=[P, KT, S], v=[P, TT * D], tmp=[P, 8 * S + 2 * (S + TAPS_B - 1)])
    with ExitStack() as rounded:
        for name, shape in shared.items():
            M[name + "_r"] = rounded.enter_context(nc.sbuf_tensor(name + "_r", shape, FR))
    for name, shape in shared.items():
        M[name] = ctx.enter_context(nc.sbuf_tensor(name, shape, F32))
    for name, shape in dict(w_high=[P, SLOTS * SLOT], x_high=[P, KT, S], act_high=[P, KT, S]).items():
        M[name] = ctx.enter_context(nc.sbuf_tensor(name, shape, FR))
    for name, shape in dict(wT=[P, GROUPS_A, P], vec2=[P, NV2], lru=[P, 6, B_HEADS], small=[P, 112]).items():
        M[name] = ctx.enter_context(nc.sbuf_tensor(name, shape, F32))
    return M


def program(nc, A):
    with ExitStack() as ctx:
        M = memory(nc, ctx)
        with ExitStack() as first:
            M1 = memory1(nc, first, M)
            prologue(nc, A, lambda name: ctx.enter_context(nc.semaphore(name)), M1)
            layer_sems = []

            def layer_sem(name):
                layer_sems.append(first.enter_context(nc.semaphore(name)))
                return layer_sems[-1]

            with nc.Fori(0, DEPTH) as l:
                layer(nc, A, layer_sem, M1, l)
                nc.gpsimd.sem_clear(range(layer_sems[0].num, layer_sems[-1].num + 1))
                nc.all_engine_barrier()
        with ExitStack() as last:
            second(nc, A, lambda name: ctx.enter_context(nc.semaphore(name)), memory2(nc, last, M))


def constants():
    import numpy as np

    c = np.zeros((P, C_ALL), np.float32)
    part = np.arange(P)
    c[:, C_IDENT:C_IDENT + P] = np.eye(P)
    half = ROPE // 2
    for m in range(P):
        first = m % ROPE < half
        c[m + half if first else m - half, C_ROT + m] = -1.0 if first else 1.0
    c[:, C_SLOT:C_SLOT + P] = part % CAP
    c[:, C_PSLOT] = part % CAP
    freq = np.float32(1.0) / np.float32(10000.0) ** (np.arange(0, ROPE, 2, dtype=np.float32) / np.float32(ROPE))
    c[:, C_PAIR + GROUP // 2:C_PAIR + GROUP] = 1.0
    c[:, C_FREQ] = freq[part % half]
    c[:, C_EPS6], c[:, C_EPS5] = EPS, 1e-5
    return c


def kernel(**inputs):
    import numpy as _np
    import concourse.bacc as _bacc
    from concourse import mybir as _mybir
    from concourse.bass_utils import run_bass_kernel_spmd as _run

    nc = _bacc.Bacc("TRN2", target_bir_lowering=False, num_devices=1)
    arrays, A = {}, {}
    for name, value in [*inputs.items(), ("const", constants())]:
        a = _np.ascontiguousarray(value)
        arrays[f"in_{name}"] = a
        A[name] = nc.dram_tensor(f"in_{name}", a.shape, _mybir.dt.from_np(a.dtype), kind="ExternalInput").ap()
    A["rope"] = nc.dram_tensor("rope_tables", (P, 2 * S), F32, kind="Internal").ap()
    A["out"] = nc.dram_tensor("out_0", (1, S, D), F32, kind="ExternalOutput").ap()
    program(nc, A)
    return _run(nc, [arrays], core_ids=[0]).results[0]["out_0"]
```

```python
import math
from contextlib import ExitStack

import concourse.bass as bass
from concourse import mybir

F32 = mybir.dt.float32
I32 = mybir.dt.int32
ALU = mybir.AluOpType
ACT = mybir.ActivationFunctionType
AX_X = mybir.AxisListType.X

P = 128
D = 1024
KT = D // P
S = 512
TT = S // P
DEPTH = 2
N_MOD = 6
HEADS, NOPE, ROPE, VD = 4, 128, 64, 128
QK = NOPE + ROPE
Q_RANK, KV_RANK = 256, 128
CONV_CH, TAPS = 512, 31
CT = CONV_CH // P
PAD = TAPS // 2
YW = S + 2 * PAD
EXPERTS, CAP = 16, 64
PAIRS = EXPERTS // 2
POOL_TAPS = {1: TAPS, 3: 6}
TAPS_A_TILE = 5
DVE_TAPS = (0, 11, 11, 9, 0, 10, 11, 10, 0)
HALF = 512
EPS = 1e-6
TABLES = 5 * TT * D + 2 * HEADS * QK + HEADS * (NOPE + VD)
QSCALE = 1.0 / math.sqrt(QK)
PI = 3.141592653589793
TWO_PI_A = 6.28125
TWO_PI_B = 0.0019350051879882812
TWO_PI_C = 2 * PI - TWO_PI_A - TWO_PI_B
ROUND = 1.5 * 2.0 ** 23

N1G, N2G, ADA, QLG, KVG, CB, CNG, CNB, QHG, KHG, QRG, KRG, NVEC = 0, 8, 16, 64, 66, 67, 71, 75, 79, 80, 81, 82, 83
SHIFT1, SCALE1, GATE1, SHIFT2, SCALE2, GATE2 = (m * KT for m in range(N_MOD))
C_IDENT, C_ROT, C_SLOT, C_PAIR, C_FREQ, C_PSLOT, C_EPS6, C_EPS5, C_ALL = 0, 128, 256, 384, 432, 433, 434, 435, 436
GROUP = 32
FR = mybir.dt.float32r


class Steps:

    def __init__(self, engine, semaphore):
        self.engine, self.semaphore, self.count = engine, semaphore, 0

    def __call__(self, instruction):
        self.count += 1
        instruction.then_inc(self.semaphore, 1)

    def settle(self):
        self.engine.wait_ge(self.semaphore, self.count)


def input_columns():
    first = Q_RANK + KV_RANK + ROPE
    return [c0 + c * P for c in range(CT) for c0 in (first + CONV_CH, first)] + [0, P, Q_RANK, Q_RANK + KV_RANK]


def input_weights(region, i):
    if i < 2 * CT:
        at = (i + 8) % 12 * KT * P
        return region[:, at:at + KT * P].rearrange("p (k n) -> p k n", k=KT)
    first = Q_RANK + KV_RANK + ROPE
    rest = region[:, TT * D:TT * D + KT * first].rearrange("p (k n) -> p k n", k=KT)
    c0 = input_columns()[i]
    return rest[:, :, c0:c0 + min(P, first - c0)]


ADA_PLACES = (0, 1, 2, 3, 0, 1, 2, 0, 1, 2, 0, 1)


def ada_place(M, i):
    region = M["h_tok"] if i == 3 else M["ring"][:, (3 + i) * TT * D:]
    return region[:, 0:TT * D].rearrange("p (k n) -> p k n", k=KT)


def ada_landed(c, n):
    place = ADA_PLACES[c]
    return 16 * ADA_PLACES.count(place) * n + 16 * (ADA_PLACES[:c].count(place) + 1)


def vector_rows(M):
    return (M["hy"][:, i * S:i * S + P] for i in (6, 7))


def load_rows(sp, A, M, n, ahead):
    rowsA, rowsB = vector_rows(M)

    def at(name):
        return A[name][bass.ds(n, 1)]

    row = 0
    for name, count in (("norm1_g", KT), ("norm2_g", KT), ("b_ada", N_MOD * KT), ("q_latent_g", 2), ("kv_latent_g", 1),
                        ("conv_b", CT), ("conv_norm_g", CT), ("conv_norm_b", CT)):
        sp.dma_start(rowsA[row:row + count, :], at(name).rearrange("a (k p) -> (a k) p", p=P)).then_inc(ahead["rows"], 16)
        row += count
    sp.dma_start(rowsA[QHG:QHG + 1, :], at("q_head_g")[:, 0:NOPE]).then_inc(ahead["rows"], 16)
    sp.dma_start(rowsA[KHG:KHG + 1, :], at("k_head_g")[:, 0:NOPE]).then_inc(ahead["rows"], 16)
    for r, name in ((QRG, "q_head_g"), (KRG, "k_head_g")):
        sp.dma_start(rowsA[r:r + 1, :].rearrange("p (a n) -> p a n", a=2),
                     at(name)[:, NOPE:QK].unsqueeze(1).to_broadcast([1, 2, ROPE])).then_inc(ahead["rows"], 16)
    sp.dma_start(rowsB[0:TAPS * CT, :], at("conv_w").rearrange("a t (c p) -> (a t c) p", p=P)).then_inc(ahead["rows"], 16)


def load_ada(sp, A, M, n, c, ahead):
    w_ada = A["w_ada"][bass.ds(n, 1)].rearrange("a (k p) n -> p (a k) n", p=P)
    sp.dma_start(ada_place(M, c), w_ada[:, :, HALF * c:HALF * (c + 1)]).then_inc(ahead["ada"][c], 16)


def load_input(sp, A, M, n, ahead):
    w = A["w_in"][bass.ds(n, 1)].rearrange("a (k p) n -> p (a k) n", p=P)
    for i, c0 in enumerate(input_columns()[0:4]):
        sp.dma_start(input_weights(M["ring"], i), w[:, :, c0:c0 + P]).then_inc(ahead["w_in"][i // 2], 16)


def prologue(nc, A, sem, M):
    ahead = dict(tables=sem("tables_out"), rows=sem("ahead_rows"), ada=[sem(f"ada_in{i}") for i in range(4)], w_in=[sem(f"ahead_w_in{i}") for i in range(2)])
    ps, const, xT = M["ps"], M["const"], M["xT"]
    ident = const[:, C_IDENT:C_IDENT + P]
    x_tok, scr = M["ring"][:, 0:TT * D].rearrange("p (t d) -> p t d", t=TT), M["scr"]
    c_rows, ones = M["one_hot_T"][:, 0:P], M["ones"]
    tables = M["ring"][:, TT * D + S:TT * D + 3 * S]
    cos, sin = tables[:, 0:S], tables[:, S:2 * S]
    pos_i = M["ring"][:, TT * D:TT * D + S].bitcast(I32)
    const_in, pos_in, c_in = (sem(n) for n in ("const_in", "pos_in", "c_in"))
    x_in = [sem(f"x_in{t}") for t in range(TT)]
    x_turned, c_turned, x_kept, c_act, ones_set = (
        sem(n) for n in ("x_turned", "c_turned", "x_kept", "c_act", "ones_set"))
    angle_ready, p_step, p_act = sem("angle_ready"), sem("p_step"), sem("p_act")
    with nc.Block() as block:
        @block.sync
        def _(sp):
            sp.dma_start(const[:], A["const"]).then_inc(const_in, 16)
            sp.dma_start(pos_i, A["positions"].to_broadcast([P, S])).then_inc(pos_in, 16)
            sp.dma_start(c_rows[0:KT, :], A["c"].rearrange("a (t p) -> (a t) p", p=P)).then_inc(c_in, 16)
            for t in range(TT):
                sp.dma_start(x_tok[:, t], A["x"][0, t * P:(t + 1) * P]).then_inc(x_in[t], 16)
            load_rows(sp, A, M, 0, ahead)
            for c in range(4):
                load_ada(sp, A, M, 0, c, ahead)
            load_input(sp, A, M, 0, ahead)
            sp.wait_ge(p_act, 2)
            sp.dma_start(A["rope"], tables).then_inc(ahead["tables"], 16)

        @block.tensor
        def _(pe):
            pe.wait_ge(const_in, 16)
            pe.wait_ge(c_in, 16)
            pe.transpose(ps[:, 7, 0:KT], c_rows[0:KT, :], ident[0:KT, 0:KT]).then_inc(c_turned, 1)
            for t in range(TT):
                pe.wait_ge(x_in[t], 16)
                for kt in range(KT):
                    if t == 0 and kt == 7:
                        pe.wait_ge(c_act, 1)
                    turn = pe.transpose(ps[:, kt, t * P:(t + 1) * P], x_tok[:, t, kt * P:(kt + 1) * P], ident)
                    if t == TT - 1:
                        turn.then_inc(x_turned, 1)

        @block.scalar
        def _(act):
            act.wait_ge(c_turned, 1)
            act.activation(M["c_col"][:], ps[:, 7, 0:KT], ACT.Silu).then_inc(c_act, 1)
            act.wait_ge(angle_ready, 1)
            act.activation(sin, sin, ACT.Sin).then_inc(p_act, 1)
            act.wait_ge(angle_ready, 2)
            act.activation(cos, cos, ACT.Sin).then_inc(p_act, 1)

        @block.vector
        def _(dve):
            step = Steps(dve, p_step)
            dve.memset(ones[:], 1.0).then_inc(ones_set, 1)
            ang, turns = scr[:, 1, :], scr[:, 2, :]
            dve.wait_ge(pos_in, 16)
            dve.wait_ge(const_in, 16)
            step(dve.tensor_copy(ang, pos_i))
            step.settle()
            step(dve.tensor_scalar(ang, ang, const[:, C_FREQ:C_FREQ + 1], None, ALU.mult))
            step.settle()
            step(dve.tensor_scalar(turns, ang, 1.0 / (2 * PI), ROUND, ALU.mult, ALU.add))
            step.settle()
            step(dve.tensor_scalar(turns, turns, ROUND, None, ALU.subtract))
            for part in (TWO_PI_A, TWO_PI_B, TWO_PI_C):
                step.settle()
                step(dve.scalar_tensor_tensor(ang, turns, -part, ang, ALU.mult, ALU.add))
            step.settle()
            dve.tensor_scalar(sin, ang, -3.1415925, 3.1415925, ALU.max, ALU.min).then_inc(angle_ready, 1)
            step(dve.tensor_scalar(turns, ang, -1.0, None, ALU.mult))
            step.settle()
            step(dve.tensor_tensor(turns, turns, ang, ALU.max))
            step.settle()
            dve.tensor_scalar(cos, turns, -1.0, PI / 2, ALU.mult, ALU.add).then_inc(angle_ready, 1)
            for kt in range(KT):
                dve.wait_ge(x_turned, kt + 1)
                dve.tensor_copy(xT[:, kt, :], ps[:, kt, :]).then_inc(x_kept, 1)

        @block.gpsimd
        def _(pool):
            pass
    return ahead


def layer(nc, A, sem, M, l, ahead):
    ps, const, xT, ring, scr = M["ps"], M["const"], M["xT"], M["ring"], M["scr"]
    ident, rot = const[:, C_IDENT:C_IDENT + P], const[:, C_ROT:C_ROT + P]
    eps = const[:, C_EPS6:C_EPS6 + 1]
    slot_row, slot_col = const[:, C_SLOT:C_SLOT + P], const[:, C_PSLOT:C_PSLOT + 1]
    ones = M["ones"]
    pair = const[:, C_PAIR:C_PAIR + 3 * GROUP // 2]
    cos, sin = ring[:, TABLES:TABLES + S], ring[:, TABLES + S:TABLES + 2 * S]
    hy, h_tok, one_hot_T = M["hy"], M["h_tok"], M["one_hot_T"]
    hT = hy[:, 0:KT * S].rearrange("p (k n) -> p k n", k=KT)
    mix = hT
    ye = hy[:, 0:D]
    rin = hy[:, KT * S:2 * KT * S].rearrange("p (k n) -> p k n", k=2 * HEADS)
    vec, convw, mod, smod = (M[n] for n in ("vec", "convw", "mod", "smod"))
    CHUNK = TT * D
    ada = [ada_place(M, i) for i in ADA_PLACES]
    ada_row = [one_hot_T[:, CHUNK + i * P:CHUNK + (i + 1) * P] for i in range(4)]
    c_rep = one_hot_T[:, CHUNK + 4 * P:CHUNK + 4 * P + KT * GROUP].rearrange("p (k n) -> p k n", k=KT)
    w_in_high = [M["one_hot_T_r"][:, i * KT * P:(i + 1) * KT * P].rearrange("p (k n) -> p k n", k=KT) for i in range(3)]
    h_low = M["hy_r"][:, 0:KT * S].rearrange("p (k n) -> p k n", k=KT)
    h_high = M["hy_r"][:, KT * S:2 * KT * S].rearrange("p (k n) -> p k n", k=KT)
    products = [one_hot_T[:, 3 * KT * P + i * S:3 * KT * P + (i + 1) * S] for i in range(2)] + [scr[:, 3, :]]
    first = Q_RANK + KV_RANK + ROPE
    in_cols = input_columns()
    IN_TILES = len(in_cols)
    w_in, w_in_low = ([input_weights(M[n], i) for i in range(IN_TILES)] for n in ("ring", "ring_r"))
    POOL_ADDS = sum(taps - 1 for taps in POOL_TAPS.values())
    w_out = ring[:, 3 * CHUNK:5 * CHUNK].rearrange("p (k n) -> p k n", k=KT)
    w_out_low = M["ring2_r"][:, 0:2 * CHUNK].rearrange("p (k n) -> p k n", k=KT)
    w_out_high = [M[n][:, a:a + CHUNK].rearrange("p (k n) -> p k n", k=4)[:, k, :] for n, a in (("ring2_r", 2 * CHUNK), ("one_hot_T_r", 0)) for k in range(4)]
    mix_low, mix_high = h_low, h_high
    MIX_ORDER = (0, 1, 2, 4, 5, 6, 7, 3)
    w_uq = ring[:, 5 * CHUNK:5 * CHUNK + 2 * HEADS * QK].rearrange("p (k n) -> p k n", k=2)
    w_ukv = ring[:, 5 * CHUNK + 2 * HEADS * QK:5 * CHUNK + 2 * HEADS * QK + HEADS * (NOPE + VD)]
    chunk = [ring[:, i * CHUNK:(i + 1) * CHUNK].rearrange("p (k n) -> p k n", k=4) for i in range(6)]
    early = [x[:, a:a + CHUNK].rearrange("p (k n) -> p k n", k=4) for x, a in ((hy, CHUNK), (one_hot_T, CHUNK), (one_hot_T, 0))]
    EARLY = len(early)
    def cut(region, at, n):
        return region[:, at * HALF:(at + n) * HALF].rearrange("p (k n) -> p k n", k=n)
    qn, qr, kn, kr = cut(ring, 0, 4), cut(ring, 4, 2), cut(ring, 6, 4), cut(ring, 10, 2)
    V, PT, prob = cut(ring, 12, 4), cut(ring, 16, 4), cut(ring, 20, 3)
    ypad = h_tok[:, 0:CT * YW].rearrange("p (c n) -> p c n", c=CT)
    w_r = h_tok[:, CT * YW:CT * YW + KT * GROUP].rearrange("p (k n) -> p k n", k=KT)
    cq = h_tok[:, 2560:2560 + 1024].rearrange("p (k n) -> p k n", k=2)
    ckv = h_tok[:, 3584:4096]
    sqs, acc, sig, krg = cut(one_hot_T, 0, 11), cut(one_hot_T, 11, 4), one_hot_T[:, 15 * HALF:16 * HALF], M["krg"]
    h_tok3 = h_tok[:].rearrange("p (t d) -> p t d", t=TT)
    ohT = M["hy_r"][:, 2 * D:2 * D + 2 * S].rearrange("p (e n) -> p e n", e=2)
    ye_hi, ye_lo = (M["one_hot_T_r"][:, EXPERTS * S // 2 + i * D:EXPERTS * S // 2 + (i + 1) * D] for i in range(2))
    SCATTER_BANKS = (1, 2, 0, 3, 5, 0, 3, 5)
    stat = M["stat"]
    mx, nmx, rsum, rrs, rqs, rqk = (stat[:, a:b] for a, b in ((0, 16), (16, 32), (32, 48), (48, 64), (64, 80), (80, 112)))
    root, head_rms, kd = M["krg"][:, 0:P], rin[:, 2, :], rin[:, 3, :]
    root2 = rin[:, 0, 0:2 * P]
    rowsA, rowsB = vector_rows(M)
    lg, aff, top8, rankT = (M[n] for n in ("lg", "aff", "top8", "rankT"))
    work, affT, rank = (hy[0:EXPERTS, i * S:(i + 1) * S] for i in range(3))
    lgT = scr[:, 0, 0:P]
    rankm = M["krg"][0:EXPERTS, :]
    sel_e, gcol = M["sel_e"], M["gcol"]
    x_e, sg, hid = scr[:, 0, :], scr[:, 1, :], scr[:, 2, :]
    x_rows = hy[:, D:D + S]
    hidT = sg
    s_e = scr[:, 3, :].rearrange("p (t n) -> p t n", t=TT)

    rowsT_done, vec_ready, ada_in = sem("rowsT_done"), sem("vec_ready"), ahead["ada"]
    c_spread, ada_used, ada_rows, ada_cols, mod_ready = (sem(n) for n in ("c_spread", "ada_used", "ada_rows", "ada_cols", "mod_ready"))
    w_in_in = {piece: sem(f"w_in_in{piece}") for piece in range(2, CT + 1)}
    uq_in, w_out_in, w_r_in = sem("uq_in"), sem("w_out_in"), sem("w_r_in")
    w_in_split, w_in_ready, h_split, h_low_ready, prod_ready, prod_used, w_out_split, w_out_ready, mix_split, mix_ready = (
        sem(n) for n in ("w_in_split", "w_in_ready", "h_split", "h_low_ready", "prod_ready", "prod_used", "w_out_split", "w_out_ready", "mix_split", "mix_ready"))
    n_sq, n_ss, n_root, n_inv, n_bc, n_xn, h_ready = (sem(n) for n in ("n_sq", "n_ss", "n_root", "n_inv", "n_bc", "n_xn", "h_ready"))
    pad_zero, proj, act_proj, dve_proj = (sem(n) for n in ("pad_zero", "proj", "act_proj", "dve_proj"))
    lat_sq, lat_ss, lat_root, lat_inv, lat_bc, lat_ready = (sem(n) for n in ("lat_sq", "lat_ss", "lat_root", "lat_inv", "lat_bc", "lat_ready"))
    qk_mm, qk_ev, rot_mm, roped, head_ss, head_root, head_cols, kd_ready, kb_mm, qk_ready = (
        sem(n) for n in ("qk_mm", "qk_ev", "rot_mm", "roped", "head_ss", "head_root", "head_cols", "kd_ready", "kb_mm", "qk_ready"))
    s_done, nm_ready, exp_done, prob_ready, t_done, pt_ev, pv_done, pv_ev = (
        sem(n) for n in ("s_done", "nm_ready", "exp_done", "prob_ready", "t_done", "pt_ev", "pv_done", "pv_ev"))
    conv_dve, cmean, cdev, csq, cvar, croot, cinv, cbc, cnorm, cmix = (
        sem(n) for n in ("conv_dve", "cmean", "cdev", "csq", "cvar", "croot", "cinv", "cbc", "cnorm", "cmix"))
    wout_done, x1_ready = sem("wout_done"), sem("x1_ready")
    r_mm, rT_kept, r_done, r_sub, r_exp, aff_ready, affT_done, htok_mm, htok_ev, rank_ready, rankT_done = (
        sem(n) for n in ("r_mm", "rT_kept", "r_done", "r_sub", "r_exp", "aff_ready", "affT_done", "htok_mm", "htok_ev", "rank_ready", "rankT_done"))
    chunk_in, early_in = [sem(f"chunk_in{i}") for i in range(6)], [sem(f"early_in{i}") for i in range(EARLY)]
    xe_kept, xeT_mm = sem("xe_kept"), sem("xeT_mm")
    chunk_used, s_built, xe_mm, xe_ready, st_mm, st_free, sg_ready, hid_ready, hidT_mm, hidT_ready, ye_free = (
        sem(n) for n in ("chunk_used", "s_built", "xe_mm", "xe_ready", "st_mm", "st_free", "sg_ready", "hid_ready", "hidT_mm", "hidT_ready", "ye_free"))
    ye_hi_ready, ye_lo_ready, out_done, x2_ready = (sem(n) for n in ("ye_hi_ready", "ye_lo_ready", "out_done", "x2_ready"))
    d_step = sem("d_step")

    def expert_chunk(e, j):
        if isinstance(e, int) and e == 0:
            return chunk[j], chunk_in[j], 16
        if isinstance(e, int) and e == 1 and j < EARLY:
            return early[j], early_in[j], 16
        slot = (j - EARLY) % 6
        return chunk[slot], chunk_in[slot], 16 * e if j < EARLY else 16 * e + 16

    def at(name):
        return A[name][bass.ds(l, 1)]

    with nc.Block() as block:
        @block.sync
        def _(sp):
            w_ada = at("w_ada").rearrange("a (k p) n -> p (a k) n", p=P)
            w = at("w_in").rearrange("a (k p) n -> p (a k) n", p=P)

            def ada_chunk(c):
                before = max(b for b in range(c) if ADA_PLACES[b] == ADA_PLACES[c])
                sp.wait_ge(ada_used, before + 1)
                sp.dma_start(ada[c], w_ada[:, :, HALF * c:HALF * (c + 1)]).then_inc(ada_in[ADA_PLACES[c]], 16)

            ada_chunk(4)
            for piece, then in ((2, (5, 6)), (3, (7,)), (CT, range(8, 12))):
                if piece < CT:
                    for i in (2 * piece, 2 * piece + 1):
                        sp.dma_start(w_in[i], w[:, :, in_cols[i]:in_cols[i] + P]).then_inc(w_in_in[piece], 16)
                else:
                    sp.wait_ge(ahead["tables"], 16)
                    sp.dma_start(ring[:, CHUNK:CHUNK + KT * first].rearrange("p (k n) -> p k n", k=KT), w[:, :, 0:first]).then_inc(w_in_in[piece], 16)
                for c in then:
                    ada_chunk(c)
            sp.wait_ge(ada_used, 12)
            sp.dma_start(w_uq, at("w_uq").rearrange("a (k p) n -> p (a k) n", p=P)).then_inc(uq_in, 16)
            sp.dma_start(w_ukv, at("w_ukv").rearrange("a p n -> p (a n)")).then_inc(uq_in, 16)
            sp.dma_start(ring[:, TABLES:TABLES + 2 * S], A["rope"]).then_inc(uq_in, 16)
            sp.dma_start(w_r[:, :, 0:EXPERTS], at("w_router").rearrange("a (k p) n -> p (a k) n", p=P)).then_inc(w_r_in, 16)
            w = at("w_out").rearrange("a (k p) n -> p (a k) n", p=P)
            for k in range(0, KT, 4):
                sp.dma_start(w_out[:, k:k + 4], w[:, k:k + 4]).then_inc(w_out_in, 16)

            def load(e, j):
                name, k = ("w_gate", "w_up", "w_down")[j // 2], 4 * (j % 2)
                w = A[name][bass.ds(l, 1), bass.ds(e, 1)].rearrange("a e (k p) n -> p (a e k) n", p=P)
                place, landed, _ = expert_chunk(e, j)
                sp.dma_start(place, w[:, k:k + 4]).then_inc(landed, 16)

            for j in range(6):
                if j in (0, 3):
                    sp.wait_ge(*((pv_done, HEADS) if j == 0 else (wout_done, KT)))
                load(0, j)
            for j in range(EARLY):
                load(1, j)
            for n in range(6):
                sp.wait_ge(chunk_used, n + 1)
                load(1 + (n + EARLY) // 6, (n + EARLY) % 6)

            with sp.If(l < DEPTH - 1):
                load_rows(sp, A, M, (l + 1) % DEPTH, ahead)

            def shifted(e, j):
                sp.wait_ge(chunk_used, 6 * e + (j - 5))
                load(e, j)

            for j in range(EARLY, 6):
                shifted(2, j)
            with sp.Fori(3, EXPERTS) as e:
                for j in range(6):
                    shifted(e, j)
            with sp.If(l < DEPTH - 1):
                after, used = (l + 1) % DEPTH, 6 * EXPERTS
                for c in range(3):
                    sp.wait_ge(chunk_used, used - (5 - c))
                    load_ada(sp, A, M, after, c, ahead)
                sp.wait_ge(xe_mm, EXPERTS)
                load_ada(sp, A, M, after, 3, ahead)
                sp.wait_ge(chunk_used, used)
                load_input(sp, A, M, after, ahead)

        @block.gpsimd
        def _(pool):
            pool.wait_ge(ada_used, 4)
            pool.memset(w_r[:, :, EXPERTS:GROUP], 0.0)
            pool.memset(ypad[:, :, 0:PAD], 0.0)
            pool.memset(ypad[:, :, PAD + S:YW], 0.0).then_inc(pad_zero, 1)
            n = 0
            for c, taps in POOL_TAPS.items():
                for t in range(1, taps):
                    pool.wait_ge(prod_ready, n + 1)
                    if n >= 1:
                        pool.wait_ge(prod_used, n)
                    pool.tensor_tensor(acc[:, c, :], acc[:, c, :], products[n % 3], ALU.add).then_inc(prod_used, 1)
                    n += 1
            for kt in range(KT):
                pool.wait_ge(w_out_split, kt + 1)
                pool.tensor_tensor(w_out_low[:, kt, :], w_out[:, kt, :], w_out_high[kt].bitcast(F32), ALU.subtract).then_inc(w_out_ready, 1)

            def outputs_rest(n, first):
                pool.wait_ge(ye_hi_ready, n + 1)
                if not first:
                    pool.wait_ge(out_done, KT * n)
                pool.tensor_tensor(ye_lo, ye, ye_hi.bitcast(F32), ALU.subtract).then_inc(ye_lo_ready, 1)

            outputs_rest(0, True)
            with pool.Fori(1, PAIRS) as n:
                outputs_rest(n, False)

        @block.tensor
        def _(pe):
            def grouped_sum(bank, col, x, start, stop):
                for g in range(TT):
                    mm = pe.matmul(ps[GROUP * g:GROUP * (g + 1), bank, col:col + P], ones[:, 0:GROUP], x[:, g * P:(g + 1) * P], start=start, stop=stop)
                return mm

            def broadcast(bank, x):
                for g in range(TT):
                    first = ident[:, GROUP * g:GROUP * g + 1].to_broadcast([P, P])
                    mm = pe.matmul(ps[:, bank, g * P:(g + 1) * P], first, x, start=True, stop=True)
                return mm

            def norm_sums(k):
                for kt in range(KT):
                    pe.wait_ge(n_sq, KT * k + kt + 1)
                    grouped_sum(6 - 6 * k, 0, scr[:, kt % 4, :], kt == 0, kt == KT - 1).then_inc(n_ss, 1)

            def norm_factor(k):
                pe.wait_ge(n_inv, k + 1)
                if k == 0:
                    pe.wait_ge(vec_ready, 2)
                broadcast(7 - 6 * k, root).then_inc(n_bc, 1)

            pe.wait_ge(ahead["rows"], 16 * 13 * (l + 1))
            pe.transpose(ps[:, 5, 0:NVEC], rowsA[0:NVEC, :], ident[0:NVEC, 0:NVEC]).then_inc(rowsT_done, 1)
            pe.transpose(ps[:, 7, 0:TAPS * CT], rowsB[0:TAPS * CT, :], ident[0:TAPS * CT, 0:TAPS * CT]).then_inc(rowsT_done, 1)

            def ada_chunk(c, bank):
                pe.wait_ge(ada_in[ADA_PLACES[c]], ada_landed(c, l))
                for kt in range(KT):
                    for g in range(4):
                        mm = pe.matmul(ps[GROUP * g:GROUP * (g + 1), bank, 0:P], c_rep[:, kt, :], ada[c][:, kt, g * P:(g + 1) * P],
                                       start=(kt == 0), stop=(kt == KT - 1))
                mm.then_inc(ada_used, 1)

            def ada_turn(c, bank):
                pe.wait_ge(ada_rows, c + 1)
                pe.transpose(ps[:, bank, (c % 4) * P:(c % 4 + 1) * P], ada_row[c % 4], ident).then_inc(ada_cols, 1)

            norm_sums(0)
            pe.wait_ge(c_spread, 1)
            ada_chunk(0, 0)
            norm_factor(0)
            for c in range(1, 4):
                ada_chunk(c, c)
            for c in range(4):
                ada_turn(c, 4)
            pe.wait_ge(vec_ready, 2)
            for i in range(IN_TILES):
                if i in (6, 8, 10):
                    pe.wait_ge(act_proj, (i - 6) // 2 + 1)
                if i in (7, 9, 11):
                    pe.wait_ge(dve_proj, (i - 7) // 2 + 1)
                pe.wait_ge(w_in_ready, i + 1)
                w_high = w_in_high[i % 3]
                w_low = w_in_low[i if i < IN_TILES - 1 else 2 * CT]
                for kt in range(KT):
                    if i == 0:
                        pe.wait_ge(h_low_ready, kt + 1)
                    pe.matmul(ps[:, i % 6, :], w_high[:, kt, :], h_high[:, kt, :], start=(kt == 0), stop=False)
                    pe.matmul(ps[:, i % 6, :], w_high[:, kt, :], h_low[:, kt, :], start=False, stop=False)
                    mm = pe.matmul(ps[:, i % 6, :], w_low[:, kt, :], h_high[:, kt, :], start=False, stop=(kt == KT - 1))
                mm.then_inc(proj, 1)
                c = 4 + i
                if 5 <= c <= 12:
                    if c == 5:
                        pe.wait_ge(n_xn, KT)
                    if c == 9:
                        pe.wait_ge(mod_ready, 2)
                    ada_turn(c - 1, 7)
                if c < 12:
                    ada_chunk(c, 6)
            pe.wait_ge(ada_rows, 12)
            for i in range(3):
                pe.wait_ge(lat_sq, i + 1)
                grouped_sum(6, P * (i // 2), scr[:, i, :], i != 1, i != 0).then_inc(lat_ss, 1)
            pe.wait_ge(mod_ready, 3)
            pe.wait_ge(lat_inv, 1)
            broadcast(7, root2[:, 0:P]).then_inc(lat_bc, 1)
            broadcast(6, root2[:, P:2 * P]).then_inc(lat_bc, 1)
            pe.wait_ge(uq_in, 48)
            pe.wait_ge(lat_ready, 3)
            for i in range(14):
                if i == 5:
                    pe.wait_ge(act_proj, 8)
                if i >= 6:
                    pe.wait_ge(qk_ev, i - 5)
                out = ps[:, i % 6, :]
                if i < 6:
                    for k in range(2):
                        go = dict(start=(k == 0), stop=(k == 1))
                        if i % 3 < 2:
                            h = 2 * (i // 3) + i % 3
                            mm = pe.matmul(out, w_uq[:, k, h * QK:h * QK + NOPE], cq[:, k, :], **go)
                        else:
                            for half in range(2):
                                h = 2 * (i // 3) + half
                                mm = pe.matmul(ps[ROPE * half:ROPE * (half + 1), i % 6, :], w_uq[:, k, h * QK + NOPE:(h + 1) * QK], cq[:, k, :], **go)
                elif i < 10:
                    h = i - 6
                    mm = pe.matmul(out, w_ukv[:, h * 2 * P:h * 2 * P + P], ckv, start=True, stop=True)
                else:
                    t = i - 10
                    mm = pe.matmul(out, ckv[:, t * P:(t + 1) * P], w_ukv.rearrange("p (h c) -> p h c", h=HEADS)[:, :, NOPE:NOPE + VD],
                                   start=True, stop=True)
                mm.then_inc(qk_mm, 1)
            for i in range(3):
                pe.wait_ge(qk_ev, 9 + i)
                pe.matmul(ps[:, 2 + i, :], rot, krg[:] if i == 0 else qr[:, i - 1, :], start=True, stop=True).then_inc(rot_mm, 1)
            query, key = pair[:, GROUP // 2:], pair[:, 0:GROUP]
            for n in range(4):
                for h in range(HEADS):
                    out, half = ps[GROUP * h:GROUP * (h + 1), 6, :], slice(ROPE * (h % 2), ROPE * (h % 2 + 1))
                    if n == 0:
                        pe.matmul(out, query, sqs[:, h, :], start=True, stop=False)
                    elif n == 1:
                        pe.matmul(out, key, sqs[:, 6 + h, :], start=False, stop=False)
                    elif n == 2:
                        pe.matmul(out, query[half, :], sqs[half, 4 + h // 2, :], start=False, stop=False)
                    else:
                        mm = pe.matmul(out, key[half, :], sqs[half, 10, :], start=False, stop=True)
            mm.then_inc(head_ss, 1)
            pe.wait_ge(head_root, 1)
            for t in range(TT):
                mm = pe.transpose(ps[:, 7, t * P:(t + 1) * P], head_rms[:, t * P:(t + 1) * P], ident)
            mm.then_inc(head_cols, 1)

            def key_factor(h):
                pe.wait_ge(kd_ready, h + 1)
                if h >= 1:
                    pe.wait_ge(qk_ready, h)
                pe.matmul(ps[:, 6, :], ones[:], kd, start=True, stop=True).then_inc(kb_mm, 1)

            key_factor(0)
            pe.wait_ge(qk_ev, 14)
            pe.wait_ge(prod_used, POOL_ADDS)
            pe.wait_ge(conv_dve, CT - 1)
            for c in range(CT):
                mm = pe.matmul(ps[:, 5, :], ones[:], acc[:, c, :], start=(c == 0), stop=(c == CT - 1))
            mm.then_inc(cmean, 1)
            pe.wait_ge(roped, 3)
            for i in range(4 * HEADS + 3):
                if i < 4 * HEADS:
                    h, q0 = i // TT, (i % TT) * P
                    pe.wait_ge(qk_ready, h + 1)
                    if i >= 3:
                        pe.wait_ge(exp_done, i - 2)
                    half = slice(ROPE * (h % 2), ROPE * (h % 2 + 1))
                    pe.matmul(ps[:, i % 3, :], qn[:, h, q0:q0 + P], kn[:, h, :], start=True, stop=False)
                    pe.matmul(ps[:, i % 3, :], qr[half, h // 2, q0:q0 + P], kr[half, h // 2, :], start=False, stop=True).then_inc(s_done, 1)
                    if i % TT == 1 and h + 1 < HEADS:
                        key_factor(h + 1)
                j = i - 2
                if 0 <= j < 4 * HEADS:
                    pe.wait_ge(prob_ready, j + 1)
                    if j >= 2:
                        pe.wait_ge(pt_ev, j - 1)
                    for kc in range(TT):
                        mm = pe.transpose(ps[:, 3 + j % 2, kc * P:(kc + 1) * P], prob[:, j % 3, kc * P:(kc + 1) * P], ident)
                    mm.then_inc(t_done, 1)
                if i >= 6 and i % TT == 2:
                    h = (i - 6) // TT
                    pe.wait_ge(pt_ev, TT * (h + 1))
                    if h == 0:
                        pe.wait_ge(cdev, CT)
                    if h >= 1:
                        pe.wait_ge(pv_ev, h)
                    for kc in range(TT):
                        mm = pe.matmul(ps[:, 5, :], V[:, kc, h * VD:(h + 1) * VD], PT[:, kc, :], start=(kc == 0), stop=(kc == TT - 1))
                    mm.then_inc(pv_done, 1)
                if i == 5:
                    pe.wait_ge(csq, CT)
                    for c in range(CT):
                        mm = grouped_sum(7, 0, scr[:, c, :], c == 0, c == CT - 1)
                    mm.then_inc(cvar, 1)
                if i == 8:
                    pe.wait_ge(cinv, 1)
                    broadcast(7, scr[:, 0, 0:P]).then_inc(cbc, 1)
            for dt in range(KT):
                tile = slice(dt * P, (dt + 1) * P)
                for n, kt in enumerate(MIX_ORDER):
                    if dt == 0:
                        pe.wait_ge(w_out_ready, kt + 1)
                        pe.wait_ge(mix_ready, n + 1)
                    pe.matmul(ps[:, dt, :], w_out_high[kt][:, tile], mix_high[:, kt, :], start=(n == 0), stop=False)
                    pe.matmul(ps[:, dt, :], w_out_high[kt][:, tile], mix_low[:, kt, :], start=False, stop=False)
                    mm = pe.matmul(ps[:, dt, :], w_out_low[:, kt, tile], mix_high[:, kt, :], start=False, stop=(n == KT - 1))
                mm.then_inc(wout_done, 1)
            norm_sums(1)
            norm_factor(1)
            pe.wait_ge(w_r_in, 16)
            pe.wait_ge(pad_zero, 1)
            for kt in range(KT):
                pe.wait_ge(h_ready, KT + kt + 1)
                for g in range(TT):
                    mm = pe.matmul(ps[GROUP * g:GROUP * (g + 1), 0, 0:P], w_r[:, kt, :], hT[:, kt, g * P:(g + 1) * P], start=(kt == 0), stop=(kt == KT - 1))
            mm.then_inc(r_mm, 1)
            pe.wait_ge(rT_kept, 1)
            pe.wait_ge(n_xn, 2 * KT)
            pe.transpose(ps[:, 1, 0:P], lgT, ident).then_inc(r_done, 1)
            for i in range(2 * TT):
                t, g = i // 2, i % 2
                if i >= 4:
                    pe.wait_ge(htok_ev, i - 3)
                for b in range(4):
                    kt = 4 * g + b
                    mm = pe.transpose(ps[:, 2 + i % 4, b * P:(b + 1) * P], hT[:, kt, t * P:(t + 1) * P], ident)
                mm.then_inc(htok_mm, 1)
            pe.wait_ge(aff_ready, 1)
            for t in range(TT):
                mm = pe.transpose(ps[0:EXPERTS, 6, t * P:(t + 1) * P], aff[:, t, :], ident)
            mm.then_inc(affT_done, 1)
            pe.wait_ge(rank_ready, 1)
            for t in range(TT):
                mm = pe.transpose(ps[:, 7, t * EXPERTS:(t + 1) * EXPERTS], rankm[:, t * P:(t + 1) * P], ident[0:EXPERTS, 0:EXPERTS])
            mm.then_inc(rankT_done, 1)
            pe.wait_ge(htok_ev, 2 * TT)

            def gather(e):
                pe.wait_ge(s_built, e + 1)
                for t in range(TT):
                    for half in range(2):
                        mm = pe.matmul(ps[CAP * half:CAP * (half + 1), 0, :], s_e[:, t, 0:CAP], h_tok3[:, t, half * HALF:(half + 1) * HALF], start=(t == 0), stop=(t == TT - 1))
                mm.then_inc(xe_mm, 1)

            def turn_tokens(e):
                pe.wait_ge(xe_kept, e + 1)
                for b in range(4):
                    mm = pe.transpose(ps[:, 5, b * P:(b + 1) * P], x_rows[:, b * P:(b + 1) * P], ident)
                mm.then_inc(xeT_mm, 1)

            def gates(e):
                pe.wait_ge(st_free, e + 1)
                for t in range(TT):
                    pe.matmul(ps[:, 7, 0:1], s_e[:, t, :], aff[:, t, bass.ds(e, 1)], start=(t == 0), stop=(t == TT - 1))
                pe.matmul(ps[:, 6, :], sel_e[:], rankm, start=True, stop=True).then_inc(st_mm, 1)

            def scatter(n):
                pe.wait_ge(ye_hi_ready, n + 1)
                for dt, bank in enumerate(SCATTER_BANKS):
                    tile = slice(dt * P, (dt + 1) * P)
                    if dt >= 5:
                        pe.wait_ge(x2_ready, KT * n + (dt - 2))
                    one_hot = ohT[:, bass.ds(n % 2, 1), :].rearrange("p a n -> p (a n)")
                    pe.matmul(ps[:, bank, :], ye_hi[:, tile], one_hot, start=True, stop=False)
                    if dt == 0:
                        pe.wait_ge(ye_lo_ready, n + 1)
                    pe.matmul(ps[:, bank, :], ye_lo[:, tile], one_hot, start=False, stop=True).then_inc(out_done, 1)

            def expert(e, last, scattered=None):
                pe.wait_ge(xe_ready, e + 1)
                if scattered is not None:
                    pe.wait_ge(x2_ready, KT * scattered + 2)
                for j in range(4):
                    weights, landed, count = expert_chunk(e, j)
                    pe.wait_ge(landed, count)
                    for k in range(4):
                        kt, at_x = 4 * (j % 2) + k, k * P + CAP * (j % 2)
                        for half in range(2):
                            mm = pe.matmul(ps[CAP * half:CAP * (half + 1), 1 + j // 2, :], x_e[:, at_x:at_x + CAP],
                                           weights[:, k, half * HALF:(half + 1) * HALF], start=(kt == 0), stop=(kt == KT - 1))
                    mm.then_inc(chunk_used, 1)
                if scattered is not None:
                    pe.wait_ge(x2_ready, KT * scattered + KT)
                if not last:
                    gather(e + 1)
                pe.wait_ge(hid_ready, e + 1)
                for b in range(4):
                    mm = pe.transpose(ps[:, 3, b * P:(b + 1) * P], hid[:, b * P:(b + 1) * P], ident)
                mm.then_inc(hidT_mm, 1)
                if not last:
                    gates(e + 1)
                    turn_tokens(e + 1)
                pe.wait_ge(hidT_ready, e + 1)
                pe.wait_ge(ye_free, e + 1)
                for j in range(4, 6):
                    weights, landed, count = expert_chunk(e, j)
                    pe.wait_ge(landed, count)
                    for k in range(4):
                        at_f = k * P + CAP * (j - 4)
                        for half in range(2):
                            mm = pe.matmul(ps[CAP * half:CAP * (half + 1), 4, :], hidT[:, at_f:at_f + CAP],
                                           weights[:, k, half * HALF:(half + 1) * HALF], start=(j == 4 and k == 0), stop=(j == 5 and k == 3))
                    mm.then_inc(chunk_used, 1)

            gather(0)
            gates(0)
            turn_tokens(0)
            for e in range(2):
                expert(e, False)
            with pe.Fori(1, PAIRS - 1) as n:
                expert(2 * n, False)
                pe.wait_ge(xe_ready, 2 * n + 2)
                scatter(n - 1)
                expert(2 * n + 1, False, n - 1)
            expert(EXPERTS - 2, False)
            pe.wait_ge(xe_ready, EXPERTS)
            scatter(PAIRS - 2)
            expert(EXPERTS - 1, True, PAIRS - 2)
            scatter(PAIRS - 1)

        @block.scalar
        def _(act):
            def norm(k, shift):
                for kt in range(KT):
                    if KT * k + kt >= 4:
                        act.wait_ge(n_ss, KT * k + kt - 3)
                    if k == 1:
                        act.wait_ge(x1_ready, kt + 1)
                    act.activation(scr[:, kt % 4, :], xT[:, kt, :], ACT.Square).then_inc(n_sq, 1)
                act.wait_ge(n_ss, KT * (k + 1))
                act.activation(root, ps[:, 6 - 6 * k, 0:P], ACT.Sqrt, bias=eps, scale=1.0 / D).then_inc(n_root, 1)

            def modulate(k, shift):
                for kt in range(KT):
                    act.wait_ge(n_xn, KT * k + kt + 1)
                    act.activation(hT[:, kt, :], hT[:, kt, :], ACT.Identity, bias=mod[:, shift + kt:shift + kt + 1],
                                   scale=smod[:, KT * k + kt:KT * k + kt + 1]).then_inc(h_ready, 1)
                    if k == 0:
                        act.wait_ge(h_ready, kt + 1)
                        act.activation(h_high[:, kt, :], hT[:, kt, :], ACT.Copy).then_inc(h_split, 1)

            norm(0, SHIFT1)

            def ada_kept(c, bank):
                act.wait_ge(ada_used, c + 1)
                if c >= 4:
                    act.wait_ge(ada_cols, c - 3)
                act.activation(ada_row[c % 4], ps[:, bank, 0:P], ACT.Copy).then_inc(ada_rows, 1)

            def w_in_split_tile(i):
                if i in (0, 2):
                    act.wait_ge(ahead["w_in"][i // 2], 32 * (l + 1))
                elif i % 2 == 0 and i <= 2 * CT:
                    act.wait_ge(w_in_in[i // 2], 32 if i < 2 * CT else 16)
                if i >= 3:
                    act.wait_ge(proj, i - 2)
                if i < IN_TILES - 1:
                    act.activation(w_in_high[i % 3], w_in[i], ACT.Copy).then_inc(w_in_split, 1)
                else:
                    act.activation(w_in_high[i % 3].rearrange("p k (a n) -> p k a n", a=2),
                                   w_in[i].unsqueeze(2).to_broadcast([P, KT, 2, ROPE]), ACT.Copy).then_inc(w_in_split, 1)

            def conv_products():
                n = 0
                for c, taps in POOL_TAPS.items():
                    for t in range(taps):
                        w, src = convw[:, t * CT + c:t * CT + c + 1], ypad[:, c, t:t + S]
                        if t == 0:
                            act.wait_ge(dve_proj, c + 1)
                            act.activation(acc[:, c, :], src, ACT.Identity, bias=vec[:, CB + c:CB + c + 1], scale=w)
                        else:
                            if n >= 3:
                                act.wait_ge(prod_used, n - 2)
                            act.activation(products[n % 3], src, ACT.Copy, scale=w).then_inc(prod_ready, 1)
                            n += 1
                        yield

            for c in range(3):
                ada_kept(c, c)
            for i in range(2):
                w_in_split_tile(i)
            ada_kept(3, 3)
            act.wait_ge(mod_ready, 1)
            modulate(0, SHIFT1)
            w_in_split_tile(2)
            conv = conv_products()
            for i in range(IN_TILES):
                act.wait_ge(proj, i + 1)
                bank = i % 6
                if i < 2 * CT:
                    if i % 2 == 0:
                        if i >= 2:
                            act.wait_ge(dve_proj, i // 2)
                        act.activation(sig, ps[:, bank, :], ACT.Sigmoid).then_inc(act_proj, 1)
                    ada_kept(4 + i, 6)
                elif i < 11:
                    n = i - 2 * CT
                    act.activation(scr[:, n, :], ps[:, bank, :], ACT.Square).then_inc(lat_sq, 1)
                    act.activation(cq[:, n, :] if n < 2 else ckv, ps[:, bank, :], ACT.Copy).then_inc(act_proj, 1)
                else:
                    act.activation(sqs[:, 10, :], ps[:, bank, :], ACT.Square)
                    act.activation(krg[:], ps[:, bank, :], ACT.Identity, scale=vec[:, KRG:KRG + 1]).then_inc(act_proj, 1)
                if i + 3 < IN_TILES:
                    w_in_split_tile(i + 3)
                for _ in range(TAPS_A_TILE if i >= 3 else 0):
                    next(conv, None)
            for i, width in enumerate((Q_RANK, KV_RANK)):
                act.wait_ge(lat_ss, 3)
                act.activation(root2[:, i * P:(i + 1) * P], ps[:, 6, i * P:(i + 1) * P], ACT.Sqrt, bias=eps, scale=1.0 / width).then_inc(lat_root, 1)
            for i in range(14):
                act.wait_ge(qk_mm, i + 1)
                src = ps[:, i % 6, :]
                if i == 6:
                    act.wait_ge(prod_used, POOL_ADDS)
                if i < 6 and i % 3 < 2:
                    h = 2 * (i // 3) + i % 3
                    act.activation(sqs[:, h, :], src, ACT.Square)
                    act.activation(qn[:, h, :], src, ACT.Identity, scale=vec[:, QHG:QHG + 1]).then_inc(qk_ev, 1)
                elif i < 6:
                    act.activation(sqs[:, 4 + i // 3, :], src, ACT.Square)
                    act.activation(qr[:, i // 3, :], src, ACT.Identity, scale=vec[:, QRG:QRG + 1]).then_inc(qk_ev, 1)
                elif i < 10:
                    act.activation(sqs[:, i, :], src, ACT.Square)
                    act.activation(kn[:, i - 6, :], src, ACT.Identity, scale=vec[:, KHG:KHG + 1]).then_inc(qk_ev, 1)
                else:
                    act.activation(V[:, i - 10, :], src, ACT.Copy).then_inc(qk_ev, 1)
            act.wait_ge(head_ss, 1)
            act.activation(head_rms, ps[:, 6, :], ACT.Sqrt, bias=eps, scale=1.0 / QK).then_inc(head_root, 1)
            for i in range(4 * HEADS + 4):
                if i < 4 * HEADS:
                    act.wait_ge(nm_ready, i + 1)
                    if i >= 3:
                        act.wait_ge(t_done, i - 2)
                    act.activation(prob[:, i % 3, :], ps[:, i % 3, :], ACT.Exp, bias=nmx[:, i:i + 1], scale=rqs[:, i:i + 1],
                                   accum_out=rsum[:, i:i + 1]).then_inc(exp_done, 1)
                j = i - 2
                if 0 <= j < 4 * HEADS:
                    act.wait_ge(t_done, j + 1)
                    if j >= TT and j % TT == 0:
                        act.wait_ge(pv_done, j // TT)
                    act.activation(PT[:, :, (j % TT) * P:(j % TT + 1) * P], ps[:, 3 + j % 2, :].rearrange("p (c n) -> p c n", c=TT), ACT.Copy).then_inc(pt_ev, 1)
                if 1 <= i <= CT:
                    act.wait_ge(cdev, i)
                    act.activation(scr[:, i - 1, :], acc[:, i - 1, :], ACT.Square).then_inc(csq, 1)
                if i == 6:
                    act.wait_ge(cvar, 1)
                    act.activation(scr[:, 0, 0:P], ps[:, 7, 0:P], ACT.Sqrt, bias=eps, scale=1.0 / CONV_CH).then_inc(croot, 1)
                if 3 <= i < 3 + KT:
                    kt = i - 3
                    act.wait_ge(w_out_in, 32)
                    act.wait_ge(roped, 3)
                    act.activation(w_out_high[kt], w_out[:, kt, :], ACT.Copy).then_inc(w_out_split, 1)
                if i == 4 * HEADS + 1:
                    for c in range(CT):
                        act.wait_ge(cnorm, c + 1)
                        act.activation(mix[:, HEADS + c, :], acc[:, c, :], ACT.Silu, bias=vec[:, CNB + c:CNB + c + 1], scale=vec[:, CNG + c:CNG + c + 1]).then_inc(cmix, 1)
                        act.wait_ge(cmix, c + 1)
                        act.activation(mix_high[:, HEADS + c, :], mix[:, HEADS + c, :], ACT.Copy).then_inc(mix_split, 1)
                if i >= 7 and i % TT == 3:
                    h = (i - 7) // TT
                    act.wait_ge(pv_done, h + 1)
                    act.activation(mix_high[:, h, :], ps[:, 5, :], ACT.Copy).then_inc(mix_split, 1)
                    act.activation(mix[:, h, :], ps[:, 5, :], ACT.Copy).then_inc(pv_ev, 1)
            norm(1, SHIFT2)
            modulate(1, SHIFT2)
            act.wait_ge(r_mm, 1)
            act.activation(lgT, ps[:, 0, 0:P], ACT.Copy).then_inc(rT_kept, 1)
            act.wait_ge(r_sub, 1)
            act.activation(lg[:], lg[:], ACT.Exp).then_inc(r_exp, 1)
            for i in range(2 * TT):
                act.wait_ge(htok_mm, i + 1)
                act.activation(h_tok3[:, i // 2, (i % 2) * HALF:(i % 2 + 1) * HALF], ps[:, 2 + i % 4, :], ACT.Copy).then_inc(htok_ev, 1)
            act.activation(stat[:, 0:1], stat[:, 0:1], ACT.Copy).then_inc(ye_free, 1)

            def gathered(e):
                act.wait_ge(xe_mm, e + 1)
                act.activation(x_rows, ps[:, 0, :], ACT.Copy).then_inc(xe_kept, 1)

            def tokens(e):
                act.wait_ge(xeT_mm, e + 1)
                act.activation(x_e, ps[:, 5, :], ACT.Copy).then_inc(xe_ready, 1)

            def pair_of_experts(n, first, last):
                for r in range(2):
                    act.wait_ge(chunk_used, 12 * n + (6 * r + 2))
                    act.activation(sg, ps[:, 1, :], ACT.Silu).then_inc(sg_ready, 1)
                    if not (last and r == 1):
                        gathered(2 * n + (r + 1))
                    act.wait_ge(hidT_mm, 2 * n + (r + 1))
                    act.activation(hidT, ps[:, 3, :], ACT.Copy).then_inc(hidT_ready, 1)
                    if not (last and r == 1):
                        tokens(2 * n + (r + 1))
                    act.wait_ge(chunk_used, 12 * n + (6 * r + 6))
                    act.wait_ge(st_free, 2 * n + (r + 2))
                    if r == 0 and not first:
                        act.wait_ge(ye_lo_ready, n)
                    out = ye[CAP * r:CAP * (r + 1), :]
                    for half in range(2):
                        rows = slice(CAP * half, CAP * (half + 1))
                        made = act.activation(out[:, half * HALF:(half + 1) * HALF], ps[rows, 4, :], ACT.Identity, scale=gcol[rows, :])
                    made.then_inc(ye_free, 1)
                act.wait_ge(ye_free, 2 * n + 3)
                act.activation(ye_hi, ye, ACT.Copy).then_inc(ye_hi_ready, 1)

            gathered(0)
            tokens(0)
            pair_of_experts(0, True, False)
            with act.Fori(1, PAIRS - 1) as n:
                pair_of_experts(n, False, False)
            pair_of_experts(PAIRS - 1, False, True)

        @block.vector
        def _(dve):
            step = Steps(dve, d_step)
            dve.wait_ge(rowsT_done, 1)
            dve.tensor_copy(vec[:], ps[:, 5, 0:NVEC]).then_inc(vec_ready, 1)
            dve.wait_ge(rowsT_done, 2)
            dve.tensor_copy(convw[:], ps[:, 7, 0:TAPS * CT]).then_inc(vec_ready, 1)

            dve.tensor_copy(c_rep, M["c_col"][:].unsqueeze(2).to_broadcast([P, KT, GROUP])).then_inc(c_spread, 1)

            def norm(k):
                dve.wait_ge(n_root, k + 1)
                dve.reciprocal(root, root).then_inc(n_inv, 1)
                dve.wait_ge(n_bc, k + 1)
                for kt in range(KT):
                    dve.tensor_tensor(hT[:, kt, :], xT[:, kt, :], ps[:, 7 - 6 * k, :], ALU.mult).then_inc(n_xn, 1)

            norm(0)
            dve.wait_ge(vec_ready, 2)

            def modulation(r):
                dve.wait_ge(ada_cols, 4 * r + 4)
                return dve.tensor_tensor(mod[:, 16 * r:16 * (r + 1)], ps[:, 4 if r == 0 else 7, :].rearrange("p (n k) -> p n k", k=GROUP)[:, :, 0],
                                         vec[:, ADA + 16 * r:ADA + 16 * (r + 1)], ALU.add)

            step(modulation(0))
            step.settle()
            dve.scalar_tensor_tensor(smod[:, 0:KT], mod[:, SCALE1:SCALE1 + KT], 1.0, vec[:, N1G:N1G + KT], ALU.add, ALU.mult).then_inc(mod_ready, 1)

            def convolve():
                for c in [c for c in range(CT) if c not in POOL_TAPS] + [c for c in POOL_TAPS if POOL_TAPS[c] < TAPS]:
                    for t in range(POOL_TAPS.get(c, 0), TAPS):
                        w, src = convw[:, t * CT + c:t * CT + c + 1], ypad[:, c, t:t + S]
                        if t == 0:
                            dve.wait_ge(dve_proj, c + 1)
                            step(dve.tensor_scalar(acc[:, c, :], src, w, vec[:, CB + c:CB + c + 1], ALU.mult, ALU.add))
                        else:
                            if c in POOL_TAPS:
                                dve.wait_ge(prod_used, POOL_ADDS)
                            step.settle()
                            op = dve.scalar_tensor_tensor(acc[:, c, :], src, w, acc[:, c, :], ALU.mult, ALU.add)
                            if t == TAPS - 1:
                                op.then_inc(conv_dve, 1)
                            else:
                                step(op)
                        yield

            def w_in_rest(i):
                dve.wait_ge(w_in_split, i + 1)
                high = w_in_high[i % 3].bitcast(F32)
                if i < IN_TILES - 1:
                    dve.tensor_tensor(w_in_low[i], w_in[i], high, ALU.subtract).then_inc(w_in_ready, 1)
                else:
                    dve.wait_ge(proj, 2 * CT + 1)
                    dve.tensor_tensor(w_in_low[2 * CT].rearrange("p k (a n) -> p k a n", a=2), w_in[i].unsqueeze(2).to_broadcast([P, KT, 2, ROPE]),
                                      high.rearrange("p k (a n) -> p k a n", a=2), ALU.subtract).then_inc(w_in_ready, 1)

            for i in range(2):
                w_in_rest(i)
            for kt in range(KT):
                dve.wait_ge(h_split, kt + 1)
                dve.tensor_tensor(h_low[:, kt, :], hT[:, kt, :], h_high[:, kt, :].bitcast(F32), ALU.subtract).then_inc(h_low_ready, 1)
            w_in_rest(2)
            dve.wait_ge(pad_zero, 1)
            conv = convolve()
            for i in range(IN_TILES - 3):
                if i == 4:
                    modulation(1).then_inc(mod_ready, 1)
                if i % 2 == 1 and i < 2 * CT:
                    c = i // 2
                    dve.wait_ge(act_proj, c + 1)
                    dve.wait_ge(proj, i + 1)
                    dve.tensor_tensor(ypad[:, c, PAD:PAD + S], ps[:, i % 6, :], sig, ALU.mult).then_inc(dve_proj, 1)
                w_in_rest(i + 3)
                for _ in range(DVE_TAPS[i]):
                    next(conv, None)
            step(modulation(2))
            step.settle()
            dve.scalar_tensor_tensor(smod[:, KT:2 * KT], mod[:, SCALE2:SCALE2 + KT], 1.0, vec[:, N2G:N2G + KT], ALU.add, ALU.mult).then_inc(mod_ready, 1)
            dve.wait_ge(lat_root, 2)
            dve.reciprocal(root2, root2).then_inc(lat_inv, 1)
            dve.wait_ge(act_proj, 7)
            dve.wait_ge(lat_bc, 2)
            for i in range(2):
                dve.scalar_tensor_tensor(cq[:, i, :], cq[:, i, :], vec[:, QLG + i:QLG + i + 1], ps[:, 7, :], ALU.mult, ALU.mult).then_inc(lat_ready, 1)
            dve.scalar_tensor_tensor(ckv, ckv, vec[:, KVG:KVG + 1], ps[:, 6, :], ALU.mult, ALU.mult).then_inc(lat_ready, 1)
            for _ in conv:
                pass
            dve.wait_ge(uq_in, 48)
            ropes = (krg[:], qr[:, 0, :], qr[:, 1, :])
            for i, x in enumerate(ropes):
                dve.wait_ge(rot_mm, i + 1)
                step(dve.tensor_tensor(rin[:, 6, :], ps[:, 2 + i, :], sin, ALU.mult))
                step(dve.tensor_tensor(x, x, cos, ALU.mult))
                step.settle()
                dve.tensor_tensor(x, x, rin[:, 6, :], ALU.add).then_inc(roped, 1)
                dve.wait_ge(roped, i + 1)
            dve.wait_ge(head_cols, 1)
            step(dve.reciprocal(rqk, ps[:, 7, :].rearrange("p (n k) -> p n k", k=GROUP // 2)[:, :, 0]))
            step.settle()
            factors = rqk.rearrange("p (t h k) -> p t h k", t=TT, h=HEADS)
            step(dve.tensor_scalar(rqs.rearrange("p (h t) -> p t h", h=HEADS), factors[:, :, :, 0], QSCALE, None, ALU.mult))

            def key_diag(h):
                dve.tensor_tensor(kd.rearrange("p (t n) -> p t n", t=TT), ident.unsqueeze(1).to_broadcast([P, TT, P]),
                                  factors[:, :, h, 1].unsqueeze(2).to_broadcast([P, TT, P]), ALU.mult).then_inc(kd_ready, 1)

            def key_norm(h):
                half = slice(ROPE * (h % 2), ROPE * (h % 2 + 1))
                dve.wait_ge(kb_mm, h + 1)
                dve.tensor_tensor(kn[:, h, :], kn[:, h, :], ps[:, 6, :], ALU.mult)
                dve.tensor_tensor(kr[half, h // 2, :], krg[half, :], ps[half, 6, :], ALU.mult).then_inc(qk_ready, 1)

            key_diag(0)
            key_norm(0)
            step.settle()
            def mix_rest(n):
                kt = MIX_ORDER[n]
                dve.wait_ge(mix_split, n + 1)
                if kt < HEADS:
                    dve.wait_ge(pv_ev, kt + 1)
                dve.tensor_tensor(mix_low[:, kt, :], mix[:, kt, :], mix_high[:, kt, :].bitcast(F32), ALU.subtract).then_inc(mix_ready, 1)

            for i in range(4 * HEADS + 1):
                if i < 4 * HEADS:
                    dve.wait_ge(s_done, i + 1)
                    step(dve.reduce_max(mx[:, i:i + 1], ps[:, i % 3, :], AX_X))
                    step.settle()
                    dve.tensor_scalar(nmx[:, i:i + 1], mx[:, i:i + 1], rqs[:, i:i + 1], -1.0, ALU.mult, ALU.mult).then_inc(nm_ready, 1)
                    if i // TT + 1 < HEADS:
                        if i % TT == 0:
                            key_diag(i // TT + 1)
                        if i % TT == 2:
                            key_norm(i // TT + 1)
                j = i - 1
                if j >= 0:
                    dve.wait_ge(exp_done, j + 1)
                    step(dve.reciprocal(rrs[:, j:j + 1], rsum[:, j:j + 1]))
                    step.settle()
                    dve.tensor_scalar(prob[:, j % 3, :], prob[:, j % 3, :], rrs[:, j:j + 1], None, ALU.mult).then_inc(prob_ready, 1)
                if i >= 8 and i % TT == 0:
                    mix_rest(i // TT - 2)
                if i < CT:
                    dve.wait_ge(cmean, 1)
                    dve.scalar_tensor_tensor(acc[:, i, :], ps[:, 5, :], -1.0 / CONV_CH, acc[:, i, :], ALU.mult, ALU.add).then_inc(cdev, 1)
                if i == 7:
                    dve.wait_ge(croot, 1)
                    dve.reciprocal(scr[:, 0, 0:P], scr[:, 0, 0:P]).then_inc(cinv, 1)
                if 9 <= i < 9 + CT:
                    dve.wait_ge(cbc, 1)
                    dve.wait_ge(csq, CT)
                    dve.tensor_tensor(acc[:, i - 9, :], acc[:, i - 9, :], ps[:, 7, :], ALU.mult).then_inc(cnorm, 1)
            for n in range(HEADS - 1, KT):
                mix_rest(n)
            for dt in range(KT):
                dve.wait_ge(wout_done, dt + 1)
                dve.scalar_tensor_tensor(xT[:, dt, :], ps[:, dt, :], mod[:, GATE1 + dt:GATE1 + dt + 1], xT[:, dt, :], ALU.mult, ALU.add).then_inc(x1_ready, 1)
            dve.wait_ge(x1_ready, KT)
            norm(1)
            dve.wait_ge(r_done, 1)
            logits = ps[:, 1, 0:P].rearrange("p (t e) -> p t e", t=TT)[:, :, 0:EXPERTS]
            step(dve.reduce_max(mx[:, 0:TT], logits, AX_X))
            step.settle()
            dve.tensor_tensor(lg[:], logits, mx[:, 0:TT].unsqueeze(2).to_broadcast([P, TT, EXPERTS]), ALU.subtract).then_inc(r_sub, 1)
            dve.wait_ge(r_exp, 1)
            step(dve.reduce_sum(rsum[:, 0:TT], lg[:], AX_X))
            step.settle()
            step(dve.reciprocal(rrs[:, 0:TT], rsum[:, 0:TT]))
            step.settle()
            dve.tensor_tensor(aff[:], lg[:], rrs[:, 0:TT].unsqueeze(2).to_broadcast([P, TT, EXPERTS]), ALU.mult).then_inc(aff_ready, 1)
            dve.wait_ge(affT_done, 1)
            step(dve.tensor_copy(work, ps[0:EXPERTS, 6, :]))
            for _ in range(CAP // 8):
                step.settle()
                step(dve.max(top8[:], work))
                step.settle()
                step(dve.match_replace(work, top8[:], work, -1.0))
            step.settle()
            step(dve.tensor_scalar(affT, work, 0.0, None, ALU.is_lt))
            step.settle()
            step(dve.tensor_tensor_scan(rank, affT, affT, 0.0, ALU.add, ALU.max))
            step.settle()
            step(dve.tensor_tensor(rank, rank, affT, ALU.mult))
            step.settle()
            dve.tensor_scalar(rankm, rank, -1.0, None, ALU.add).then_inc(rank_ready, 1)
            dve.wait_ge(rankT_done, 1)
            step(dve.tensor_copy(rankT[:].rearrange("p t e -> p (t e)"), ps[:, 7, 0:TT * EXPERTS]))
            step.settle()
            dve.memset(gcol[:], 0.0).then_inc(st_free, 1)

            def build(e):
                for t in range(TT):
                    dve.tensor_scalar(s_e[:, t, :], slot_row, rankT[:, t, bass.ds(e, 1)], None, ALU.is_equal)
                dve.tensor_scalar(sel_e[:], ones[0:EXPERTS, :], const[0:EXPERTS, bass.ds(e, 1)], None, ALU.mult).then_inc(s_built, 1)


            def add_pair(n):
                for dt, bank in enumerate(SCATTER_BANKS):
                    dve.wait_ge(out_done, KT * n + (dt + 1))
                    dve.scalar_tensor_tensor(xT[:, dt, :], ps[:, bank, :], mod[:, GATE2 + dt:GATE2 + dt + 1], xT[:, dt, :], ALU.mult, ALU.add).then_inc(x2_ready, 1)

            def pair_of_experts(n, first, last):
                for r in range(2):
                    dve.wait_ge(st_mm, 2 * n + (r + 1))
                    dve.wait_ge(ye_free, 2 * n + (r + 1))
                    dve.tensor_copy(gcol[:], ps[:, 7, 0:1])
                    rows = slice(CAP * r, CAP * (r + 1))
                    dve.tensor_scalar(ohT[rows, bass.ds(n % 2, 1), :].rearrange("p a n -> p (a n)"), ps[rows, 6, :], slot_col[rows, :], None, ALU.is_equal).then_inc(st_free, 1)
                    if not (last and r == 1):
                        build(2 * n + (r + 1))
                    dve.wait_ge(sg_ready, 2 * n + (r + 1))
                    dve.wait_ge(chunk_used, 12 * n + (6 * r + 4))
                    dve.tensor_tensor(hid, sg, ps[:, 2, :], ALU.mult).then_inc(hid_ready, 1)
                    if r == 0 and not first:
                        add_pair(n - 1)

            build(0)
            pair_of_experts(0, True, False)
            with dve.Fori(1, PAIRS - 1) as n:
                pair_of_experts(n, False, False)
            pair_of_experts(PAIRS - 1, False, True)
            add_pair(PAIRS - 1)


def memory(nc, ctx):
    M = dict(ps=ctx.enter_context(nc.psum_tensor("ps", [P, 8, 512], F32)))
    with nc.sbuf_tensor("xT_r", [P, KT, S], FR) as rounded:
        M["xT_r"] = rounded
    for name, shape in dict(xT=[P, KT, S], const=[P, C_ALL], ones=[P, P]).items():
        M[name] = ctx.enter_context(nc.sbuf_tensor(name, shape, F32))
    return M


def memory1(nc, ctx, M):
    M = dict(M)
    shared = dict(hy=[P, 2 * KT * S], h_tok=[P, TT * D], one_hot_T=[P, EXPERTS * S], ring=[P, 6 * TT * D])
    with ExitStack() as rounded:
        halves = dict(ring=[P, 3 * TT * D], ring2=[P, 3 * TT * D])
        for name, shape in {**shared, **halves}.items():
            M[name + "_r"] = rounded.enter_context(nc.sbuf_tensor(name + "_r", shape, FR))
    for name, shape in dict(
        **shared, scr=[P, 4, S],
        krg=[P, S], c_col=[P, KT], vec=[P, NVEC], convw=[P, TAPS * CT],
        mod=[P, N_MOD * KT], smod=[P, 2 * KT], stat=[P, 112],
        lg=[P, TT, EXPERTS], aff=[P, TT, EXPERTS], rankT=[P, TT, EXPERTS], top8=[EXPERTS, 8],
        sel_e=[EXPERTS, P], gcol=[P, 1],
    ).items():
        M[name] = ctx.enter_context(nc.sbuf_tensor(name, shape, F32))
    return M

MEM = 256
MT = MEM // P
GROUPS_A = 8
B_W, B_HEADS, TAPS_B = 1280, 10, 4
C_HEADS, C_DIM = 4, 256
A_W, C_W = 1024, C_HEADS * C_DIM
EXP_GROUPS, PER_GROUP, FF2 = 4, 4, 256
ALPHA = 2.0 ** 0.25
CSCALE = C_DIM ** -0.5
LRU_C = 8.0
Z_U, Z_V, Z_X, Z_G, Z_Q, Z_M = 0, A_W, 2 * A_W, 2 * A_W + B_W, 2 * A_W + 2 * B_W, 2 * A_W + 2 * B_W + C_W
SLOTS, SLOT = 4, KT * 2 * P
O_BANKS = (2, 3, 4, 5, 6, 7, 1, 0)
V_BANKS = (2, 3, 4, 5, 0, 1)
GROUP_CHUNKS = 3 * PER_GROUP
AHEAD = 2
LIFT = 2.0 ** 60
V_BIN, V_CB, V_BA, V_BX, V_LAM, NV1 = 0, 68, 78, 88, 98, 108
V_CW, V_BO, V_LIG, V_LIB, V_LMG, V_LMB, V_L1G, V_L1B, V_L2G, V_L2B, NV2 = (108 + n for n in (0, 40, 48, 56, 64, 72, 80, 88, 96, 104, 112))


def second(nc, A, sem, M):
    ps, const, xT, ones = M["ps"], M["const"], M["xT"], M["ones"]
    ident = const[:, C_IDENT:C_IDENT + P]
    eps = const[:, C_EPS5:C_EPS5 + 1]
    flat, u, v, ob, wT, vec, lru = (M[n] for n in ("tmp", "u", "v", "ob", "wT", "vec2", "lru"))
    tmp = flat[:, 0:10 * S].rearrange("p (k n) -> p k n", k=10)
    y, small = M["y"], M["small"]
    raw, w_low, w_high = ([M[name][:, i * SLOT:(i + 1) * SLOT] for i in range(SLOTS)] for name in ("raw", "raw_r", "w_high"))
    x_high, x_low = M["x_high"], M["xT_r"]
    act_high, u_low, ob_low, y_low, v_high = M["act_high"], M["u_r"], M["ob_r"], M["y_r"], M["v_r"]
    y_high = v_high[:].rearrange("p (k n) -> p k n", k=KT)
    ob_high = [act_high[:, k, :] for k in range(KT)] + [u_low[:, k, :] for k in range(B_HEADS - KT)]
    memT_high = act_high[:].rearrange("p k n -> p (k n)")[:, 0:KT * MEM].rearrange("p (k m) -> p k m", k=KT)
    memT_low = M["tmp_r"][:, 2048:2048 + KT * MEM].rearrange("p (k m) -> p k m", k=KT)
    rows1, rows2 = u[:, 0, 0:P], u[:, 1, 0:P]
    v3 = v[:].rearrange("p (t d) -> p t d", t=TT)
    wab = v[:, 0:2 * B_HEADS * P].rearrange("p (h n) -> p h n", h=2 * B_HEADS)
    row_in_y = y[:].rearrange("p k n -> p (k n)")
    bv_row, lvg_row, lvb_row, bs_row = (row_in_y[:, i * D:(i + 1) * D] for i in range(4))
    w_s = ob[:, 0:2, :].rearrange("p a n -> p (a n)").rearrange("p (g s) -> p g s", g=GROUPS_A)
    padded = S + TAPS_B - 1
    xpad = [flat[:, 8 * S + i * padded:8 * S + (i + 1) * padded] for i in range(2)]
    xc, gt = [tmp[:, i, :] for i in range(2)], [tmp[:, 2 + i, :] for i in range(2)]
    rr, ii, aa, th = (tmp[:, 4 + i, :] for i in range(4))
    gate_sg = [tmp[:, 8 + i, :] for i in range(2)]
    mem_tok = flat[:, 0:MT * D].rearrange("p (t d) -> p t d", t=MT)
    memT = flat[:, 2048:2048 + KT * MEM].rearrange("p (k m) -> p k m", k=KT)
    kT = v[:, 0:KT * MEM].rearrange("p (k m) -> p k m", k=KT)
    vm = v[:, 2048:2048 + MT * C_W].rearrange("p (t d) -> p t d", t=MT)
    prob = flat[:, 0:768].rearrange("p (i m) -> p i m", i=3)
    PT = flat[:, 768:1792].rearrange("p (c n) -> p c n", c=MT)
    diag = flat[:, 2048:2432].rearrange("p (i n) -> p i n", i=3)
    obf = ob[:].rearrange("p k n -> p (k n)")
    w_g = obf[:, 0:KT * 20].rearrange("p (k n) -> p k n", k=KT)
    bg_row = obf[:, 160:180]
    gl = obf[:, 256:256 + TT * 20].rearrange("p (t n) -> p t n", t=TT)
    gw = [obf[:, 512 + 64 * i:512 + 64 * (i + 1)].rearrange("p (t n) -> p t n", t=TT) for i in range(6)]
    gateT = obf[0:EXPERTS, 1024:1536]
    sel = obf[0:EXPERTS, 1536:2048].rearrange("p (j n) -> p j n", j=PER_GROUP)
    prio = small[:, 0:4]
    w_g_high, w_g_low = (M["ob_r"][:].rearrange("p k n -> p (k n)")[:, a:a + KT * 20].rearrange("p (k n) -> p k n", k=KT) for a in (2048, 2304))
    glT = obf[0:20, 2560:2560 + S]

    rows_in2, rows_turned, vec2_ready, bc_in, wab_in, ws_in, wg_in, mem_in = (
        sem(n) for n in ("rows_in2", "rows_turned", "vec2_ready", "bc_in", "wab_in", "ws_in", "wg_in", "mem_in"))
    slot_in = [sem(f"slot_in{i}") for i in range(SLOTS)]
    w_split, w_ready, x_split, x_ready, u_split, u_low_ready, ob_split, ob_low_ready, y_split, y_low_ready, x_whole = (
        sem(n) for n in ("w_split", "w_ready", "x_split", "x_ready", "u_split", "u_low_ready", "ob_split", "ob_low_ready", "y_split", "y_low_ready", "x_whole"))
    memT_split, memT_low_ready, hid_split, hid_low, wg_split, wg_ready, glT_kept = (
        sem(n) for n in ("memT_split", "memT_low_ready", "hid_split", "hid_low", "wg_split", "wg_ready", "glT_kept"))
    l_inv, l_bc = sem("l_inv"), sem("l_bc")
    l_sum, l_dev, l_sq, l_ss, l_root, l_norm, l_ready = (sem(n) for n in ("l_sum", "l_dev", "l_sq", "l_ss", "l_root", "l_norm", "l_ready"))
    bz_mm, bz_ev, xc_ready, bg_mm, bg_ev, at_ready, m2_ready, mult_ready, ob_ready, lru_ready, pads_zero = (
        sem(n) for n in ("bz_mm", "bz_ev", "xc_ready", "bg_mm", "bg_ev", "at_ready", "m2_ready", "mult_ready", "ob_ready", "lru_ready", "pads_zero"))
    lru_exp = sem("lru_exp")
    ws_turned, ws_kept, wT_ready = sem("ws_turned"), sem("ws_kept"), sem("wT_ready")
    v_mm, v_biased, v_gelu, v_var, v_root, v_ready, u_mm, u_ready, sp_mm, oa_ready = (
        sem(n) for n in ("v_mm", "v_biased", "v_gelu", "v_var", "v_root", "v_ready", "u_mm", "u_ready", "sp_mm", "oa_ready"))
    mz_mm, m_mm, m_sg, m_y = sem("mz_mm"), sem("m_mm"), sem("m_sg"), sem("m_y")
    mem_var, mem_root, mem_norm, memT_mm, memT_ready, kv_mm, kv_ready, q_mm, q_ready = (
        sem(n) for n in ("mem_var", "mem_root", "mem_norm", "memT_mm", "memT_ready", "kv_mm", "kv_ready", "q_mm", "q_ready"))
    cs_done, cnm_ready, cexp_done, cdiag_ready, ct_done, cpt_ev, cpv_done, oc_ready = (
        sem(n) for n in ("cs_done", "cnm_ready", "cexp_done", "cdiag_ready", "ct_done", "cpt_ev", "cpv_done", "oc_ready"))
    ax_ready, wo_mm, wo_used, gl_mm = sem("ax_ready"), sem("wo_mm"), sem("wo_used"), sem("gl_mm")
    g_mm, g_sub, g_exp, e_sub, e_exp, gate_ready, gate_turned, gateT_ready, prio_ready, f_init = (
        sem(n) for n in ("g_mm", "g_sub", "g_exp", "e_sub", "e_exp", "gate_ready", "gate_turned", "gateT_ready", "prio_ready", "f_init"))
    sel_ready, bc_mm, up_mm, sg2_ready, hid2_ready, dn_mm, dn_used = (
        sem(n) for n in ("sel_ready", "bc_mm", "up_mm", "sg2_ready", "hid2_ready", "dn_mm", "dn_used"))
    o_mm, o_first, o_second, stored, d2_step, a2_step, m_loop = (sem(n) for n in ("o_mm", "o_first", "o_second", "stored", "d2_step", "a2_step", "m_loop"))

    def cols(name, c0, n=2 * P):
        w = A[name][0].rearrange("(k p) n -> p k n", p=P)
        return w[:, :, c0:c0 + n]

    def two(name, c0, step, at):
        return cols(name, c0, 2 * step).rearrange("p k (a c) -> p k a c", a=2)[:, :, :, at:at + P]

    chunks, last_use = [], []

    def chunk(src, used, count):
        chunks.append(src)
        last_use.append((used, count))

    for h in range(B_HEADS):
        chunk(two("w_in_2", Z_X, B_W, h * P), bz_mm, 2 * h + 2)
    CH_V = len(chunks)
    for n in range(4):
        chunk(cols("w_in_2", Z_V + 2 * P * n), v_mm, TT * (n + 1))
    CH_U = len(chunks)
    for n in range(4):
        chunk(cols("w_in_2", Z_U + 2 * P * n), u_mm, 2 * n + 2)

    def dense(branch, name):
        first = len(chunks)
        for n in range(4):
            chunk(cols("w_in_2", Z_M + branch * D + 2 * P * n), mz_mm, KT * branch + 2 * n + 2)
            chunk(cols(name, 2 * P * n), m_mm, KT * branch + 2 * n + 2)
        return first

    CH_MA = dense(0, "p_a_2")
    CH_MB = len(chunks)
    for n in range(4):
        chunk(cols("w_in_2", Z_M + D + 2 * P * n), mz_mm, KT + 2 * n + 2)
        for dt in (2 * n, 2 * n + 1):
            chunk(cols("p_b_2", P * dt, P), m_mm, KT + dt + 1)
    CH_Q = len(chunks)
    for n in range(4):
        chunk(cols("w_in_2", Z_Q + 2 * P * n), q_mm, 2 * n + 2)
    CH_K = len(chunks)
    for n in range(8):
        chunk(cols("w_kv_2", 2 * P * n), kv_mm, 2 * n + 2)
    CH_MC = dense(2, "p_c_2")
    CH_O = len(chunks)
    for n in range(4):
        chunk(cols("w_o_2", 2 * P * n), wo_mm, 2 * n + 2)
    CH_E = len(chunks)

    def slot_of(tensors, i):
        src = chunks[i]
        k, n = src.shape[1], math.prod(src.shape[2:])
        return tensors[i % SLOTS][:, 0:k * n].rearrange("p (k n) -> p k n", k=k)

    def group_slot(tensors, n):
        return tensors[(CH_E + n) % SLOTS].rearrange("p (k n) -> p k n", k=KT)

    sizes = [16 * (2 if len(src.shape) == 4 else 1) for src in chunks]
    group_sizes = [32] * (2 * PER_GROUP) + [16] * PER_GROUP
    per_group = sum(group_sizes[0::SLOTS])

    def landed(i):
        return sum(sizes[i % SLOTS:i + 1:SLOTS])

    def group_landed(g, n):
        return per_group * g + (sum(sizes[(CH_E + n) % SLOTS::SLOTS]) + sum(group_sizes[n % SLOTS:n + 1:SLOTS]))

    with nc.Block() as block:
        @block.sync
        def _(sp):
            row = 0
            for name, n in (("b_in_2", 68), ("conv_b_2", 10), ("b_a_2", 10), ("b_x_2", 10), ("lam_2", 10)):
                sp.dma_start(rows1[row:row + n, :], A[name].rearrange("a (k p) -> (a k) p", p=P)).then_inc(rows_in2, 16)
                row += n
            sp.dma_start(rows2[0:40, :], A["conv_w_2"].rearrange("a t (c p) -> (a t c) p", p=P)).then_inc(rows_in2, 16)
            row = 40
            for name in ("b_o_2", "ln_in_g_2", "ln_in_b_2", "ln_mem_g_2", "ln_mem_b_2", "ln1_g_2", "ln1_b_2", "ln2_g_2", "ln2_b_2"):
                src = A[name] if len(A[name].shape) == 1 else A[name].rearrange("a d -> (a d)")
                sp.dma_start(rows2[row:row + KT, :], src.rearrange("(k p) -> k p", p=P)).then_inc(rows_in2, 16)
                row += KT
            for i, src in enumerate(chunks):
                if i >= SLOTS:
                    sp.wait_ge(*last_use[i - SLOTS])
                dst = slot_of(raw, i)
                if len(src.shape) == 3:
                    sp.dma_start(dst, src).then_inc(slot_in[i % SLOTS], 16)
                else:
                    for a in range(2):
                        sp.dma_start(dst[:, :, a * P:(a + 1) * P], src[:, :, a, :]).then_inc(slot_in[i % SLOTS], 16)

            def experts(g):
                for n in range(GROUP_CHUNKS):
                    if n < SLOTS and g is None:
                        sp.wait_ge(*last_use[CH_E + n - SLOTS])
                    elif n < SLOTS:
                        sp.wait_ge(dn_mm, 8 * g + (2 * n - 6))
                    elif n < 8 + SLOTS:
                        sp.wait_ge(up_mm, (0 if g is None else 16 * g) + 2 * (n - SLOTS) + 2)
                    e = (0 if g is None else PER_GROUP * g) + n // 2
                    dst, there = group_slot(raw, n), slot_in[(CH_E + n) % SLOTS]
                    if n < 8:
                        w = A["w_up_2"][0, bass.ds(e, 1)].rearrange("e (k p) n -> p (e k) n", p=P)
                        for a in range(2):
                            c0 = FF2 * a + P * (n % 2)
                            sp.dma_start(dst[:, :, a * P:(a + 1) * P], w[:, :, c0:c0 + P]).then_inc(there, 16)
                    else:
                        cs = slice(2 * P * (n - 8), 2 * P * (n - 7))
                        w = A["w_down_2"][0, bass.ds(0 if g is None else PER_GROUP * g, PER_GROUP), :, cs]
                        sp.dma_start(dst, w.rearrange("e (i p) n -> p (e i) n", p=P)).then_inc(there, 16)

            experts(None)
            with sp.Fori(1, EXP_GROUPS) as g:
                experts(g)
            out = A["out"][0].rearrange("(t p) d -> p t d", p=P)
            for n, kept in enumerate((o_first, o_second)):
                for t in range(TT):
                    sp.wait_ge(kept, t + 1)
                    sp.dma_start(out[:, t, n * HALF:(n + 1) * HALF], v3[:, t, n * HALF:(n + 1) * HALF]).then_inc(stored, 16)
            sp.wait_ge(stored, 2 * 16 * TT)

        @block.gpsimd
        def _(pool):
            for i in range(2):
                zero = pool.memset(xpad[i][:, 0:TAPS_B - 1], 0.0)
            zero.then_inc(pads_zero, 1)
            for n in range(4):
                last = pool.memset(prio[:, n:n + 1], float(4 - n))
            last.then_inc(prio_ready, 1)
            for dst, src in ((bv_row, A["b_in_2"][:, Z_V:Z_V + A_W]), (lvg_row, A["ln_v_g_2"]), (lvb_row, A["ln_v_b_2"]),
                             (bs_row, A["b_s_2"].rearrange("a g t -> a (g t)"))):
                pool.dma_start(dst, src.to_broadcast([P, D])).then_inc(bc_in, 16)
            def low(i, dst, src, high):
                pool.wait_ge(w_split, i + 1)
                pool.tensor_tensor(dst, src, high.bitcast(F32), ALU.subtract).then_inc(w_ready, 1)

            for i in range(CH_Q + SLOTS):
                low(i, slot_of(w_low, i), slot_of(raw, i), slot_of(w_high, i))
                if i == AHEAD:
                    pool.wait_ge(ws_kept, 2)
                    pool.affine_select(out=wT[:], in_=wT[:], compare_op=ALU.is_ge, fill=0.0, base=0, pattern=[[0, GROUPS_A], [1, P]], channel_multiplier=-1).then_inc(wT_ready, 1)
            pool.wait_ge(m_y, 2 * KT)
            pool.dma_start(w_g[:, :, 0:4], A["w_rg_2"][0].rearrange("(k p) n -> p k n", p=P)).then_inc(wg_in, 16)
            pool.dma_start(w_g[:, :, 4:20], A["w_re_2"][0].rearrange("(k p) n -> p k n", p=P)).then_inc(wg_in, 16)
            pool.dma_start(bg_row[:, 0:4], A["b_rg_2"].to_broadcast([P, 4])).then_inc(wg_in, 16)
            pool.dma_start(bg_row[:, 4:20], A["b_re_2"].to_broadcast([P, 16])).then_inc(wg_in, 16)
            for i in range(CH_Q + SLOTS, CH_E):
                low(i, slot_of(w_low, i), slot_of(raw, i), slot_of(w_high, i))
            with pool.Fori(0, EXP_GROUPS) as g:
                for n in range(GROUP_CHUNKS):
                    low(GROUP_CHUNKS * g + (CH_E + n), group_slot(w_low, n), group_slot(raw, n), group_slot(w_high, n))

        @block.tensor
        def _(pe):
            def passes(out, terms, ready=None):
                for n, (s_high, s_low, m_high, m_low) in enumerate(terms):
                    if ready is not None:
                        pe.wait_ge(ready[0], ready[1] + (n + 1))
                    pe.matmul(out, s_high, m_high, start=(n == 0), stop=False)
                    pe.matmul(out, s_high, m_low, start=False, stop=False)
                    mm = pe.matmul(out, s_low, m_high, start=False, stop=(n == len(terms) - 1))
                return mm

            def feature_tile(bank, i, n, high, low, ready=None):
                pe.wait_ge(w_ready, i + 1)
                h, l, tile = slot_of(w_high, i), slot_of(w_low, i), slice(n * P, (n + 1) * P)
                return passes(ps[:, bank, :], [(h[:, k, tile], l[:, k, tile], high[k], low[k]) for k in range(chunks[i].shape[1])], ready)

            def tiles(x):
                return [x[:, k, :] for k in range(x.shape[1])]

            def z_tile(bank, i, n, ready=None):
                return feature_tile(bank, i, n, tiles(x_high), tiles(x_low), ready)

            def turn_vectors():
                pe.wait_ge(rows_in2, 16 * 15)
                pe.transpose(ps[:, 6, 0:NV1], rows1[0:NV1, :], ident[0:NV1, 0:NV1]).then_inc(rows_turned, 1)
                pe.transpose(ps[:, 7, 0:NV2 - NV1], rows2[0:NV2 - NV1, :], ident[0:NV2 - NV1, 0:NV2 - NV1]).then_inc(rows_turned, 1)
            def norm_sum(x, kt):
                return pe.matmul(ps[:, 0, :], ones[:], x[:, kt, :], start=(kt == 0), stop=(kt == KT - 1))

            def layer_norm(k, x):
                for kt in range(KT):
                    pe.wait_ge(l_sq, KT * k + kt + 1)
                    for g in range(TT):
                        mm = pe.matmul(ps[GROUP * g:GROUP * (g + 1), 1, 0:P], ones[:, 0:GROUP], tmp[:, kt % 4, g * P:(g + 1) * P], start=(kt == 0), stop=(kt == KT - 1))
                    mm.then_inc(l_ss, 1)
                if k == 0:
                    turn_vectors()
                pe.wait_ge(l_inv, k + 1)
                pe.wait_ge(l_dev, KT * (k + 1))
                for g in range(TT):
                    first = ident[:, GROUP * g:GROUP * g + 1].to_broadcast([P, P])
                    mm = pe.matmul(ps[:, 0, g * P:(g + 1) * P], first, tmp[:, 4, 0:P], start=True, stop=True)
                mm.then_inc(l_bc, 1)

            for kt in range(KT):
                mm = norm_sum(xT, kt)
            mm.then_inc(l_sum, 1)
            layer_norm(0, xT)
            pe.wait_ge(vec2_ready, 2)
            pe.wait_ge(wab_in, 32)
            for h in range(B_HEADS + 1):
                if h < B_HEADS:
                    for part in range(2):
                        i = 2 * h + part
                        if i >= 4:
                            pe.wait_ge(bz_ev, i - 3)
                        z_tile(2 + i % 4, h, part, (x_ready, 0) if i == 0 else None).then_inc(bz_mm, 1)
                if h == 0:
                    pe.wait_ge(ws_in, 16)
                    for g in range(GROUPS_A):
                        mm = pe.transpose(ps[:, 6 + g // 4, (g % 4) * P:(g % 4 + 1) * P], w_s[:, g, :], ident)
                        if g % 4 == 3:
                            mm.then_inc(ws_turned, 1)
                if h == 1:
                    pe.wait_ge(ws_kept, 2)
                if h >= 1:
                    pe.wait_ge(xc_ready, h)
                    if h >= 2:
                        pe.wait_ge(bg_ev, h - 1)
                    pe.matmul(ps[:, 6, :], wab[:, h - 1, :], xc[(h - 1) % 2], start=True, stop=True)
                    pe.matmul(ps[:, 7, :], wab[:, B_HEADS + h - 1, :], xc[(h - 1) % 2], start=True, stop=True).then_inc(bg_mm, 1)
            pe.wait_ge(bz_ev, 2 * B_HEADS)
            for i in range(4 * TT):
                n, t = i // TT, i % TT
                pe.wait_ge(w_ready, CH_V + n + 1)
                if i >= len(V_BANKS):
                    pe.wait_ge(v_biased, i - len(V_BANKS) + 1)
                h, l, rows = slot_of(w_high, CH_V + n), slot_of(w_low, CH_V + n), slice(t * P, (t + 1) * P)
                passes(ps[:, V_BANKS[i % len(V_BANKS)], 0:2 * P], [(x_high[:, k, rows], x_low[:, k, rows], h[:, k, :], l[:, k, :]) for k in range(KT)]).then_inc(v_mm, 1)
            for i in range(KT):
                pe.wait_ge(v_biased, min(i + 13, 16))
                if i >= 4:
                    pe.wait_ge(u_ready, i - 3)
                z_tile(2 + i % 4, CH_U + i // 2, i % 2).then_inc(u_mm, 1)
            pe.wait_ge(wT_ready, 1)
            pe.wait_ge(v_ready, TT)
            pe.wait_ge(u_ready, KT)
            for g in range(GROUPS_A):
                if g >= 4:
                    pe.wait_ge(oa_ready, g - 3)
                for c in range(TT):
                    mm = pe.matmul(ps[:, 2 + g % 4, c * P:(c + 1) * P], v3[:, c, g * P:(g + 1) * P], wT[:, g, :], start=True, stop=True)
                mm.then_inc(sp_mm, 1)

            def merge_dense(branch, first, high, low):
                for dt in range(KT):
                    n, zc = KT * branch + dt, first + 2 * (dt // 2)
                    a = 2 + 2 * (n % 2)
                    if n >= 2:
                        pe.wait_ge(m_y, n - 1)
                    z_tile(a, zc, dt % 2).then_inc(mz_mm, 1)
                    pe.wait_ge(u_low_ready, KT * (branch // 2 + 1))
                    feature_tile(a + 1, zc + 1, dt % 2, high, low).then_inc(m_mm, 1)

            pe.wait_ge(oa_ready, 5)
            merge_dense(0, CH_MA, tiles(act_high), tiles(u_low))
            for dt in range(KT):
                n, zc = KT + dt, CH_MB + 3 * (dt // 2)
                a = 2 + 2 * (n % 2)
                pe.wait_ge(m_y, n - 1)
                z_tile(a, zc, dt % 2).then_inc(mz_mm, 1)
                pe.wait_ge(ob_low_ready, B_HEADS)
                feature_tile(a + 1, zc + 1 + dt % 2, 0, ob_high, tiles(ob_low)).then_inc(m_mm, 1)
            for kt in range(KT):
                if kt < MT:
                    pe.wait_ge(mem_norm, MT)
                if kt >= 2:
                    pe.wait_ge(memT_ready, kt - 1)
                for t in range(MT):
                    mm = pe.transpose(ps[:, 6 + kt % 2, t * P:(t + 1) * P], mem_tok[:, t, kt * P:(kt + 1) * P], ident)
                mm.then_inc(memT_mm, 1)
            pe.wait_ge(m_y, 2 * KT)
            for i in range(KT):
                if i >= 4:
                    pe.wait_ge(q_ready, i - 3)
                z_tile(2 + i % 4, CH_Q + i // 2, i % 2).then_inc(q_mm, 1)
            pe.wait_ge(memT_low_ready, KT)
            for i in range(KT + 4 * MT):
                if i >= 2:
                    pe.wait_ge(kv_ready, i - 1)
                bank = 6 + i % 2
                if i < KT:
                    c, tile = CH_K + i // 2, slice((i % 2) * P, (i % 2 + 1) * P)
                    pe.wait_ge(w_ready, c + 1)
                    h, l = slot_of(w_high, c), slot_of(w_low, c)
                    mm = passes(ps[:, bank, 0:MEM], [(h[:, k, tile], l[:, k, tile], memT_high[:, k, :], memT_low[:, k, :]) for k in range(KT)])
                else:
                    c, t = CH_K + 4 + (i - KT) // MT, (i - KT) % MT
                    pe.wait_ge(w_ready, c + 1)
                    h, l, rows = slot_of(w_high, c), slot_of(w_low, c), slice(t * P, (t + 1) * P)
                    mm = passes(ps[:, bank, 0:2 * P], [(memT_high[:, k, rows], memT_low[:, k, rows], h[:, k, :], l[:, k, :]) for k in range(KT)])
                mm.then_inc(kv_mm, 1)
            pe.wait_ge(q_ready, KT)
            pe.wait_ge(kv_ready, KT + 4 * MT)
            N = C_HEADS * TT
            for i in range(N + 3):
                if i < N:
                    h, q0 = i // TT, (i % TT) * P
                    if i >= 3:
                        pe.wait_ge(cexp_done, i - 2)
                    for k in range(2):
                        mm = pe.matmul(ps[:, i % 3, 0:MEM], u[:, 2 * h + k, q0:q0 + P], kT[:, 2 * h + k, :], start=(k == 0), stop=(k == 1))
                    mm.then_inc(cs_done, 1)
                j = i - 2
                if 0 <= j < N:
                    pe.wait_ge(cdiag_ready, j + 1)
                    if j >= 2:
                        pe.wait_ge(cpt_ev, j - 1)
                    for c in range(MT):
                        mm = pe.matmul(ps[:, 3 + j % 2, c * P:(c + 1) * P], prob[:, j % 3, c * P:(c + 1) * P], diag[:, j % 3, :], start=True, stop=True)
                    mm.then_inc(ct_done, 1)
                if i >= 6 and i % TT == 2:
                    h = (i - 6) // TT
                    pe.wait_ge(cpt_ev, TT * (h + 1))
                    if h >= 1:
                        pe.wait_ge(oc_ready, h)
                    for d in range(2):
                        for c in range(MT):
                            mm = pe.matmul(ps[:, 5 + d, :], vm[:, c, h * C_DIM + d * P:h * C_DIM + (d + 1) * P], PT[:, c, :], start=(c == 0), stop=(c == MT - 1))
                    mm.then_inc(cpv_done, 1)
            merge_dense(2, CH_MC, tiles(act_high), tiles(u_low))
            pe.wait_ge(m_y, 3 * KT)
            for dt in range(KT + 2):
                if dt < KT:
                    if dt >= 4:
                        pe.wait_ge(wo_used, dt - 3)
                    feature_tile(2 + dt % 4, CH_O + dt // 2, dt % 2, tiles(y_high), tiles(y_low), (y_low_ready, 0) if dt == 0 else None).then_inc(wo_mm, 1)
                if dt >= 2:
                    pe.wait_ge(wo_used, dt - 1)
                    mm = norm_sum(xT, dt - 2)
            mm.then_inc(l_sum, 1)
            layer_norm(1, xT)
            pe.wait_ge(wg_ready, 1)
            passes(ps[0:20, 6, :], [(w_g_high[:, k, :], w_g_low[:, k, :], x_high[:, k, :], x_low[:, k, :]) for k in range(KT)], (x_ready, KT)).then_inc(gl_mm, 1)
            pe.wait_ge(glT_kept, 1)
            for t in range(TT):
                mm = pe.transpose(ps[:, 7, t * 20:(t + 1) * 20], glT[:, t * P:(t + 1) * P], ident[0:20, 0:20])
            mm.then_inc(g_mm, 1)

            def up(g, n):
                i = n % 2
                pe.wait_ge(w_ready, GROUP_CHUNKS * g + (CH_E + n + 1))
                if n >= 2:
                    pe.wait_ge(hid2_ready, 8 * g + n)
                h, l = group_slot(w_high, n), group_slot(w_low, n)
                for part in range(2):
                    tile = slice(part * P, (part + 1) * P)
                    passes(ps[:, 2 * i + part, :], [(h[:, k, tile], l[:, k, tile], x_high[:, k, :], x_low[:, k, :]) for k in range(KT)]).then_inc(up_mm, 1)

            up(0, 0)
            pe.wait_ge(gate_ready, 1)
            for t in range(TT):
                mm = pe.transpose(ps[0:EXPERTS, 6, t * P:(t + 1) * P], gw[0][:, t, :], ident)
            mm.then_inc(gate_turned, 1)
            pe.wait_ge(gateT_ready, 1)

            def group(g, last):
                pe.wait_ge(sel_ready, g + 1)
                for n in range(2 * PER_GROUP):
                    j = n // 2
                    if n % 2 == 0:
                        pe.wait_ge(hid2_ready, 8 * g + max(1, 2 * j - 1))
                        pe.matmul(ps[:, 4 + j % 2, :], sel[:, j, :], gateT, start=True, stop=True).then_inc(bc_mm, 1)
                    if n >= 1:
                        up(g, n)
                for dt in range(KT):
                    pe.wait_ge(w_ready, GROUP_CHUNKS * g + (CH_E + 8 + dt // 2 + 1))
                    pe.wait_ge(dn_used, 8 * g + (dt + 1))
                    h, l, tile = group_slot(w_high, 8 + dt // 2), group_slot(w_low, 8 + dt // 2), slice((dt % 2) * P, (dt % 2 + 1) * P)
                    passes(ps[:, 6 + dt % 2, :], [(h[:, k, tile], l[:, k, tile], act_high[:, k, :], u_low[:, k, :]) for k in range(KT)],
                           (hid_low, 8 * g) if dt == 0 else None).then_inc(dn_mm, 1)
                    if last and dt >= 2:
                        pe.wait_ge(dn_used, 8 * g + (dt + 1))
                        norm_sum(y, dt - 2)
                if not last:
                    up(g + 1, 0)

            with pe.Fori(0, EXP_GROUPS - 1) as g:
                group(g, False)
            group(EXP_GROUPS - 1, True)
            pe.wait_ge(dn_used, 8 * EXP_GROUPS + 2)
            for kt in (KT - 2, KT - 1):
                mm = norm_sum(y, kt)
            mm.then_inc(l_sum, 1)
            layer_norm(2, y)
            for i in range(2 * TT):
                n, t = i // TT, i % TT
                pe.wait_ge(l_ready, 2 * KT + 4 * (n + 1))
                for b in range(4):
                    mm = pe.transpose(ps[:, O_BANKS[i], b * P:(b + 1) * P], y[:, 4 * n + b, t * P:(t + 1) * P], ident)
                mm.then_inc(o_mm, 1)

        @block.scalar
        def _(act):
            step = Steps(act, a2_step)
            act.dma_start(w_s, A["w_s_2"][0].rearrange("g t s -> t g s")).then_inc(ws_in, 16)
            act.dma_start(wab[:, 0:B_HEADS], A["w_a_2"][0].rearrange("h i j -> i h j")).then_inc(wab_in, 16)
            act.dma_start(wab[:, B_HEADS:], A["w_x_2"][0].rearrange("h i j -> i h j")).then_inc(wab_in, 16)

            def col(n):
                return vec[:, n:n + 1]

            split = [0]

            def ahead(i):
                while split[0] <= min(i + AHEAD, CH_E - 1):
                    n = split[0]
                    act.wait_ge(slot_in[n % SLOTS], landed(n))
                    act.activation(slot_of(w_high, n), slot_of(raw, n), ACT.Copy).then_inc(w_split, 1)
                    split[0] += 1

            def group_split(g, n):
                act.wait_ge(slot_in[(CH_E + n) % SLOTS], group_landed(g, n))
                act.activation(group_slot(w_high, n), group_slot(raw, n), ACT.Copy).then_inc(w_split, 1)

            def layer_norm(k, x, gain, bias, last=None):
                for kt in range(KT):
                    act.wait_ge(l_dev, KT * k + kt + 1)
                    if kt >= 4:
                        act.wait_ge(l_ss, KT * k + kt - 3)
                    act.activation(tmp[:, kt % 4, :], x[:, kt, :], ACT.Square).then_inc(l_sq, 1)
                if k == 0:
                    ahead(-AHEAD)
                act.wait_ge(l_ss, KT * (k + 1))
                act.activation(tmp[:, 4, 0:P], ps[:, 1, 0:P], ACT.Sqrt, bias=eps, scale=1.0 / D).then_inc(l_root, 1)
                if k == 0:
                    ahead(1 - AHEAD)
                    act.wait_ge(vec2_ready, 2)
                for kt in range(KT):
                    act.wait_ge(l_norm, KT * k + kt + 1)
                    act.activation(x[:, kt, :], x[:, kt, :], ACT.Identity, bias=col(bias + kt), scale=col(gain + kt)).then_inc(l_ready, 1)
                    if k < 2:
                        act.wait_ge(l_ready, KT * k + kt + 1)
                        act.activation(x_high[:, kt, :], x[:, kt, :], ACT.Copy).then_inc(x_split, 1)

            layer_norm(0, xT, V_LIG, V_LIB)
            act.wait_ge(lru_ready, 1)
            act.activation(lru[:, 1, :], lru[:, 0, :], ACT.Exp, scale=-1.0).then_inc(lru_exp, 1)
            act.wait_ge(pads_zero, 1)
            for h in range(B_HEADS + 1):
                if h < B_HEADS:
                    ahead(h)
                    act.wait_ge(bz_mm, 2 * h + 1)
                    if h >= 2:
                        act.wait_ge(xc_ready, h - 1)
                    act.activation(xpad[h % 2][:, TAPS_B - 1:], ps[:, 2 + (2 * h) % 4, :], ACT.Identity, bias=col(V_BIN + Z_X // P + h)).then_inc(bz_ev, 1)
                    act.wait_ge(bz_mm, 2 * h + 2)
                    if h >= 2:
                        act.wait_ge(ob_ready, h - 1)
                    act.activation(gt[h % 2], ps[:, 2 + (2 * h + 1) % 4, :], ACT.Gelu_apprx_tanh, bias=col(V_BIN + Z_G // P + h)).then_inc(bz_ev, 1)
                if h == 0:
                    for i in range(2):
                        act.wait_ge(ws_turned, i + 1)
                        act.activation(wT[:, 4 * i:4 * i + 4, :], ps[:, 6 + i, :].rearrange("p (g t) -> p g t", g=4), ACT.Copy).then_inc(ws_kept, 1)
                if h >= 1:
                    k = h - 1
                    act.wait_ge(bg_mm, k + 1)
                    if k >= 1:
                        act.wait_ge(ob_ready, k)
                    step(act.activation(rr, ps[:, 6, :], ACT.Sigmoid, bias=col(V_BA + k)))
                    act.activation(ii, ps[:, 7, :], ACT.Sigmoid, bias=col(V_BX + k)).then_inc(bg_ev, 1)
                    step.settle()
                    act.wait_ge(lru_ready, 2)
                    act.activation(aa, rr, ACT.Exp, scale=lru[:, 2, k:k + 1])
                    act.activation(th, rr, ACT.Tanh, scale=lru[:, 3, k:k + 1]).then_inc(at_ready, 1)
                    act.wait_ge(m2_ready, k + 1)
                    act.activation(th, rr, ACT.Sqrt, scale=LIFT).then_inc(mult_ready, 1)
            for i in range(4 * TT):
                n, t = i // TT, i % TT
                ahead(CH_V + n)
                act.wait_ge(v_biased, i + 1)
                part = v3[:, t, n * 2 * P:(n + 1) * 2 * P]
                act.activation(part, part, ACT.Gelu_apprx_tanh).then_inc(v_gelu, 1)
            for i in range(KT):
                ahead(CH_U + i // 2)
                if i == 1:
                    act.wait_ge(v_var, TT)
                    act.activation(small[:, 16:20], small[:, 8:16].rearrange("p (t s) -> p t s", s=2)[:, :, 1], ACT.Sqrt, bias=eps).then_inc(v_root, 1)
                act.wait_ge(u_mm, i + 1)
                act.activation(u[:, i, :], ps[:, 2 + i % 4, :], ACT.Gelu_apprx_tanh, bias=col(V_BIN + i)).then_inc(u_ready, 1)

            def merge(branch, first, per):
                for dt in range(KT):
                    n = KT * branch + dt
                    ahead(first + per * (dt // 2) + (per - 2) * (dt % 2) + 1)
                    if n == KT + 2:
                        act.wait_ge(mem_var, MT)
                        act.activation(small[:, 16:18], small[:, 8:12].rearrange("p (t s) -> p t s", s=2)[:, :, 1], ACT.Sqrt, bias=eps).then_inc(mem_root, 1)
                    act.wait_ge(mz_mm, n + 1)
                    if n >= 2:
                        act.wait_ge(m_y, n - 1)
                    act.activation(gate_sg[n % 2], ps[:, 2 + 2 * (n % 2), :], ACT.Sigmoid, bias=col(V_BIN + Z_M // P + n)).then_inc(m_sg, 1)
                    if branch == 2 and dt >= 2:
                        whole_split(dt - 2)
            def whole_split(kt):
                act.wait_ge(m_y, 2 * KT + kt + 1)
                act.activation(y_high[:, kt, :], y[:, kt, :], ACT.Copy).then_inc(y_split, 1)

            for g in range(GROUPS_A):
                act.wait_ge(oa_ready, g + 1)
                act.activation(act_high[:, g, :], u[:, g, :], ACT.Copy).then_inc(u_split, 1)
            merge(0, CH_MA, 2)
            act.wait_ge(ob_ready, B_HEADS)
            act.wait_ge(m_mm, KT)
            for h in range(B_HEADS):
                act.activation(ob_high[h], ob[:, h, :], ACT.Copy).then_inc(ob_split, 1)
            act.dma_start(mem_tok, A["mem_2"][0].rearrange("(t p) d -> p t d", p=P)).then_inc(mem_in, 16)
            merge(1, CH_MB, 3)
            for kt in range(KT):
                act.wait_ge(memT_mm, kt + 1)
                act.activation(memT[:, kt, :], ps[:, 6 + kt % 2, 0:MEM], ACT.Identity, bias=col(V_LMB + kt), scale=col(V_LMG + kt)).then_inc(memT_ready, 1)
                act.wait_ge(memT_ready, kt + 1)
                act.activation(memT_high[:, kt, :], memT[:, kt, :], ACT.Copy).then_inc(memT_split, 1)
            for i in range(KT):
                ahead(CH_Q + i // 2)
                act.wait_ge(q_mm, i + 1)
                act.activation(u[:, i, :], ps[:, 2 + i % 4, :], ACT.Identity, bias=col(V_BIN + Z_Q // P + i)).then_inc(q_ready, 1)
            for i in range(KT + 4 * MT):
                ahead(CH_K + i // 2)
                act.wait_ge(kv_mm, i + 1)
                if i < KT:
                    act.activation(kT[:, i, :], ps[:, 6 + i % 2, 0:MEM], ACT.Copy).then_inc(kv_ready, 1)
                else:
                    n, t = (i - KT) // MT, (i - KT) % MT
                    act.activation(vm[:, t, n * 2 * P:(n + 1) * 2 * P], ps[:, 6 + i % 2, 0:2 * P], ACT.Copy).then_inc(kv_ready, 1)
            ahead(CH_MC)
            N = C_HEADS * TT
            for i in range(N + 4):
                if i < N:
                    act.wait_ge(cnm_ready, i + 1)
                    if i >= 3:
                        act.wait_ge(ct_done, i - 2)
                    act.activation(prob[:, i % 3, :], ps[:, i % 3, 0:MEM], ACT.Exp, bias=small[:, 64 + i:65 + i], scale=CSCALE, accum_out=small[:, 32 + i:33 + i]).then_inc(cexp_done, 1)
                j = i - 2
                if 0 <= j < N:
                    act.wait_ge(ct_done, j + 1)
                    if j >= TT and j % TT == 0:
                        act.wait_ge(cpv_done, j // TT)
                    act.activation(PT[:, :, (j % TT) * P:(j % TT + 1) * P], ps[:, 3 + j % 2, 0:MEM].rearrange("p (c n) -> p c n", c=MT), ACT.Copy).then_inc(cpt_ev, 1)
                if i >= 7 and i % TT == 3:
                    h = (i - 7) // TT
                    act.wait_ge(cpv_done, h + 1)
                    for d in range(2):
                        act.activation(u[:, 2 * h + d, :], ps[:, 5 + d, :], ACT.Copy)
                        last = act.activation(act_high[:, 2 * h + d, :], ps[:, 5 + d, :], ACT.Copy)
                    last.then_inc(oc_ready, 1)
            merge(2, CH_MC, 2)
            for kt in (KT - 2, KT - 1):
                whole_split(kt)
            ahead(CH_O)
            for kt in range(KT):
                if kt % 2 == 0:
                    ahead(CH_O + kt // 2)
                act.wait_ge(x_whole, kt + 1)
                act.activation(xT[:, kt, :], xT[:, kt, :], ACT.Identity, bias=col(V_BO + kt), scale=ALPHA).then_inc(ax_ready, 1)
            act.wait_ge(wg_in, 64)
            act.activation(w_g_high, w_g, ACT.Copy).then_inc(wg_split, 1)
            for n in range(AHEAD):
                group_split(0, n)
            layer_norm(1, xT, V_L1G, V_L1B)
            act.wait_ge(gl_mm, 1)
            act.activation(glT, ps[0:20, 6, :], ACT.Copy).then_inc(glT_kept, 1)
            act.wait_ge(g_sub, 1)
            act.activation(gw[0][:, :, 0:4], gw[0][:, :, 0:4], ACT.Exp).then_inc(g_exp, 1)
            act.wait_ge(e_sub, 1)
            act.activation(gw[3][:, :, 0:4], gw[3][:, :, 0:4], ACT.Exp).then_inc(e_exp, 1)

            def experts(g, last):
                def high(n):
                    act.wait_ge(hid2_ready, 8 * g + n + 2)
                    act.activation(act_high[:, n, :], u[:, n, :], ACT.Copy).then_inc(hid_split, 1)

                for n in range(2 * PER_GROUP):
                    group_split(g, n + AHEAD)
                    act.wait_ge(up_mm, 16 * g + 2 * n + 1)
                    act.wait_ge(hid2_ready, 8 * g + n + 1)
                    act.activation(tmp[:, n % 2, :], ps[:, 2 * (n % 2), :], ACT.Silu).then_inc(sg2_ready, 1)
                    if n >= 1:
                        high(n - 1)
                high(2 * PER_GROUP - 1)
                for n in range(2 * PER_GROUP + AHEAD, GROUP_CHUNKS):
                    group_split(g, n)
                if not last:
                    for n in range(AHEAD):
                        group_split(g + 1, n)

            with act.Fori(0, EXP_GROUPS - 1) as g:
                experts(g, False)
            experts(EXP_GROUPS - 1, True)
            layer_norm(2, y, V_L2G, V_L2B)
            for t in range(TT):
                act.wait_ge(o_mm, TT + t + 1)
                act.activation(v3[:, t, HALF:D], ps[:, O_BANKS[TT + t], :], ACT.Copy).then_inc(o_second, 1)

        @block.vector
        def _(dve):
            step = Steps(dve, d2_step)

            def col(n):
                return vec[:, n:n + 1]

            def vectors():
                dve.wait_ge(rows_turned, 1)
                dve.tensor_copy(vec[:, 0:NV1], ps[:, 6, 0:NV1]).then_inc(vec2_ready, 1)
                dve.wait_ge(rows_turned, 2)
                dve.tensor_copy(vec[:, NV1:NV2], ps[:, 7, 0:NV2 - NV1]).then_inc(vec2_ready, 1)
                dve.wait_ge(vec2_ready, 2)
                lam = vec[:, V_LAM:V_LAM + B_HEADS]
                step(dve.tensor_scalar(lru[:, 4, :], lam, -1.0, None, ALU.mult))
                step.settle()
                dve.tensor_tensor(lru[:, 0, :], lam, lru[:, 4, :], ALU.max).then_inc(lru_ready, 1)

            def layer_norm(k, x):
                dve.wait_ge(l_sum, k + 1)
                for kt in range(KT):
                    dve.scalar_tensor_tensor(x[:, kt, :], ps[:, 0, :], -1.0 / D, x[:, kt, :], ALU.mult, ALU.add).then_inc(l_dev, 1)
                if k == 0:
                    vectors()
                dve.wait_ge(l_root, k + 1)
                dve.reciprocal(tmp[:, 4, 0:P], tmp[:, 4, 0:P]).then_inc(l_inv, 1)
                dve.wait_ge(l_bc, k + 1)
                for n in range(KT + 3 if k < 2 else KT):
                    if n < KT:
                        dve.tensor_tensor(x[:, n, :], x[:, n, :], ps[:, 0, :], ALU.mult).then_inc(l_norm, 1)
                    kt = n - 3
                    if kt < 0 or k == 2:
                        continue
                    dve.wait_ge(x_split, KT * k + kt + 1)
                    if k == 1:
                        dve.tensor_scalar(y[:, kt, :], x[:, kt, :], ALPHA, None, ALU.mult).then_inc(f_init, 1)
                    dve.tensor_tensor(x_low[:, kt, :], x[:, kt, :], x_high[:, kt, :].bitcast(F32), ALU.subtract).then_inc(x_ready, 1)

            layer_norm(0, xT)
            e, s, s2, acc = lru[:, 1, :], lru[:, 2, :], lru[:, 3, :], lru[:, 5, :]
            dve.wait_ge(lru_exp, 1)
            step(dve.tensor_scalar(s, e, 2.0, None, ALU.add))
            step.settle()
            step(dve.reciprocal(s, s))
            step.settle()
            step(dve.tensor_tensor(s, s, e, ALU.mult))
            step.settle()
            step(dve.tensor_tensor(s2, s, s, ALU.mult))
            step(dve.memset(acc, 2.0 / 19))
            for n in range(17, 0, -2):
                step.settle()
                step(dve.tensor_tensor(acc, acc, s2, ALU.mult))
                step.settle()
                step(dve.tensor_scalar(acc, acc, 2.0 / n, None, ALU.add))
            step.settle()
            step(dve.tensor_tensor(acc, acc, s, ALU.mult))
            step.settle()
            step(dve.scalar_tensor_tensor(acc, lru[:, 4, :], 0.0, acc, ALU.max, ALU.add))
            step.settle()
            step(dve.tensor_scalar(s, acc, -LRU_C, None, ALU.mult))
            dve.tensor_scalar(s2, acc, LRU_C, None, ALU.mult).then_inc(lru_ready, 1)

            for h in range(B_HEADS + 1):
                if h < B_HEADS:
                    dve.wait_ge(bz_ev, 2 * h + 1)
                    if h >= 2:
                        dve.wait_ge(bg_mm, h - 1)
                    x, src = xc[h % 2], xpad[h % 2]
                    for t in range(TAPS_B):
                        w = col(V_CW + t * B_HEADS + h)
                        if t == 0:
                            step(dve.tensor_scalar(x, src[:, 0:S], w, col(V_CB + h), ALU.mult, ALU.add))
                        else:
                            step.settle()
                            op = dve.scalar_tensor_tensor(x, src[:, t:t + S], w, x, ALU.mult, ALU.add)
                            if t < TAPS_B - 1:
                                step(op)
                            else:
                                op.then_inc(xc_ready, 1)
                if h >= 1:
                    k = h - 1
                    dve.wait_ge(at_ready, k + 1)
                    step(dve.tensor_tensor(rr, aa, aa, ALU.mult))
                    step(dve.tensor_tensor(ii, ii, xc[k % 2], ALU.mult))
                    step.settle()
                    dve.scalar_tensor_tensor(rr, rr, 1.0, th, ALU.add, ALU.mult).then_inc(m2_ready, 1)
                    dve.wait_ge(mult_ready, k + 1)
                    step(dve.scalar_tensor_tensor(ii, th, LIFT ** -0.5, ii, ALU.mult, ALU.mult))
                    step.settle()
                    step(dve.tensor_tensor_scan(rr, aa, ii, 0.0, ALU.mult, ALU.add))
                    step.settle()
                    dve.tensor_tensor(ob[:, k, :], rr, gt[k % 2], ALU.mult).then_inc(ob_ready, 1)

            dve.wait_ge(bc_in, 64)
            for i in range(4 * TT):
                n, t = i // TT, i % TT
                dve.wait_ge(v_mm, i + 1)
                cs = slice(n * 2 * P, (n + 1) * 2 * P)
                dve.tensor_tensor(v3[:, t, cs], ps[:, V_BANKS[i % len(V_BANKS)], 0:2 * P], bv_row[:, cs], ALU.add).then_inc(v_biased, 1)

            def row_stats(x, t, done):
                for n in range(2):
                    step(dve.bn_stats(small[:, 100 + 6 * n:106 + 6 * n], x[:, t, n * HALF:(n + 1) * HALF]))
                step.settle()
                dve.bn_aggr(small[:, 8 + 2 * t:10 + 2 * t], small[:, 100:112]).then_inc(done, 1)
                dve.wait_ge(done, t + 1)

            for t in range(TT):
                dve.wait_ge(v_gelu, 3 * TT + t + 1)
                row_stats(v3, t, v_var)
            dve.wait_ge(v_root, 1)
            step(dve.reciprocal(small[:, 16:20], small[:, 16:20]))
            step.settle()
            for t in range(TT):
                step(dve.tensor_scalar(v3[:, t], v3[:, t], small[:, 8 + 2 * t:9 + 2 * t], small[:, 16 + t:17 + t], ALU.subtract, ALU.mult))
                step.settle()
                step(dve.tensor_tensor(v3[:, t], v3[:, t], lvg_row, ALU.mult))
                step.settle()
                dve.tensor_tensor(v3[:, t], v3[:, t], lvb_row, ALU.add).then_inc(v_ready, 1)
            def u_rest(use, k):
                dve.wait_ge(u_split, KT * use + k + 1)
                dve.tensor_tensor(u_low[:, k, :], u[:, k, :], act_high[:, k, :].bitcast(F32), ALU.subtract).then_inc(u_low_ready, 1)

            for g in range(GROUPS_A):
                dve.wait_ge(sp_mm, g + 1)
                s = tmp[:, 4 + g % 2, :]
                step(dve.tensor_tensor(s.rearrange("p (c t) -> p c t", c=TT), ps[:, 2 + g % 4, :].rearrange("p (c t) -> p c t", c=TT),
                                       bs_row[:, g * P:(g + 1) * P].unsqueeze(1).to_broadcast([P, TT, P]), ALU.add))
                step.settle()
                dve.tensor_tensor(u[:, g, :], u[:, g, :], s, ALU.mult).then_inc(oa_ready, 1)
                if g >= 1:
                    u_rest(0, g - 1)
            u_rest(0, GROUPS_A - 1)

            def merge(branch):
                for dt in range(KT):
                    n = KT * branch + dt
                    dve.wait_ge(m_sg, n + 1)
                    dve.wait_ge(m_mm, n + 1)
                    sg, out = gate_sg[n % 2], ps[:, 3 + 2 * (n % 2), :]
                    if branch == 0:
                        dve.tensor_tensor(y[:, dt, :], sg, out, ALU.mult).then_inc(m_y, 1)
                    else:
                        step(dve.tensor_tensor(sg, sg, out, ALU.mult))
                        step.settle()
                        dve.tensor_tensor(y[:, dt, :], y[:, dt, :], sg, ALU.add).then_inc(m_y, 1)
                    if branch == 2 and dt >= 3:
                        whole_rest(dt - 3)
                    if n == KT + 3:
                        dve.wait_ge(mem_root, 1)
                        step(dve.reciprocal(small[:, 16:18], small[:, 16:18]))
                        step.settle()
                        for t in range(MT):
                            dve.tensor_scalar(mem_tok[:, t], mem_tok[:, t], small[:, 8 + 2 * t:9 + 2 * t], small[:, 16 + t:17 + t], ALU.subtract, ALU.mult).then_inc(mem_norm, 1)

            def whole_rest(kt):
                dve.wait_ge(y_split, kt + 1)
                dve.tensor_tensor(y_low[:, kt, :], y[:, kt, :], y_high[:, kt, :].bitcast(F32), ALU.subtract).then_inc(y_low_ready, 1)

            merge(0)
            for h in range(B_HEADS):
                dve.wait_ge(ob_split, h + 1)
                dve.tensor_tensor(ob_low[:, h, :], ob[:, h, :], ob_high[h].bitcast(F32), ALU.subtract).then_inc(ob_low_ready, 1)
            dve.wait_ge(mem_in, 16)
            for t in range(MT):
                row_stats(mem_tok, t, mem_var)
            merge(1)
            for kt in range(KT):
                dve.wait_ge(memT_split, kt + 1)
                dve.tensor_tensor(memT_low[:, kt, :], memT[:, kt, :], memT_high[:, kt, :].bitcast(F32), ALU.subtract).then_inc(memT_low_ready, 1)

            def oc_rest(h):
                dve.wait_ge(oc_ready, h + 1)
                for k in (2 * h, 2 * h + 1):
                    dve.tensor_tensor(u_low[:, k, :], u[:, k, :], act_high[:, k, :].bitcast(F32), ALU.subtract).then_inc(u_low_ready, 1)

            N = C_HEADS * TT
            for i in range(N + 1):
                if i < N:
                    dve.wait_ge(cs_done, i + 1)
                    step(dve.reduce_max(small[:, 48 + i:49 + i], ps[:, i % 3, 0:MEM], AX_X))
                    step.settle()
                    dve.tensor_scalar(small[:, 64 + i:65 + i], small[:, 48 + i:49 + i], -CSCALE, None, ALU.mult).then_inc(cnm_ready, 1)
                j = i - 1
                if j >= 0:
                    dve.wait_ge(cexp_done, j + 1)
                    step(dve.reciprocal(small[:, 80 + j:81 + j], small[:, 32 + j:33 + j]))
                    step.settle()
                    if j >= 3:
                        dve.wait_ge(ct_done, j - 2)
                    dve.tensor_scalar(diag[:, j % 3, :], ident, small[:, 80 + j:81 + j], None, ALU.mult).then_inc(cdiag_ready, 1)
                if i >= 9 and i % TT == 1:
                    oc_rest((i - 9) // TT)
            for h in (C_HEADS - 2, C_HEADS - 1):
                oc_rest(h)
            merge(2)
            for kt in range(KT - 3, KT):
                whole_rest(kt)
            dve.wait_ge(m_mm, 3 * KT)
            for kt in range(KT):
                dve.tensor_tensor(xT[:, kt, :], x_low[:, kt, :].bitcast(F32), x_high[:, kt, :].bitcast(F32), ALU.add).then_inc(x_whole, 1)
            for dt in range(KT):
                dve.wait_ge(ax_ready, dt + 1)
                dve.wait_ge(wo_mm, dt + 1)
                dve.tensor_tensor(xT[:, dt, :], ps[:, 2 + dt % 4, :], xT[:, dt, :], ALU.add).then_inc(wo_used, 1)
            dve.wait_ge(wg_split, 1)
            dve.tensor_tensor(w_g_low, w_g, w_g_high.bitcast(F32), ALU.subtract).then_inc(wg_ready, 1)
            layer_norm(1, xT)
            dve.wait_ge(g_mm, 1)
            dve.wait_ge(prio_ready, 1)
            dve.wait_ge(wg_in, 64)

            def op(instruction):
                step(instruction)
                step.settle()

            def wide(x, n=4):
                return x.unsqueeze(2).to_broadcast([P, TT, n])

            def first_best(out, x, top, rest):
                op(dve.tensor_tensor(out, x, wide(top), ALU.is_equal))
                op(dve.tensor_tensor(out, out, prio.unsqueeze(1).to_broadcast([P, TT, 4]), ALU.mult))
                op(dve.reduce_max(rest, out, AX_X))
                op(dve.tensor_tensor(out, out, wide(rest), ALU.is_equal))

            top, rest, ptop = small[:, 8:12], small[:, 12:16], small[:, 16:20]
            op(dve.tensor_tensor(gl, ps[:, 7, 0:TT * 20].rearrange("p (t n) -> p t n", t=TT), bg_row.unsqueeze(1).to_broadcast([P, TT, 20]), ALU.add))
            op(dve.reduce_max(top, gl[:, :, 0:4], AX_X))
            dve.tensor_tensor(gw[0][:, :, 0:4], gl[:, :, 0:4], wide(top), ALU.subtract).then_inc(g_sub, 1)
            group = gw[1][:, :, 0:4]
            first_best(group, gl[:, :, 0:4], top, rest)
            dve.wait_ge(g_exp, 1)
            op(dve.reduce_sum(ptop, gw[0][:, :, 0:4], AX_X))
            op(dve.reciprocal(ptop, ptop))
            per = gw[2].rearrange("p t (g j) -> p t g j", g=4)
            op(dve.tensor_tensor(per, gl[:, :, 4:20].rearrange("p t (g j) -> p t g j", g=4), group.unsqueeze(3).to_broadcast([P, TT, 4, 4]), ALU.mult))
            inside = gw[3][:, :, 0:4]
            op(dve.reduce_sum(inside, per.rearrange("p t g j -> p t j g"), AX_X))
            op(dve.reduce_max(top, inside, AX_X))
            dve.tensor_tensor(inside, inside, wide(top), ALU.subtract).then_inc(e_sub, 1)
            dve.wait_ge(e_exp, 1)
            one, two = gw[4][:, :, 0:4], gw[5][:, :, 0:4]
            op(dve.reduce_max(top, inside, AX_X))
            first_best(one, inside, top, rest)
            op(dve.scalar_tensor_tensor(gw[4][:, :, 4:8], one, -2.0, inside, ALU.mult, ALU.add))
            op(dve.reduce_max(top, gw[4][:, :, 4:8], AX_X))
            first_best(two, gw[4][:, :, 4:8], top, rest)
            op(dve.tensor_tensor(one, one, two, ALU.add))
            op(dve.tensor_tensor(one, one, inside, ALU.mult))
            op(dve.reduce_sum(rest, one, AX_X))
            op(dve.reciprocal(rest, rest))
            op(dve.tensor_tensor(rest, rest, ptop, ALU.mult))
            op(dve.tensor_tensor(one, one, wide(rest), ALU.mult))
            dve.tensor_tensor(gw[0].rearrange("p t (g j) -> p t g j", g=4), group.unsqueeze(3).to_broadcast([P, TT, 4, 4]),
                              one.unsqueeze(2).to_broadcast([P, TT, 4, 4]), ALU.mult).then_inc(gate_ready, 1)
            dve.wait_ge(gate_turned, 1)
            dve.tensor_copy(gateT, ps[0:EXPERTS, 6, :]).then_inc(gateT_ready, 1)
            dve.wait_ge(f_init, KT)
            dve.memset(small[:, 20:21], 0.0).then_inc(hid2_ready, 1)
            dve.memset(small[:, 21:22], 0.0).then_inc(dn_used, 2)
            def select(g):
                for j in range(PER_GROUP):
                    last = dve.tensor_scalar(sel[:, j, :], ones[0:EXPERTS, :], const[0:EXPERTS, bass.ds(PER_GROUP * g + j, 1)], None, ALU.mult)
                last.then_inc(sel_ready, 1)

            select(0)
            with dve.Fori(0, EXP_GROUPS) as g:
                def rest(n):
                    dve.wait_ge(hid_split, 8 * g + n + 1)
                    dve.tensor_tensor(u_low[:, n, :], u[:, n, :], act_high[:, n, :].bitcast(F32), ALU.subtract).then_inc(hid_low, 1)

                for n in range(2 * PER_GROUP):
                    j, i = n // 2, n % 2
                    dve.wait_ge(up_mm, 16 * g + 2 * n + 2)
                    dve.wait_ge(sg2_ready, 8 * g + n + 1)
                    dve.tensor_tensor(tmp[:, 2 + i, :], tmp[:, i, :], ps[:, 2 * i + 1, :], ALU.mult).then_inc(m_loop, 1)
                    dve.wait_ge(m_loop, 8 * g + n + 1)
                    dve.wait_ge(bc_mm, 4 * g + j + 1)
                    dve.tensor_tensor(u[:, n, :], tmp[:, 2 + i, :], ps[:, 4 + j % 2, :], ALU.mult).then_inc(hid2_ready, 1)
                    if n >= 1:
                        rest(n - 1)
                rest(2 * PER_GROUP - 1)
                select(g + 1)
                for dt in range(KT):
                    dve.wait_ge(dn_mm, 8 * g + dt + 1)
                    dve.tensor_tensor(y[:, dt, :], y[:, dt, :], ps[:, 6 + dt % 2, :], ALU.add).then_inc(dn_used, 1)
            layer_norm(2, y)
            for t in range(TT):
                dve.wait_ge(o_mm, t + 1)
                dve.tensor_copy(v3[:, t, 0:HALF], ps[:, O_BANKS[t], :]).then_inc(o_first, 1)


def memory2(nc, ctx, M):
    M = dict(M)
    shared = dict(raw=[P, SLOTS * SLOT], u=[P, KT, S], ob=[P, B_HEADS, S], y=[P, KT, S], v=[P, TT * D], tmp=[P, 8 * S + 2 * (S + TAPS_B - 1)])
    with ExitStack() as rounded:
        for name, shape in shared.items():
            M[name + "_r"] = rounded.enter_context(nc.sbuf_tensor(name + "_r", shape, FR))
    for name, shape in shared.items():
        M[name] = ctx.enter_context(nc.sbuf_tensor(name, shape, F32))
    for name, shape in dict(w_high=[P, SLOTS * SLOT], x_high=[P, KT, S], act_high=[P, KT, S]).items():
        M[name] = ctx.enter_context(nc.sbuf_tensor(name, shape, FR))
    for name, shape in dict(wT=[P, GROUPS_A, P], vec2=[P, NV2], lru=[P, 6, B_HEADS], small=[P, 112]).items():
        M[name] = ctx.enter_context(nc.sbuf_tensor(name, shape, F32))
    return M


def program(nc, A):
    with ExitStack() as ctx:
        M = memory(nc, ctx)
        with ExitStack() as first:
            M1 = memory1(nc, first, M)
            ahead = prologue(nc, A, lambda name: ctx.enter_context(nc.semaphore(name)), M1)
            layer_sems = []

            def layer_sem(name):
                layer_sems.append(first.enter_context(nc.semaphore(name)))
                return layer_sems[-1]

            with nc.Fori(0, DEPTH) as l:
                layer(nc, A, layer_sem, M1, l, ahead)
                nc.gpsimd.sem_clear(range(layer_sems[0].num, layer_sems[-1].num + 1))
                nc.all_engine_barrier()
        with ExitStack() as last:
            second(nc, A, lambda name: ctx.enter_context(nc.semaphore(name)), memory2(nc, last, M))


def constants():
    import numpy as np

    c = np.zeros((P, C_ALL), np.float32)
    part = np.arange(P)
    c[:, C_IDENT:C_IDENT + P] = np.eye(P)
    half = ROPE // 2
    for m in range(P):
        first = m % ROPE < half
        c[m + half if first else m - half, C_ROT + m] = -1.0 if first else 1.0
    c[:, C_SLOT:C_SLOT + P] = part % CAP
    c[:, C_PSLOT] = part % CAP
    freq = np.float32(1.0) / np.float32(10000.0) ** (np.arange(0, ROPE, 2, dtype=np.float32) / np.float32(ROPE))
    c[:, C_PAIR + GROUP // 2:C_PAIR + GROUP] = 1.0
    c[:, C_FREQ] = freq[part % half]
    c[:, C_EPS6], c[:, C_EPS5] = EPS, 1e-5
    return c


def kernel(**inputs):
    import numpy as _np
    import concourse.bacc as _bacc
    from concourse import mybir as _mybir
    from concourse.bass_utils import run_bass_kernel_spmd as _run

    nc = _bacc.Bacc("TRN2", target_bir_lowering=False, num_devices=1)
    arrays, A = {}, {}
    for name, value in [*inputs.items(), ("const", constants())]:
        a = _np.ascontiguousarray(value)
        arrays[f"in_{name}"] = a
        A[name] = nc.dram_tensor(f"in_{name}", a.shape, _mybir.dt.from_np(a.dtype), kind="ExternalInput").ap()
    A["rope"] = nc.dram_tensor("rope_tables", (P, 2 * S), F32, kind="Internal").ap()
    A["out"] = nc.dram_tensor("out_0", (1, S, D), F32, kind="ExternalOutput").ap()
    program(nc, A)
    return _run(nc, [arrays], core_ids=[0]).results[0]["out_0"]
```
